# Optimizing a Trainium2 kernel written in Bass

```python
import jax, jax.numpy as jnp
from jax import lax
import numpy as np
import jax
import jax.numpy as jnp

D_MODEL = 1024
BATCH = 1
SEQ = 256
DEPTH = 1

N_META = 16
RET_HEADS = 8
RET_QK_DIM = 128
RET_V_DIM = 128
RET_CHUNK = 128
ROPE_BASE = 10000.0
LRU_WIDTH = D_MODEL
LRU_BLOCKS = 4
LRU_BLOCK = LRU_WIDTH // LRU_BLOCKS
CONV_WIDTH = 4
LRU_C = 8.0
FFN_HIDDEN = ((8 * D_MODEL // 3 + 255) // 256) * 256
RET_QK = RET_HEADS * RET_QK_DIM
RET_V = RET_HEADS * RET_V_DIM
IN_COLS = 2 * RET_QK + 2 * RET_V + 2 * LRU_WIDTH + 2 * D_MODEL
NORM_EPS = 1e-6


def rmsnorm(x, w):
    xf = x.astype(jnp.float32)
    y = xf * lax.rsqrt(jnp.mean(xf * xf, axis=-1, keepdims=True) + NORM_EPS)
    return (y * w.astype(jnp.float32)).astype(x.dtype)

def rotary(x, pos):
    d = x.shape[-1]
    inv_freq = ROPE_BASE ** (-jnp.arange(0, d, 2, dtype=jnp.float32) / d)
    ang = pos.astype(jnp.float32)[:, None] * inv_freq[None, :]
    cos = jnp.cos(ang)[None, :, None, :]
    sin = jnp.sin(ang)[None, :, None, :]
    x1, x2 = x[..., : d // 2], x[..., d // 2:]
    return jnp.concatenate([x1 * cos - x2 * sin, x2 * cos + x1 * sin], axis=-1)

def chunk_retention(q, k, v):
    B, T, H, dk = q.shape
    dv = v.shape[-1]
    C = RET_CHUNK
    pad = C - N_META
    padw = ((0, 0), (pad, 0), (0, 0), (0, 0))
    q, k, v = jnp.pad(q, padw), jnp.pad(k, padw), jnp.pad(v, padw)
    Tp = T + pad
    n_chunks = Tp // C
    log_g = jnp.log(1.0 - 2.0 ** (-5.0 - jnp.arange(H, dtype=jnp.float32)))
    idx = jnp.arange(C, dtype=jnp.float32)
    diff = idx[:, None] - idx[None, :]
    intra = jnp.where(diff[None] >= 0,
                      jnp.exp(jnp.maximum(diff, 0.0)[None] * log_g[:, None, None]), 0.0)
    q_decay = jnp.exp((idx + 1.0)[:, None] * log_g[None, :])
    k_decay = jnp.exp((C - 1.0 - idx)[:, None] * log_g[None, :])
    chunk_decay = jnp.exp(C * log_g)

    def to_chunks(a):
        return a.reshape(B, n_chunks, C, H, a.shape[-1]).transpose(1, 0, 2, 3, 4)

    def step(state, qkv):
        qc, kc, vc = qkv
        s = jnp.einsum('bchd,bmhd->bhcm', qc, kc) * intra[None]
        inner = jnp.einsum('bhcm,bmhe->bche', s, vc)
        cross = jnp.einsum('bchd,bhde->bche', qc, state) * q_decay[None, :, :, None]
        state = state * chunk_decay[None, :, None, None] + jnp.einsum(
            'bmhd,bmhe->bhde', kc * k_decay[None, :, :, None], vc)
        return state, inner + cross

    s0 = jnp.zeros((B, H, dk, dv), jnp.float32)
    _, ys = lax.scan(step, s0, (to_chunks(q), to_chunks(k), to_chunks(v)))
    out = ys.transpose(1, 0, 2, 3, 4).reshape(B, Tp, H, dv)
    return out[:, pad:]

def causal_depthwise_conv(x, w, b):
    T = x.shape[1]
    xp = jnp.pad(x, ((0, 0), (CONV_WIDTH - 1, 0), (0, 0)))
    y = b[None, None, :]
    for j in range(CONV_WIDTH):
        y = y + xp[:, j:j + T] * w[j][None, None, :]
    return y

def rg_lru(x, wa, ba, wx, bx, lam):
    B, T, W = x.shape
    xb = x.reshape(B, T, LRU_BLOCKS, LRU_BLOCK)
    r = jax.nn.sigmoid(jnp.einsum('btgi,gij->btgj', xb, wa).reshape(B, T, W) + ba)
    i = jax.nn.sigmoid(jnp.einsum('btgi,gij->btgj', xb, wx).reshape(B, T, W) + bx)
    log_a = -LRU_C * r * jax.nn.softplus(-lam)
    a = jnp.exp(log_a)
    u = jnp.sqrt(-jnp.expm1(2.0 * log_a)) * (i * x)

    def step(h, au):
        a_t, u_t = au
        h = a_t * h + u_t
        return h, h

    _, hs = lax.scan(step, jnp.zeros((B, W), jnp.float32),
                     (a.transpose(1, 0, 2), u.transpose(1, 0, 2)))
    return hs.transpose(1, 0, 2)

def first_inputs(seed: int = 0) -> dict:
    key = jax.random.key(seed)
    ks = jax.random.split(key, 20)
    f32 = jnp.float32
    nrm = lambda k, s, sc: jax.random.normal(k, s, f32) * sc
    a0 = jax.random.uniform(ks[9], (DEPTH, LRU_WIDTH), f32, minval=0.9, maxval=0.999)
    a0r = a0 ** (1.0 / LRU_C)
    return {
        'x': nrm(ks[0], (BATCH, SEQ, D_MODEL), 1.0),
        'meta_tokens': nrm(ks[1], (N_META, D_MODEL), 1.0),
        'mix_norm_w': 1.0 + nrm(ks[2], (DEPTH, D_MODEL), 0.02),
        'w_in': nrm(ks[3], (DEPTH, D_MODEL, IN_COLS), D_MODEL ** -0.5),
        'conv_w': nrm(ks[4], (DEPTH, CONV_WIDTH, LRU_WIDTH), CONV_WIDTH ** -0.5),
        'conv_b': nrm(ks[5], (DEPTH, LRU_WIDTH), 0.01),
        'lru_wa': nrm(ks[6], (DEPTH, LRU_BLOCKS, LRU_BLOCK, LRU_BLOCK), LRU_BLOCK ** -0.5),
        'lru_ba': nrm(ks[7], (DEPTH, LRU_WIDTH), 0.01),
        'lru_wx': nrm(ks[8], (DEPTH, LRU_BLOCKS, LRU_BLOCK, LRU_BLOCK), LRU_BLOCK ** -0.5),
        'lru_bx': nrm(ks[10], (DEPTH, LRU_WIDTH), 0.01),
        'lru_lambda': jnp.log(a0r) - jnp.log1p(-a0r),
        'w_branch_ret': nrm(ks[11], (DEPTH, RET_V, D_MODEL), RET_V ** -0.5),
        'w_branch_lru': nrm(ks[12], (DEPTH, LRU_WIDTH, D_MODEL), LRU_WIDTH ** -0.5),
        'w_out': nrm(ks[13], (DEPTH, D_MODEL, D_MODEL), D_MODEL ** -0.5),
        'ffn_norm_w': 1.0 + nrm(ks[14], (DEPTH, D_MODEL), 0.02),
        'w_ffn_in': nrm(ks[15], (DEPTH, D_MODEL, 2 * FFN_HIDDEN), D_MODEL ** -0.5),
        'w_ffn_out': nrm(ks[16], (DEPTH, FFN_HIDDEN, D_MODEL), FFN_HIDDEN ** -0.5),
        'final_norm_w': 1.0 + nrm(ks[17], (D_MODEL,), 0.02),
    }

def first_block(x, meta_tokens, mix_norm_w, w_in, conv_w, conv_b, lru_wa, lru_ba, lru_wx,
              lru_bx, lru_lambda, w_branch_ret, w_branch_lru, w_out, ffn_norm_w,
              w_ffn_in, w_ffn_out, final_norm_w):
    B = x.shape[0]
    f32 = jnp.float32
    meta = jnp.broadcast_to(meta_tokens.astype(x.dtype)[None], (B, N_META, D_MODEL))
    h = jnp.concatenate([meta, x], axis=1)
    T = h.shape[1]
    pos = jnp.arange(T)
    sizes = (RET_QK, RET_QK, RET_V, RET_V, LRU_WIDTH, LRU_WIDTH, D_MODEL, D_MODEL)
    split_at = [int(s) for s in np.cumsum(sizes)[:-1]]
    for l in range(DEPTH):
        u = rmsnorm(h, mix_norm_w[l])
        proj = u @ w_in[l]
        q, k, v, g_ret, lru_in, lru_gate, gate_a, gate_b = jnp.split(proj, split_at, axis=-1)
        q = rotary(q.reshape(B, T, RET_HEADS, RET_QK_DIM).astype(f32), pos)
        k = rotary(k.reshape(B, T, RET_HEADS, RET_QK_DIM).astype(f32), pos) * (RET_QK_DIM ** -0.5)
        v = v.reshape(B, T, RET_HEADS, RET_V_DIM).astype(f32)
        o = chunk_retention(q, k, v)
        o = o * lax.rsqrt(jnp.mean(o * o, axis=-1, keepdims=True) + NORM_EPS)
        o = o.reshape(B, T, RET_V).astype(h.dtype)
        y_ret = (jax.nn.silu(g_ret) * o) @ w_branch_ret[l]
        c = causal_depthwise_conv(lru_in.astype(f32), conv_w[l].astype(f32), conv_b[l].astype(f32))
        r = rg_lru(c, lru_wa[l].astype(f32), lru_ba[l].astype(f32), lru_wx[l].astype(f32),
                   lru_bx[l].astype(f32), lru_lambda[l].astype(f32)).astype(h.dtype)
        y_lru = (jax.nn.gelu(lru_gate) * r) @ w_branch_lru[l]
        mixed = jax.nn.sigmoid(gate_a) * y_ret + jax.nn.sigmoid(gate_b) * y_lru
        h = h + mixed @ w_out[l]
        u = rmsnorm(h, ffn_norm_w[l])
        gu = u @ w_ffn_in[l]
        g, up = gu[..., :FFN_HIDDEN], gu[..., FFN_HIDDEN:]
        h = h + (jax.nn.silu(g) * up) @ w_ffn_out[l]
    h = rmsnorm(h, final_norm_w)
    return h[:, N_META:]


MEM_LEN = 256
EPS = 1e-6

GLA_HEADS = 4
GLA_DK = D_MODEL // 8
GLA_DV = D_MODEL // 4
GLA_GATE_RANK = 16
GLA_GATE_TEMP = 16.0
GLA_CHUNK = 64

DSA_HEADS = 8
DSA_KV_HEADS = 2
DSA_HEAD_DIM = 128
IDX_HEADS = 8
IDX_DIM = 64
IDX_TOPK_MAX = 256
Q_BLOCK = 128

MEM_HEADS = 4
MEM_HEAD_DIM = D_MODEL // 4

N_GROUPS = 4
EXPERTS_PER_GROUP = 4
N_EXPERTS = N_GROUPS * EXPERTS_PER_GROUP
EXPERT_TOPK = 2
D_EXPERT = D_MODEL // 4

N_BRANCH = 3
IN_SPLITS = (
    GLA_HEADS * GLA_DK,
    GLA_HEADS * GLA_DK,
    GLA_HEADS * GLA_DV,
    GLA_HEADS * GLA_DV,
    GLA_GATE_RANK,
    DSA_HEADS * DSA_HEAD_DIM,
    DSA_KV_HEADS * DSA_HEAD_DIM,
    DSA_KV_HEADS * DSA_HEAD_DIM,
    IDX_HEADS * IDX_DIM,
    IDX_DIM,
    IDX_HEADS,
    MEM_HEADS * MEM_HEAD_DIM,
    N_BRANCH * D_MODEL,
)
D_IN = sum(IN_SPLITS)


def _rmsnorm(x, g):
    xf = x.astype(jnp.float32)
    y = xf * lax.rsqrt(jnp.mean(xf * xf, axis=-1, keepdims=True) + EPS)
    return y.astype(x.dtype) * g

def _split_in(z):
    offs = []
    acc = 0
    for w in IN_SPLITS[:-1]:
        acc += w
        offs.append(acc)
    return jnp.split(z, offs, axis=-1)

def _gla(q, k, v, g_out, a_low, w_a2, b_a2, norm_g):
    B, T = q.shape[:2]
    C = GLA_CHUNK
    N = T // C
    shp_k = (B, N, C, GLA_HEADS, GLA_DK)
    qf = q.astype(jnp.float32).reshape(shp_k) * GLA_DK ** -0.5
    kf = k.astype(jnp.float32).reshape(shp_k)
    vf = v.astype(jnp.float32).reshape(B, N, C, GLA_HEADS, GLA_DV)
    log_a = jax.nn.log_sigmoid((a_low @ w_a2 + b_a2).astype(jnp.float32)) / GLA_GATE_TEMP
    cum = jnp.cumsum(log_a.reshape(shp_k), axis=2)
    last = cum[:, :, -1:]
    q_dec = qf * jnp.exp(cum)
    k_inv = kf * jnp.exp(-cum)
    k_end = kf * jnp.exp(last - cum)
    causal = jnp.tril(jnp.ones((C, C), dtype=bool))
    att = jnp.where(causal, jnp.einsum('bnihd,bnjhd->bnhij', q_dec, k_inv), 0.0)
    o_intra = jnp.einsum('bnhij,bnjhv->bnihv', att, vf)
    upd = jnp.einsum('bnjhd,bnjhv->nbhdv', k_end, vf)
    decay = jnp.exp(last[:, :, 0]).transpose(1, 0, 2, 3)

    def step(state, inp):
        dec, u = inp
        return dec[..., None] * state + u, state

    s0 = jnp.zeros((B, GLA_HEADS, GLA_DK, GLA_DV), jnp.float32)
    _, s_prev = lax.scan(step, s0, (decay, upd))
    o_inter = jnp.einsum('bnihd,nbhdv->bnihv', q_dec, s_prev)
    o = (o_intra + o_inter).reshape(B, T, GLA_HEADS, GLA_DV)
    o = _rmsnorm(o, norm_g.astype(jnp.float32)).reshape(B, T, GLA_HEADS * GLA_DV)
    return (o * jax.nn.silu(g_out.astype(jnp.float32))).astype(q.dtype)

def _dsa(q, k, v, q_idx, k_idx, w_idx, q_gain, k_gain, kidx_gain):
    B, T = q.shape[:2]
    topk = min(IDX_TOPK_MAX, T // 4)
    grp = DSA_HEADS // DSA_KV_HEADS
    q = _rmsnorm(q.reshape(B, T, DSA_HEADS, DSA_HEAD_DIM), q_gain) * DSA_HEAD_DIM ** -0.5
    k = _rmsnorm(k.reshape(B, T, DSA_KV_HEADS, DSA_HEAD_DIM), k_gain)
    v = v.reshape(B, T, DSA_KV_HEADS, DSA_HEAD_DIM)
    q_idx = q_idx.reshape(B, T, IDX_HEADS, IDX_DIM)
    k_idx = _rmsnorm(k_idx, kidx_gain)
    w_idx = w_idx * (IDX_HEADS ** -0.5 * IDX_DIM ** -0.5)
    key_pos = jnp.arange(T)

    def block(i):
        start = i * Q_BLOCK
        qb = lax.dynamic_slice_in_dim(q, start, Q_BLOCK, axis=1)
        qib = lax.dynamic_slice_in_dim(q_idx, start, Q_BLOCK, axis=1)
        wb = lax.dynamic_slice_in_dim(w_idx, start, Q_BLOCK, axis=1)
        qpos = start + jnp.arange(Q_BLOCK)
        rel = jax.nn.relu(jnp.einsum('bqhd,bsd->bqhs', qib, k_idx).astype(jnp.float32))
        score = jnp.einsum('bqh,bqhs->bqs', wb.astype(jnp.float32), rel)
        allowed = key_pos[None, :] <= qpos[:, None]
        score = jnp.where(allowed, score, -jnp.inf)
        _, idx = lax.top_k(score, topk)
        valid = idx <= qpos[None, :, None]
        kg = jax.vmap(lambda kk, ii: kk[ii])(k, idx)
        vg = jax.vmap(lambda vv, ii: vv[ii])(v, idx)
        qg = qb.reshape(B, Q_BLOCK, DSA_KV_HEADS, grp, DSA_HEAD_DIM)
        logits = jnp.einsum('bqgrd,bqkgd->bqgrk', qg, kg).astype(jnp.float32)
        logits = jnp.where(valid[:, :, None, None, :], logits, -jnp.inf)
        p = jax.nn.softmax(logits, axis=-1).astype(v.dtype)
        o = jnp.einsum('bqgrk,bqkgd->bqgrd', p, vg)
        return o.reshape(B, Q_BLOCK, DSA_HEADS * DSA_HEAD_DIM)

    out = lax.map(block, jnp.arange(T // Q_BLOCK))
    return out.transpose(1, 0, 2, 3).reshape(B, T, DSA_HEADS * DSA_HEAD_DIM)

def _memory_attn(q, mem_h, w_kv, q_gain, k_gain):
    B, T = q.shape[:2]
    M = mem_h.shape[1]
    q = _rmsnorm(q.reshape(B, T, MEM_HEADS, MEM_HEAD_DIM), q_gain) * MEM_HEAD_DIM ** -0.5
    kv = (mem_h @ w_kv).reshape(B, M, 2, MEM_HEADS, MEM_HEAD_DIM)
    k = _rmsnorm(kv[:, :, 0], k_gain)
    v = kv[:, :, 1]
    logits = jnp.einsum('bthd,bmhd->bhtm', q, k).astype(jnp.float32)
    p = jax.nn.softmax(logits, axis=-1).astype(v.dtype)
    o = jnp.einsum('bhtm,bmhd->bthd', p, v)
    return o.reshape(B, T, MEM_HEADS * MEM_HEAD_DIM)

def _hier_moe(h, w_r1, b_r1, w_r2, b_r2, w_gate, w_up, w_down):
    B, T, D = h.shape
    hf = h.reshape(B * T, D)
    g_logits = (hf @ w_r1 + b_r1).astype(jnp.float32)
    g_prob = jax.nn.softmax(g_logits, axis=-1)
    g_sel = jnp.argmax(g_logits, axis=-1)
    g_w = jnp.take_along_axis(g_prob, g_sel[:, None], axis=-1)
    e_logits = (hf @ w_r2 + b_r2).astype(jnp.float32).reshape(-1, N_GROUPS, EXPERTS_PER_GROUP)
    e_logits = jnp.take_along_axis(e_logits, g_sel[:, None, None], axis=1)[:, 0]
    e_prob = jax.nn.softmax(e_logits, axis=-1)
    top_p, top_i = lax.top_k(e_prob, EXPERT_TOPK)
    top_p = top_p / jnp.sum(top_p, axis=-1, keepdims=True)
    expert_id = g_sel[:, None] * EXPERTS_PER_GROUP + top_i
    combine = jnp.sum(jax.nn.one_hot(expert_id, N_EXPERTS, dtype=jnp.float32)
                      * (g_w * top_p)[..., None], axis=1)
    hid = jax.nn.silu(jnp.einsum('nd,edf->nef', hf, w_gate)) * jnp.einsum('nd,edf->nef', hf, w_up)
    hid = hid * combine[..., None].astype(hid.dtype)
    out = jnp.einsum('nef,efd->nd', hid, w_down)
    return out.reshape(B, T, D)

def second_inputs(seed: int = 0) -> dict:
    key = jax.random.key(seed)
    ks = iter(jax.random.split(key, 40))
    L = DEPTH

    def w(shape, fan_in):
        return jax.random.normal(next(ks), shape, jnp.float32) * fan_in ** -0.5

    def gain(shape):
        return 1.0 + 0.02 * jax.random.normal(next(ks), shape, jnp.float32)

    def bias(shape, s=0.01):
        return s * jax.random.normal(next(ks), shape, jnp.float32)

    return {
        'x': jax.random.normal(next(ks), (BATCH, SEQ, D_MODEL), jnp.float32),
        'mem': jax.random.normal(next(ks), (BATCH, MEM_LEN, D_MODEL), jnp.float32),
        'g_mix': gain((L, D_MODEL)),
        'g_mem': gain((L, D_MODEL)),
        'w_in': w((L, D_MODEL, D_IN), D_MODEL),
        'w_gla_a2': w((L, GLA_GATE_RANK, GLA_HEADS * GLA_DK), GLA_GATE_RANK),
        'b_gla_a2': bias((L, GLA_HEADS * GLA_DK), 0.1),
        'gla_norm': gain((L, GLA_DV)),
        'w_mem_kv': w((L, D_MODEL, 2 * MEM_HEADS * MEM_HEAD_DIM), D_MODEL),
        'dsa_q_norm': gain((L, DSA_HEAD_DIM)),
        'dsa_k_norm': gain((L, DSA_HEAD_DIM)),
        'idx_k_norm': gain((L, IDX_DIM)),
        'mem_q_norm': gain((L, MEM_HEAD_DIM)),
        'mem_k_norm': gain((L, MEM_HEAD_DIM)),
        'b_gate': bias((L, N_BRANCH * D_MODEL), 0.1),
        'w_o_gla': w((L, GLA_HEADS * GLA_DV, D_MODEL), GLA_HEADS * GLA_DV),
        'w_o_dsa': w((L, DSA_HEADS * DSA_HEAD_DIM, D_MODEL), DSA_HEADS * DSA_HEAD_DIM),
        'w_o_mem': w((L, MEM_HEADS * MEM_HEAD_DIM, D_MODEL), MEM_HEADS * MEM_HEAD_DIM),
        'w_out': w((L, D_MODEL, D_MODEL), D_MODEL),
        'g_ffn': gain((L, D_MODEL)),
        'w_r1': w((L, D_MODEL, N_GROUPS), D_MODEL),
        'b_r1': bias((L, N_GROUPS)),
        'w_r2': w((L, D_MODEL, N_EXPERTS), D_MODEL),
        'b_r2': bias((L, N_EXPERTS)),
        'w_gate': w((L, N_EXPERTS, D_MODEL, D_EXPERT), D_MODEL),
        'w_up': w((L, N_EXPERTS, D_MODEL, D_EXPERT), D_MODEL),
        'w_down': w((L, N_EXPERTS, D_EXPERT, D_MODEL), D_EXPERT),
    }

def second_block(x, mem, g_mix, g_mem, w_in, w_gla_a2, b_gla_a2, gla_norm, w_mem_kv,
              dsa_q_norm, dsa_k_norm, idx_k_norm, mem_q_norm, mem_k_norm, b_gate,
              w_o_gla, w_o_dsa, w_o_mem, w_out, g_ffn, w_r1, b_r1, w_r2, b_r2,
              w_gate, w_up, w_down):
    B, T, D = x.shape
    for l in range(DEPTH):
        h = _rmsnorm(x, g_mix[l])
        (gq, gk, gv, gg, ga, dq, dk, dv, iq, ik, iw, mq, gates) = _split_in(h @ w_in[l])
        o_gla = _gla(gq, gk, gv, gg, ga, w_gla_a2[l], b_gla_a2[l], gla_norm[l])
        o_dsa = _dsa(dq, dk, dv, iq, ik, iw, dsa_q_norm[l], dsa_k_norm[l], idx_k_norm[l])
        mem_h = _rmsnorm(mem, g_mem[l])
        o_mem = _memory_attn(mq, mem_h, w_mem_kv[l], mem_q_norm[l], mem_k_norm[l])
        gate = jax.nn.sigmoid((gates + b_gate[l]).astype(jnp.float32)).astype(x.dtype)
        gate = gate.reshape(B, T, N_BRANCH, D)
        merged = (gate[:, :, 0] * (o_gla @ w_o_gla[l])
                  + gate[:, :, 1] * (o_dsa @ w_o_dsa[l])
                  + gate[:, :, 2] * (o_mem @ w_o_mem[l]))
        x = x + merged @ w_out[l]
        x = x + _hier_moe(_rmsnorm(x, g_ffn[l]), w_r1[l], b_r1[l], w_r2[l], b_r2[l],
                          w_gate[l], w_up[l], w_down[l])
    return x


def setup_inputs(seed=0):
    out = dict(first_inputs(seed))
    for name, value in second_inputs(seed + 1).items():
        if name != "x":
            out[name + "_2"] = value
    return out


def reference(
    x, meta_tokens, mix_norm_w, w_in, conv_w, conv_b, lru_wa, lru_ba, lru_wx, lru_bx,
    lru_lambda, w_branch_ret, w_branch_lru, w_out, ffn_norm_w, w_ffn_in, w_ffn_out,
    final_norm_w, mem_2, g_mix_2, g_mem_2, w_in_2, w_gla_a2_2, b_gla_a2_2, gla_norm_2,
    w_mem_kv_2, dsa_q_norm_2, dsa_k_norm_2, idx_k_norm_2, mem_q_norm_2, mem_k_norm_2, b_gate_2,
    w_o_gla_2, w_o_dsa_2, w_o_mem_2, w_out_2, g_ffn_2, w_r1_2, b_r1_2, w_r2_2, b_r2_2, w_gate_2,
    w_up_2, w_down_2,
):
    x = first_block(
        x, meta_tokens, mix_norm_w, w_in, conv_w, conv_b, lru_wa, lru_ba, lru_wx, lru_bx,
        lru_lambda, w_branch_ret, w_branch_lru, w_out, ffn_norm_w, w_ffn_in, w_ffn_out,
        final_norm_w,
    )
    return second_block(
        x, mem_2, g_mix_2, g_mem_2, w_in_2, w_gla_a2_2, b_gla_a2_2, gla_norm_2, w_mem_kv_2,
        dsa_q_norm_2, dsa_k_norm_2, idx_k_norm_2, mem_q_norm_2, mem_k_norm_2, b_gate_2,
        w_o_gla_2, w_o_dsa_2, w_o_mem_2, w_out_2, g_ffn_2, w_r1_2, b_r1_2, w_r2_2, b_r2_2,
        w_gate_2, w_up_2, w_down_2,
    )


_drawn_inputs = setup_inputs


def setup_inputs(seed=0):
    import zlib

    import numpy as np

    out = dict(_drawn_inputs(seed))
    spreads = {}
    factors = {'lru_ba': 8.0,
     'lru_bx': 8.0,
     'g_mem_2': 6.032,
     'gla_norm_2': 35.487,
     'dsa_q_norm_2': 31.674,
     'dsa_k_norm_2': 26.09,
     'mem_q_norm_2': 6.08,
     'mem_k_norm_2': 8.0,
     'b_r1_2': 52.656,
     'b_r2_2': 52.12,
     'idx_k_norm_2': 3.041,
     'g_ffn_2': 8.0}
    for name, (base, spread) in spreads.items():
        noise = np.random.default_rng([zlib.crc32(name.encode()), seed]).standard_normal(out[name].shape)
        drawn = base * np.exp(spread * noise) if base else spread * noise
        out[name] = jnp.asarray(drawn.astype(out[name].dtype))
    for name, factor in factors.items():
        out[name] = (out[name] * factor).astype(out[name].dtype)
    return out
```

```python
from contextlib import ExitStack

import numpy as np

P = 128
T = 256
RT = T // P
D = 1024
KT = D // P
META = 16
TM = META + T
HR = 8
CONV = 4
LRUB = 4
FFN = 2816
FSTEPS = FFN // 256
EXPERTS = 16
GH, GCH = 4, 64
DH, DKVH, DGRP = 8, 2, 4
TOPK = 64
MH = 4
EPS = 1e-6
SLOTS = 6
PW = 2048

PIECES = [("k", 4), ("q", 4), ("v", 4), ("lru_in", 4), ("g_ret", 4), ("lru_gates", 2), ("lru_gate", 4),
          ("gate_a", 4), ("gate_b", 4), ("br_ret", 4), ("br_lru", 4), ("out1", 4), ("mem_k", 4),
          ("ffn", 3 * FSTEPS), ("mem_v", 4), ("iq", 2), ("gq", 2), ("gk", 2), ("gv", 4), ("dkv", 2), ("dq", 4),
          ("gg", 4), ("mq", 4), ("gate0", 4), ("o_gla", 4), ("gate1", 4), ("o_dsa", 4), ("gate2", 4),
          ("o_mem", 4), ("out2", 4), ("moe", 3 * EXPERTS)]
PB, NP = {}, 0
for _name, _n in PIECES:
    PB[_name] = NP
    NP += _n

BANKS = {}
_uses = [0] * 8
_next = 0


def _fill(*names):
    global _next
    for n in names:
        assert n not in BANKS, n
        BANKS[n] = (_next, _uses[_next])
        _uses[_next] += 1
        _next = (_next + 1) % 8


def _n(prefix, *dims):
    out = [prefix]
    for d in dims:
        out = [f"{o}.{i}" for o in out for i in (d if isinstance(d, (list, tuple)) else range(d))]
    return out


_fill(*_n("tx", 4), "txm")
_fill(*_n("k", 2, [0, 1, "m"]), *_n("q", 2, 2), *_n("v", 2, [0, 1, "m"]))
_fill(*_n("tk", 4), "tkm", *_n("tq", 4))
for _p in range(4):
    _fill(f"s.{2 * _p}", f"s.{2 * _p + 1}", f"sm.{_p}", f"li.{2 * _p}", f"li.{2 * _p + 1}", f"o.{_p}")
_fill(*_n("g", 2, 2), *_n("lg", KT, 2), *_n("lgate", 4), *_n("ga", 4), *_n("tm", 4), *_n("gb", 4))
_fill(*_n("tr", 4), *_n("br", 4), *_n("bl", 4), *_n("out1", 2, 2), *_n("mk", 2, 2), *_n("th", 4))
_next = 4
_ffn_uses = list(_uses)
_fill(*_n("mv", 2, 2), *_n("tmk", 4), *_n("t2", 4), "al", "ik.0", "ik.1")
_fill(*_n("z", 2), *_n("iq", 2), *_n("gq", 2), *_n("gk", 2), "tik", *_n("gv", 2, 2))
_fill(*_n("sc0", 4), *_n("sc1", 4), *_n("tke", 4), *_n("dkv", 2), *_n("dq", 2, 2))
for _h in range(GH):
    _fill(f"at.{_h}", f"up.{_h}.0", f"up.{_h}.1", f"og.{_h}")
_fill(*_n("gg", 2, 2), "tdk", *_n("tdq", 4), *_n("mq", 2, 2))
for _g in range(DKVH):
    _fill(f"dl.{_g}.0", f"dl.{_g}.1", f"dl.{_g}.2", f"dp.{_g}.0", f"dp.{_g}.1", f"dp.{_g}.2", f"do.{_g}.0", f"do.{_g}.1")
_fill(*_n("tog", 4), *_n("tmq", 4), *_n("gt0", 4))
_fill(*_n("ml", 4), *_n("mp", 4), *_n("mo", 4))
_fill(*_n("wo0", 4))
for _b in (1, 2):
    for _j in range(4):
        _fill(f"gt{_b}.{_j}")
    for _j in range(4):
        _fill(f"wo{_b}.{_j}")
_fill(*_n("out2", 2, 2), *_n("t3", 4), "rl", "tc", *_n("cb", 8))

CONSTS = [("ident", P), ("tri", P), ("triq", P), ("blk", P), ("cos", RT * P), ("sin", RT * P), ("cosm", P), ("sinm", P),
          ("gown", HR), ("gprev", HR), ("gq", HR), ("gm", 2 * HR), ("rank", 4)]
PARAMS = [("mixw", 8), ("ffnw", 8), ("gmix", 8), ("gmem", 8), ("gffn", 8), ("convw", 32), ("convb", 8), ("ba", 8),
          ("bx", 8), ("lam", 8), ("ba2", 4), ("glan", 2), ("dqn", 1), ("dkn", 1), ("ikn", 1), ("mqn", 2), ("mkn", 2),
          ("bgate", 24), ("brt", 20), ("smallw", 8 * 108), ("wa2", 512)]


def columns(table):
    at, out = 0, {}
    for n, w in table:
        out[n] = (at, at + w)
        at += w
    return out, at


CC, NC_ = columns(CONSTS)
PC, NPAR = columns(PARAMS)


def shape_constants():
    c = np.zeros((P, NC_), np.float32)

    def put(name, a):
        lo, hi = CC[name]
        c[:a.shape[0], lo:hi] = a.reshape(a.shape[0], hi - lo)

    i = np.arange(P)
    put("ident", np.eye(P, dtype=np.float32))
    put("tri", (i[:, None] <= i[None, :]).astype(np.float32))
    put("triq", (i[None, :] <= i[:, None]).astype(np.float32))
    put("blk", ((i[:, None] <= i[None, :]) & (i[:, None] // GCH == i[None, :] // GCH)).astype(np.int32).view(np.float32))
    inv = np.float32(10000.0) ** (-np.arange(0, P, 2, dtype=np.float32) / np.float32(P))
    ang = (np.arange(TM, dtype=np.float32)[:, None] * inv[None, :]).astype(np.float64)
    cos, sin = np.cos(ang).astype(np.float32), np.sin(ang).astype(np.float32)
    cos, sin = np.concatenate([cos, cos], 1), np.concatenate([-sin, sin], 1)
    for name, a in (("cos", cos), ("sin", sin)):
        put(name, a[META:].reshape(RT, P, P).transpose(1, 0, 2))
        put(name + "m", a[:META])
    lg = np.log(1.0 - 2.0 ** (-5.0 - np.arange(HR)))[None, :]
    m, scale = i[:, None].astype(np.float64), float(P) ** -0.5
    put("gown", (np.exp(-(m + 1) * lg) * scale).astype(np.float32))
    put("gprev", (np.exp((P - 1 - m) * lg) * scale).astype(np.float32))
    put("gq", np.exp((m + 1) * lg).astype(np.float32))
    first = np.exp((META - 1 - m[:META]) * lg) * scale
    put("gm", np.stack([first, first * np.exp(P * lg)], 1).astype(np.float32))
    put("rank", np.tile(np.arange(4, 0, -1, dtype=np.float32), (P, 1)))
    return c


def program(nc, weights, x, meta, mem, consts, params, final_w, out):
    import concourse.bass as bass
    from concourse import mybir

    f32, i32 = mybir.dt.float32, mybir.dt.int32
    ALU, ACT, AX = mybir.AluOpType, mybir.ActivationFunctionType, mybir.AxisListType
    V, S, G, E = nc.vector, nc.scalar, nc.gpsimd, nc.tensor
    mult, add, sub, amax, amin = ALU.mult, ALU.add, ALU.subtract, ALU.max, ALU.min

    with ExitStack() as ctx:
        def sb(name, shape, dt=f32):
            return ctx.enter_context(nc.sbuf_tensor(name, shape, dt))

        def sem(name):
            return ctx.enter_context(nc.semaphore(name))

        ring = sb("ring", [P, SLOTS, PW])
        con = sb("con", [P, NC_])
        par = sb("par", [P, NPAR])
        buf = [sb(f"buf{i}", [P, 8 * 275]) for i in range(15)]
        wide = sb("wide", [P, 4096])
        small = sb("small", [P, 640])
        banks = [ctx.enter_context(nc.psum_tensor(f"bank{i}", [P, 512], f32)) for i in range(8)]

        def C(name):
            return con[:, CC[name][0]:CC[name][1]]

        def W(name):
            return par[:, PC[name][0]:PC[name][1]]

        def rows(b, at=0):
            return (wide if b is wide else buf[b])[:, at:at + 2048].rearrange("p (r c) -> p r c", r=RT)

        def cols(b, n=T, at=0):
            return (wide if b is wide else buf[b])[:, at:at + KT * n].rearrange("p (k t) -> p k t", k=KT)

        used = [0]

        def tiny(*dims):
            n = int(np.prod(dims))
            a = small[:, used[0]:used[0] + n]
            used[0] += n
            assert used[0] <= 640
            if len(dims) == 2:
                a = a.rearrange("p (a b) -> p a b", a=dims[0])
            if len(dims) == 3:
                a = a.rearrange("p (a b c) -> p a b c", a=dims[0], b=dims[1])
            return a

        def bc(a, *shape):
            return a.unsqueeze(len(a.shape)).to_broadcast(list(a.shape) + list(shape))

        def bc1(a, n):
            return a.unsqueeze(1).to_broadcast([a.shape[0], n] + list(a.shape[1:]))

        ident = C("ident")
        smallw = W("smallw").rearrange("p (k c) -> p k c", k=KT)

        piece_loaded = [sem(f"piece_loaded{s}") for s in range(SLOTS)]
        pieces_used = sem("pieces_used")
        evacuated = [sem(f"evacuated{b}") for b in range(8)]
        const_loaded, x_loaded, mem_loaded, final_w_loaded = (sem(n) for n in ("const_loaded", "x_loaded", "mem_loaded", "final_w_loaded"))
        out_stored = sem("out_stored")
        dve_chain, act_chain, pool_chain = sem("dve_chain"), sem("act_chain"), sem("pool_chain")
        NORMS = ("x", "mem", "h", "fin", "y", "z")
        squares = {n: sem(f"squares_{n}") for n in NORMS}
        meansq = {n: sem(f"meansq_{n}") for n in NORMS}
        rooted = {n: sem(f"rooted_{n}") for n in NORMS}
        normed = {n: sem(f"normed_{n}") for n in NORMS}
        turned = sem("turned")
        rotated = sem("rotated")
        padded = sem("padded")
        stat_cleared = sem("stat_cleared")
        idx_used, o_reduced, og_reduced = sem("idx_used"), sem("o_reduced"), sem("og_reduced")
        scored = sem("scored")
        retained = sem("retained")
        o_squared, o_summed, o_rooted, o_ready = (sem(n) for n in ("o_squared", "o_summed", "o_rooted", "o_ready"))
        lam_exp, lam_ready = sem("lam_exp"), sem("lam_ready")
        convolved = sem("convolved")
        decay_ready, lru_m2, lru_m, lru_gated, lru_ready = (sem(n) for n in ("decay_ready", "lru_m2", "lru_m", "lru_gated", "lru_ready"))
        mix_part, mixed = sem("mix_part"), sem("mixed")
        ffn_silu, ffn_act, ffn_added = sem("ffn_silu"), sem("ffn_act"), sem("ffn_added")
        mk_squared, mk_summed, mk_rooted, mk_ready = (sem(n) for n in ("mk_squared", "mk_summed", "mk_rooted", "mk_ready"))
        small_full = sem("small_full")
        ik_squared, ik_summed, ik_rooted, ik_ready = (sem(n) for n in ("ik_squared", "ik_summed", "ik_rooted", "ik_ready"))
        la_ready, cum_ready, e_ready, gla_ke = (sem(n) for n in ("la_ready", "cum_ready", "e_ready", "gla_ke"))
        idx_full = sem("idx_full")
        topped = sem("topped")
        gla_full = sem("gla_full")
        og_squared, og_summed, og_rooted, og_ready = (sem(n) for n in ("og_squared", "og_summed", "og_rooted", "og_ready"))
        dk_squared, dk_summed, dk_rooted, dk_ready = (sem(n) for n in ("dk_squared", "dk_summed", "dk_rooted", "dk_ready"))
        dq_squared, dq_summed, dq_rooted, dq_ready = (sem(n) for n in ("dq_squared", "dq_summed", "dq_rooted", "dq_ready"))
        mq_squared, mq_summed, mq_rooted, mq_ready = (sem(n) for n in ("mq_squared", "mq_summed", "mq_rooted", "mq_ready"))
        dsa_full, dsa_max, dsa_exp, dsa_p = (sem(n) for n in ("dsa_full", "dsa_max", "dsa_exp", "dsa_p"))
        mem_full, mem_max, mem_exp, mem_p = (sem(n) for n in ("mem_full", "mem_max", "mem_exp", "mem_p"))
        merged = sem("merged")
        route_full, route_max, route_exp, combined = (sem(n) for n in ("route_full", "route_max", "route_exp", "combined"))
        moe_silu, moe_scaled, moe_act, moe_added = (sem(n) for n in ("moe_silu", "moe_scaled", "moe_act", "moe_added"))

        X = rows(0)
        XN, XT = rows(1), cols(2, TM)
        KR, QR, KTr, QTr, Vr = rows(3), rows(4), cols(5), cols(6), rows(7)
        LI = cols(8, TM + CONV - 1)
        CV = cols(9, TM)
        ROT = buf[10][:, 0:2048].rearrange("p (a b c) -> p a b c", a=2, b=2)
        ST = buf[11][:, 0:4 * 384].rearrange("p (h c) -> p h c", h=4)
        VM, KM = buf[12][0:META, 0:1024], buf[12][0:META, 1024:2048]
        KTM = buf[12][:, 2048:2048 + 128].rearrange("p (h t) -> p h t", h=HR)
        MR, MT = rows(13), cols(14)
        XM = wide[0:META, 3072:4096]
        SMT = wide[0:META, 0:1024].rearrange("p (a h t) -> p a h t", a=2, h=2)
        SQ = wide[:, 1024:2048].rearrange("p (a c) -> p a c", a=2)
        GR = rows(wide, 2048)
        O = rows(1)
        RG, IG, TH, AA, A2, HS = cols(3, TM), cols(4, TM), cols(10, TM), cols(8, TM), cols(11, TM), cols(9, TM)
        LT, GA, GB, RTt = cols(5), cols(6), cols(7), cols(12)
        MIX = cols(wide)
        PART = buf[11][:, 0:1024].rearrange("p (a c) -> p a c", a=2)
        HT = cols(2)
        SILU = buf[10][:, 0:1024].rearrange("p (a c) -> p a c", a=2)
        SILC = buf[10][:, 1024:2048].rearrange("p (a c) -> p a c", a=2)
        HID = buf[11][:, 1024:2048].rearrange("p (a f t) -> p a f t", a=2, f=2)
        FW = buf[9][:, 0:1024]
        MKR, MKT, MV = rows(3), cols(6), rows(7)
        MSQ = buf[13][:, 0:1024].rearrange("p (a c) -> p a c", a=2)
        g4 = lambda a: a.rearrange("p (h t) -> p h t", h=GH)
        ZA, ZB = buf[3][:, 0:1024], buf[3][:, 1024:2048]
        CUM, EC = buf[4][:, 0:1024], buf[4][:, 1024:2048]
        EI, RM = buf[5][:, 0:1024], buf[5][:, 1024:2048]
        QD, KI = g4(buf[8][:, 0:1024]), g4(buf[8][:, 1024:2048])
        KET = g4(buf[9][:, 0:1024])
        KE = buf[9][:, 1024:2048].rearrange("p (h r d) -> p h r d", h=GH, r=RT)
        GV = rows(10)
        ST8 = buf[11][:, 0:1536].rearrange("p (a n c) -> p a n c", a=2, n=3)
        OG, GG, OGT = rows(12), rows(13), cols(10)
        IQT = g4(buf[14][:, 0:1024])
        IKT, IKR = buf[14][:, 1024:1280], buf[14][:, 1280:1536].rearrange("p (r c) -> p r c", r=RT)
        SC = (buf[14][:, 1536:1664], buf[14][:, 1664:1920])
        RL = wide[:, 0:1024].rearrange("p (a c) -> p a c", a=2)
        WK = (wide[:, 1024:1152], wide[:, 1152:1408])
        MB = (wide[:, 1408:1536], wide[:, 1536:1792])
        DQR, DKV = rows(4), buf[5][:, 0:1024].rearrange("p (r c) -> p r c", r=RT)
        DSQ = buf[5][:, 1024:2048].rearrange("p (a c) -> p a c", a=2)
        DQT, DKT = cols(3), wide[:, 2048:2560].rearrange("p (g t) -> p g t", g=DKVH)
        DP = wide[:, 2560:4096].rearrange("p (a c) -> p a c", a=3)
        DPT0 = buf[14][:, 0:512]
        DPT1 = buf[14][:, 512:1536].rearrange("p (s c) -> p s c", s=2)
        ODT = cols(8)
        MQR, MQT = rows(11), cols(12)
        MP = buf[5][:, 0:2048].rearrange("p (a c) -> p a c", a=4)
        MPT = buf[9][:, 0:2048].rearrange("p (h s t) -> p h s t", h=MH, s=2)
        OMT = cols(4)
        GS = cols(1)
        SG = buf[14][:, 0:2048].rearrange("p (a c) -> p a c", a=4)
        MPART = buf[3][:, 0:1024].rearrange("p (a c) -> p a c", a=2)
        MRG = cols(13)
        CB = wide[:, :].rearrange("p (e t) -> p e t", e=EXPERTS)
        GSQ = wide[:, 0:1024]
        ATM = wide[:, 3072:3584].rearrange("p (a c) -> p a c", a=2)

        stat = {n: tiny(3) for n in NORMS}
        oss, mkss, ogss = tiny(RT, HR), tiny(RT, MH), tiny(RT, GH)
        ikss, dkss, dqss, mqss = tiny(RT), tiny(RT, DKVH), tiny(RT, DH), tiny(RT, MH)
        lam = [tiny(8) for _ in range(6)]
        sp8, nsp8 = tiny(8), tiny(8)
        iwr = tiny(RT, 8)
        dec = tiny(GH, 4)
        top8 = tiny(RT, 8)
        dmx, dsum, mmx, msum = tiny(RT, DH), tiny(RT, DH), tiny(MH, RT), tiny(MH, RT)
        lr = tiny(RT, 20)
        gmx, gsh, gex, gsm, oh = tiny(RT), tiny(RT, 4), tiny(RT, 4), tiny(RT), tiny(RT, 4)
        el, eex, oh1, oh2, emx, tmp4, tmp16 = tiny(RT, 4), tiny(RT, 4), tiny(RT, 4), tiny(RT, 4), tiny(RT), tiny(RT, 4), tiny(RT, 4, 4)
        cmb = tiny(RT, 16)
        ALT = buf[14][0:16, 1920:2176]
        CT = buf[14][0:16, 0:256]

        def full(eng, name):
            eng.wait_ge(pieces_used, name)

        def moved(eng, *names):
            for n in names:
                b, use = BANKS[n]
                eng.wait_ge(evacuated[b], use + 1)

        def release(ins, name):
            return ins.then_inc(evacuated[BANKS[name][0]], 1)

        def bank(name):
            return banks[BANKS[name][0]]

        class Chain:
            def __init__(self, eng, s):
                self.eng, self.s, self.n = eng, s, 0

            def __call__(self, ins):
                self.n += 1
                ins.then_inc(self.s, 1)
                self.eng.wait_ge(self.s, self.n)

        turns = {}
        for i, n in enumerate([*_n("tx", 4), "txm", *_n("tk", 4), "tkm", *_n("tq", 4), *_n("tm", 4), *_n("tr", 4), *_n("th", 4),
                               *_n("tmk", 4), *_n("t2", 4), "tik", *_n("tke", 4), "tdk", *_n("tdq", 4), *_n("tog", 4),
                               *_n("tmq", 4), *_n("t3", 4), "tc"]):
            turns[n] = i + 1

        block = ctx.enter_context(nc.Block())

        @block.sync
        def _(sp):
            for n in range(SLOTS):
                sp.dma_start(ring[:, n, :], weights[n]).then_inc(piece_loaded[n], 16)
            laps = (NP - SLOTS) // SLOTS
            with sp.Fori(0, laps) as lap:
                for s in range(SLOTS):
                    sp.wait_ge(pieces_used, lap * SLOTS + (s + 1))
                    sp.dma_start(ring[:, s, :], weights[bass.ds(lap * SLOTS + (SLOTS + s), 1), :, :].rearrange("a p c -> p (a c)"))\
                        .then_inc(piece_loaded[s], 16)
            for n in range((laps + 1) * SLOTS, NP):
                sp.wait_ge(pieces_used, n - SLOTS + 1)
                sp.dma_start(ring[:, n % SLOTS, :], weights[n]).then_inc(piece_loaded[n % SLOTS], 16)
            for r in range(RT):
                sp.wait_ge(moe_added, 2 * r + 2)
                sp.dma_start(out[r * P:(r + 1) * P, :], X[:, r, :]).then_inc(out_stored, 16)
            sp.wait_ge(out_stored, 16 * RT)

        @block.tensor
        def _(pe):
            order = iter(BANKS)

            def begin(name):
                assert next(order) == name, name
                b, use = BANKS[name]
                if use:
                    pe.wait_ge(evacuated[b], use)
                return banks[b]

            def piece(n):
                pe.wait_ge(piece_loaded[n % SLOTS], 16 * (n // SLOTS + 1))
                return ring[:, n % SLOTS, :]

            def cols_product(n, act, names, width=T, k0=0):
                w = piece(n).rearrange("p (k c) -> p k c", k=KT)
                outs = [begin(x) for x in names]
                for c in range(2):
                    o = outs[c][:, 0:width] if len(outs) == 2 else outs[0][:, c * width:(c + 1) * width]
                    for k in range(KT):
                        last = E.matmul(o, w[:, k, c * P:(c + 1) * P], act[:, k, :], start=k == 0, stop=k == KT - 1)
                last.then_inc(pieces_used, 1)

            def rows_product(n, act, names, tiles):
                outs = [begin(x) for x in names]
                for half in range(2):
                    w = piece(n + half).rearrange("p (k c) -> p k c", k=4)
                    for o, (lo, hi) in zip(outs, tiles):
                        for k in range(4):
                            last = E.matmul(o[0:hi - lo, :], act[:, 4 * half + k, lo:hi], w[:, k, :],
                                            start=half == 0 and k == 0, stop=half == 1 and k == 3)
                    last.then_inc(pieces_used, 1)

            TX = [(META, META + P), (META + P, TM)]
            TT = [(0, P), (P, T)]

            def turn(name, pairs):
                b = begin(name)
                for o, i in pairs:
                    n = i.shape[0]
                    last = E.transpose(b[0:i.shape[1], o:o + n], i, ident[0:n, 0:n])
                last.then_inc(turned, 1)

            def turn_rows(prefix, src):
                for j in range(4):
                    turn(f"{prefix}.{j}", [(kk * T + r * P, src[:, r, (2 * j + kk) * P:(2 * j + kk + 1) * P])
                                           for kk in range(2) for r in range(RT)])

            pe.wait_ge(const_loaded, 32)
            pe.wait_ge(normed["x"], 3)
            turn_rows("tx", XN)
            turn("txm", [(k * META, XM[:, k * P:(k + 1) * P]) for k in range(KT)])
            moved(pe, *_n("tx", 4), "txm")
            for c in range(2):
                rows_product(PB["k"] + 2 * c, XT, _n(f"k.{c}", [0, 1, "m"]), TX + [(0, META)])
            for c in range(2):
                rows_product(PB["q"] + 2 * c, XT, _n(f"q.{c}", 2), TX)
            for c in range(2):
                rows_product(PB["v"] + 2 * c, XT, _n(f"v.{c}", [0, 1, "m"]), TX + [(0, META)])
            pe.wait_ge(rotated, 6)
            for j in range(4):
                turn(f"tk.{j}", [(hh * T + r * P, KR[:, r, (2 * j + hh) * P:(2 * j + hh + 1) * P]) for hh in range(2) for r in range(RT)])
            turn("tkm", [(h * META, KM[:, h * P:(h + 1) * P]) for h in range(HR)])
            pe.wait_ge(rotated, 10)
            for j in range(4):
                turn(f"tq.{j}", [(hh * T + r * P, QR[:, r, (2 * j + hh) * P:(2 * j + hh + 1) * P]) for hh in range(2) for r in range(RT)])
            moved(pe, *_n("tk", 4), "tkm", *_n("tq", 4), *_n("v", 2, [0, 1, "m"]))
            for p in range(4):
                for h in (2 * p, 2 * p + 1):
                    b = begin(f"s.{h}")
                    E.matmul(b[:, 0:T], KTr[:, h, 0:P], QTr[:, h, :], start=True, stop=True)
                    E.matmul(b[:, T:T + P], KTr[:, h, P:T], QTr[:, h, P:T], start=True, stop=True).then_inc(scored, 1)
                b = begin(f"sm.{p}")
                for hh in range(2):
                    h = 2 * p + hh
                    last = E.matmul(b[0:META, hh * T:(hh + 1) * T], KTM[:, h, :], QTr[:, h, :], start=True, stop=True)
                last.then_inc(scored, 1)
                cols_product(PB["lru_in"] + p, XT, [f"li.{2 * p}", f"li.{2 * p + 1}"], TM)
                b = begin(f"o.{p}")
                moved(pe, f"s.{2 * p}", f"s.{2 * p + 1}", f"sm.{p}")
                for hh in range(2):
                    h = 2 * p + hh
                    hc = slice(h * P, (h + 1) * P)
                    s, sm = ST[:, h % 4, :], SMT[:, p % 2, hh, :]
                    for r in range(RT):
                        o = b[:, (hh * RT + r) * P:(hh * RT + r + 1) * P]
                        E.matmul(o, s[:, 0:P] if r == 0 else s[:, 2 * P:3 * P], Vr[:, r, hc], start=True, stop=False)
                        if r:
                            E.matmul(o, s[:, P:2 * P], Vr[:, 0, hc], start=False, stop=False)
                        last = E.matmul(o, sm[:, r * P:(r + 1) * P], VM[:, hc], start=False, stop=True)
                last.then_inc(retained, 1)
            for c in range(2):
                rows_product(PB["g_ret"] + 2 * c, XT, _n(f"g.{c}", 2), TX)
            wa = piece(PB["lru_gates"]).rearrange("p (g k c) -> p g k c", g=LRUB, k=2)
            wx = piece(PB["lru_gates"] + 1).rearrange("p (g k c) -> p g k c", g=LRUB, k=2)
            pe.wait_ge(convolved, KT)
            for kt in range(KT):
                g, c = kt // 2, kt % 2
                for which, w in enumerate((wa, wx)):
                    b = begin(f"lg.{kt}.{which}")
                    for k in range(2):
                        last = E.matmul(b[:, 0:TM], w[:, g, k, c * P:(c + 1) * P], CV[:, 2 * g + k, :], start=k == 0, stop=k == 1)
                    if kt < KT - 1:
                        last.then_inc(small_full, 1)
                    else:
                        last.then_inc(pieces_used, 1)
            for j in range(4):
                cols_product(PB["lru_gate"] + j, XT[:, :, META:], [f"lgate.{j}"])
            for j in range(4):
                cols_product(PB["gate_a"] + j, XT[:, :, META:], [f"ga.{j}"])
            pe.wait_ge(normed["mem"], RT)
            turn_rows("tm", MR)
            for j in range(4):
                cols_product(PB["gate_b"] + j, XT[:, :, META:], [f"gb.{j}"])
            pe.wait_ge(o_ready, 1)
            turn_rows("tr", O)
            moved(pe, *_n("tr", 4))
            for j in range(4):
                cols_product(PB["br_ret"] + j, RTt, [f"br.{j}"])
            pe.wait_ge(lru_ready, 1)
            for j in range(4):
                cols_product(PB["br_lru"] + j, LT, [f"bl.{j}"])
            pe.wait_ge(mixed, 4)
            for c in range(2):
                rows_product(PB["out1"] + 2 * c, MIX, _n(f"out1.{c}", 2), TT)
            moved(pe, *_n("tm", 4))
            for c in range(2):
                rows_product(PB["mem_k"] + 2 * c, MT, _n(f"mk.{c}", 2), TT)
            pe.wait_ge(normed["h"], RT)
            turn_rows("th", XN)
            moved(pe, *_n("th", 4))

            def up_step(base, s, ready_gate=None, ready_up=None):
                for which, ready in ((0, ready_gate), (1, ready_up)):
                    sl, lap = base[which]
                    pe.wait_ge(piece_loaded[sl], lap)
                    w = ring[:, sl, :].rearrange("p (k c) -> p k c", k=KT)
                    if ready is not None:
                        pe.wait_ge(*ready)
                    b = banks[4 + 2 * (s % 2) + which]
                    for c in range(2):
                        for k in range(KT):
                            last = E.matmul(b[:, c * T:(c + 1) * T], w[:, k, c * P:(c + 1) * P], HT[:, k, :], start=k == 0, stop=k == KT - 1)
                    last.then_inc(pieces_used, 1)

            def down_step(where, s, act_sem, act_count, first=False, final=False):
                sl, lap = where
                pe.wait_ge(piece_loaded[sl], lap)
                w = ring[:, sl, :].rearrange("p (f c) -> p f c", f=2)
                pe.wait_ge(act_sem, act_count)
                for f in range(2):
                    for r in range(RT):
                        for c in range(2):
                            last = E.matmul(banks[2 * r + c][:, :], HID[:, s % 2, f, r * P:(r + 1) * P], w[:, f, c * 512:(c + 1) * 512],
                                            start=first and f == 0, stop=final and f == 1)
                last.then_inc(pieces_used, 1)

            def hidden(base, steps, silu_done, act_done):
                def at(n, it=0):
                    return (base + n) % SLOTS, it * 16 + ((base + n) // SLOTS + 1) * 16

                up_step([at(0), at(1)], 0)
                up_step([at(2), at(3)], 1)
                down_step(at(4), 0, act_done, 1, first=True)
                pairs = (steps - 2) // 2
                with pe.Fori(0, pairs) as it:
                    for u in range(2):
                        n = 5 + 3 * u
                        up_step([at(n, it), at(n + 1, it)], u, (silu_done, it * 2 + (1 + u)), (act_done, it * 2 + (1 + u)))
                        down_step(at(n + 2, it), 1 + u, act_done, it * 2 + (2 + u))
                s = 1 + 2 * pairs
                while s < steps - 1:
                    n = 2 + 3 * s
                    up_step([at(n), at(n + 1)], s + 1, (silu_done, s), (act_done, s))
                    down_step(at(n + 2), s, act_done, s + 1)
                    s += 1
                down_step(at(3 * steps - 1), steps - 1, act_done, steps, final=True)

            for b in range(8):
                pe.wait_ge(evacuated[b], _ffn_uses[b])
            hidden(PB["ffn"], FSTEPS, ffn_silu, ffn_act)
            pe.wait_ge(ffn_silu, FSTEPS)
            for c in range(2):
                rows_product(PB["mem_v"] + 2 * c, MT, _n(f"mv.{c}", 2), TT)
            pe.wait_ge(ffn_added, 4)
            pe.wait_ge(mk_ready, 1)
            turn_rows("tmk", MKR)
            pe.wait_ge(normed["y"], RT)
            turn_rows("t2", XN)
            moved(pe, *_n("t2", 4))
            b = begin("al")
            for k in range(KT):
                last = E.matmul(b[0:16, 0:T], smallw[:, k, 0:16], HT[:, k, :], start=k == 0, stop=k == KT - 1)
            last.then_inc(small_full, 1)
            for r in range(RT):
                b = begin(f"ik.{r}")
                for k in range(KT):
                    last = E.matmul(b[:, 0:72], HT[:, k, r * P:(r + 1) * P], smallw[:, k, 16:88], start=k == 0, stop=k == KT - 1)
                last.then_inc(small_full, 1)
            moved(pe, "al")
            for j in range(2):
                b = begin(f"z.{j}")
                for hh in range(2):
                    h = 2 * j + hh
                    last = E.matmul(b[:, hh * T:(hh + 1) * T], W("wa2")[0:16, h * P:(h + 1) * P], ALT, start=True, stop=True)
                last.then_inc(small_full, 1)
            for j in range(2):
                cols_product(PB["iq"] + j, HT, [f"iq.{j}"])
            for j in range(2):
                cols_product(PB["gq"] + j, HT, [f"gq.{j}"])
            for j in range(2):
                cols_product(PB["gk"] + j, HT, [f"gk.{j}"])
            pe.wait_ge(ik_ready, 1)
            turn("tik", [(r * P, IKR[:, r, :]) for r in range(RT)])
            for c in range(2):
                rows_product(PB["gv"] + 2 * c, HT, _n(f"gv.{c}", 2), TT)
            moved(pe, "tik", "iq.0", "iq.1")
            for r, n in enumerate((P, T)):
                for j in range(4):
                    b = begin(f"sc{r}.{j}")
                    half = slice(64 * (j % 2), 64 * (j % 2) + 64)
                    for hh in range(2):
                        last = E.matmul(b[:, hh * n:(hh + 1) * n], IQT[half, 2 * (j // 2) + hh, r * P:(r + 1) * P], IKT[half, 0:n], start=True, stop=True)
                    last.then_inc(idx_full, 1)
            pe.wait_ge(gla_ke, 1)
            for h in range(GH):
                turn(f"tke.{h}", [(r * P, KET[:, h, r * P:(r + 1) * P]) for r in range(RT)])
            rows_product(PB["dkv"], HT, _n("dkv", 2), TT)
            for c in range(2):
                rows_product(PB["dq"] + 2 * c, HT, _n(f"dq.{c}", 2), TT)
            moved(pe, *_n("tke", 4), *_n("gv", 2, 2), "gk.0", "gk.1", "gq.0", "gq.1")
            pe.wait_ge(gla_ke, 1)
            for h in range(GH):
                hv = slice(h * T, (h + 1) * T)
                b = begin(f"at.{h}")
                for r in range(RT):
                    last = E.matmul(b[:, r * P:(r + 1) * P], KI[:, h, r * P:(r + 1) * P], QD[:, h, r * P:(r + 1) * P], start=True, stop=True)
                last.then_inc(gla_full, 1)
                b = begin(f"up.{h}.0")
                for r in range(RT):
                    last = E.matmul(b[:, r * T:(r + 1) * T], KE[0:GCH, h, r, :], GV[0:GCH, r, hv], start=True, stop=True)
                last.then_inc(gla_full, 1)
                b = begin(f"up.{h}.1")
                E.matmul(b[:, 0:T], KE[GCH:P, h, 0, :], GV[GCH:P, 0, hv], start=True, stop=True).then_inc(gla_full, 1)
                b = begin(f"og.{h}")
                moved(pe, f"at.{h}", f"up.{h}.0", f"up.{h}.1")
                for r in range(RT):
                    E.matmul(b[:, r * T:(r + 1) * T], ATM[:, h % 2, r * P:(r + 1) * P], GV[:, r, hv], start=True, stop=True, skip_group_check=True)
                    for n in range(2):
                        chunk = 2 * r + n
                        if chunk:
                            last = E.matmul(b[GCH * n:GCH * (n + 1), r * T:(r + 1) * T], QD[:, h, GCH * chunk:GCH * (chunk + 1)],
                                            ST8[:, h % 2, chunk - 1, :], start=False, stop=True, skip_group_check=True)
                last.then_inc(gla_full, 1)
            for c in range(2):
                rows_product(PB["gg"] + 2 * c, HT, _n(f"gg.{c}", 2), TT)
            pe.wait_ge(dk_ready, 1)
            turn("tdk", [(g * T + r * P, DKV[:, r, g * P:(g + 1) * P]) for g in range(DKVH) for r in range(RT)])
            pe.wait_ge(dq_ready, 1)
            turn_rows("tdq", DQR)
            for c in range(2):
                rows_product(PB["mq"] + 2 * c, HT, _n(f"mq.{c}", 2), TT)
            moved(pe, "tdk", *_n("tdq", 4), *_n("dkv", 2))
            for g in range(DKVH):
                for n in range(3):
                    b = begin(f"dl.{g}.{n}")
                    for hh in range(4 if n == 0 else 2):
                        h = DGRP * g + (hh if n == 0 else 2 * (n - 1) + hh)
                        keys, r = (P, 0) if n == 0 else (T, 1)
                        last = E.matmul(b[:, hh * keys:(hh + 1) * keys], DQT[:, h, r * P:(r + 1) * P], DKT[:, g, 0:keys], start=True, stop=True)
                    last.then_inc(dsa_full, 1)
                for n in range(3):
                    b = begin(f"dp.{g}.{n}")
                    pe.wait_ge(dsa_p, 3 * g + (1 if n == 0 else 3))
                    for hh in range(4):
                        if n == 0:
                            src = DP[:, 0, hh * P:(hh + 1) * P]
                        else:
                            src = DP[:, 1 + hh // 2, (hh % 2) * T + (n - 1) * P:(hh % 2) * T + n * P]
                        last = E.transpose(b[:, hh * P:(hh + 1) * P], src, ident)
                    last.then_inc(dsa_full, 1)
                for r in range(RT):
                    b = begin(f"do.{g}.{r}")
                    vc = slice(DKVH * P + g * P, DKVH * P + (g + 1) * P)
                    if r == 0:
                        moved(pe, f"dp.{g}.0")
                        E.matmul(b[:, :], DKV[:, 0, vc], DPT0, start=True, stop=True).then_inc(dsa_full, 1)
                    else:
                        moved(pe, f"dp.{g}.1", f"dp.{g}.2")
                        for s in range(2):
                            last = E.matmul(b[:, :], DKV[:, s, vc], DPT1[:, s, :], start=s == 0, stop=s == 1)
                        last.then_inc(dsa_full, 1)
            pe.wait_ge(og_ready, 1)
            turn_rows("tog", OG)
            pe.wait_ge(mq_ready, 1)
            turn_rows("tmq", MQR)
            for j in range(4):
                cols_product(PB["gate0"] + j, HT, [f"gt0.{j}"])
            moved(pe, *_n("tmq", 4), *_n("tmk", 4), *_n("mv", 2, 2))
            for j in range(4):
                r = j // 2
                b = begin(f"ml.{j}")
                for hh in range(2):
                    h = 2 * (j % 2) + hh
                    for k in range(2):
                        last = E.matmul(b[:, hh * T:(hh + 1) * T], MQT[:, 2 * h + k, r * P:(r + 1) * P], MKT[:, 2 * h + k, :], start=k == 0, stop=k == 1)
                last.then_inc(mem_full, 1)
            pe.wait_ge(mem_p, 4)
            for h in range(MH):
                b = begin(f"mp.{h}")
                for s in range(2):
                    for r in range(RT):
                        last = E.transpose(b[:, s * T + r * P:s * T + (r + 1) * P],
                                           MP[:, 2 * r + h // 2, (h % 2) * T + s * P:(h % 2) * T + (s + 1) * P], ident)
                last.then_inc(mem_full, 1)
            for h in range(MH):
                b = begin(f"mo.{h}")
                moved(pe, f"mp.{h}")
                for c in range(2):
                    for s in range(2):
                        last = E.matmul(b[:, c * T:(c + 1) * T], MV[:, s, h * T + c * P:h * T + (c + 1) * P], MPT[:, h, s, :], start=s == 0, stop=s == 1)
                last.then_inc(mem_full, 1)
            moved(pe, *_n("tog", 4))
            for j in range(4):
                cols_product(PB["o_gla"] + j, OGT, [f"wo0.{j}"])
            for i, (gate, proj, act) in enumerate((("gate1", "o_dsa", ODT), ("gate2", "o_mem", OMT))):
                for j in range(4):
                    cols_product(PB[gate] + j, HT, [f"gt{i + 1}.{j}"])
                if i == 0:
                    moved(pe, *_n("do", 2, 2))
                else:
                    moved(pe, *_n("mo", 4))
                for j in range(4):
                    cols_product(PB[proj] + j, act, [f"wo{i + 1}.{j}"])
            pe.wait_ge(merged, 8)
            for c in range(2):
                rows_product(PB["out2"] + 2 * c, MRG, _n(f"out2.{c}", 2), TT)
            pe.wait_ge(normed["z"], RT)
            turn_rows("t3", XN)
            moved(pe, *_n("t3", 4))
            b = begin("rl")
            for r in range(RT):
                for k in range(KT):
                    last = E.matmul(b[:, r * 20:(r + 1) * 20], HT[:, k, r * P:(r + 1) * P], smallw[:, k, 88:108], start=k == 0, stop=k == KT - 1)
            last.then_inc(route_full, 1)
            pe.wait_ge(combined, 1)
            turn("tc", [(r * P, cmb[:, r, :]) for r in range(RT)])
            moved(pe, "tc")
            for j in range(8):
                b = begin(f"cb.{j}")
                for e in range(2):
                    sel = ident[0:16, 2 * j + e:2 * j + e + 1].to_broadcast([16, P])
                    last = E.matmul(b[:, e * T:(e + 1) * T], sel, CT, start=True, stop=True)
                last.then_inc(route_full, 1)
            moved(pe, *_n("cb", 8))
            hidden(PB["moe"], EXPERTS, moe_silu, moe_act)
            assert next(order, None) is None

        @block.scalar
        def _(act):
            chain = Chain(act, act_chain)

            def A(out_, in_, func, **kw):
                return S.activation(out_, in_, func, **kw)

            act.dma_start(X, x.rearrange("(r p) c -> p r c", p=P)).then_inc(x_loaded, 16)
            act.dma_start(XM, meta).then_inc(x_loaded, 16)
            act.dma_start(con[:, :], consts).then_inc(const_loaded, 16)
            act.dma_start(par[:, :], params).then_inc(const_loaded, 16)
            act.dma_start(MR, mem.rearrange("(r p) c -> p r c", p=P)).then_inc(mem_loaded, 16)

            def row_squares(name, src):
                for r in range(RT):
                    A(XN[:, r, :], src[:, r, :], ACT.Square, accum_out=stat[name][:, r:r + 1]).then_inc(squares[name], 1)

            def row_roots(name, n=RT):
                act.wait_ge(meansq[name], 1)
                A(stat[name][:, 0:n], stat[name][:, 0:n], ACT.Sqrt).then_inc(rooted[name], 1)

            act.wait_ge(x_loaded, 32)
            act.wait_ge(stat_cleared, 1)
            row_squares("x", X)
            A(ROT[0:META, 0, :, :].rearrange("p a c -> p (a c)"), XM, ACT.Square, accum_out=stat["x"][0:META, 2:3]).then_inc(squares["x"], 1)
            row_roots("x", 3)
            act.wait_ge(const_loaded, 32)
            chain(A(lam[0], W("lam"), ACT.Abs))
            A(lam[1], lam[0], ACT.Exp, scale=-1.0).then_inc(lam_exp, 1)
            for c in range(2):
                full(act, PB["v"] + 2 * c + 2)
                for r in range(RT):
                    release(A(Vr[:, r, c * 512:(c + 1) * 512], bank(f"v.{c}.{r}")[:, :], ACT.Copy), f"v.{c}.{r}")
                release(A(VM[:, c * 512:(c + 1) * 512], bank(f"v.{c}.m")[0:META, :], ACT.Copy), f"v.{c}.m")
            for j in range(4):
                act.wait_ge(turned, turns[f"tk.{j}"])
                release(A(KTr[:, 2 * j:2 * j + 2, :], bank(f"tk.{j}")[:, :].rearrange("p (k t) -> p k t", k=2), ACT.Copy), f"tk.{j}")
            act.wait_ge(turned, turns["tkm"])
            release(A(KTM, bank("tkm")[:, 0:P].rearrange("p (h t) -> p h t", h=HR), ACT.Copy), "tkm")
            for j in range(4):
                act.wait_ge(turned, turns[f"tq.{j}"])
                release(A(QTr[:, 2 * j:2 * j + 2, :], bank(f"tq.{j}")[:, :].rearrange("p (k t) -> p k t", k=2), ACT.Copy), f"tq.{j}")
            gm = C("gm").rearrange("p (c h) -> p c h", c=2)
            act.wait_ge(padded, 1)
            for p in range(4):
                act.wait_ge(scored, 3 * p + 3)
                if p >= 2:
                    act.wait_ge(retained, p - 1)
                for hh in range(2):
                    for r in range(RT):
                        last = A(SMT[:, p % 2, hh, r * P:(r + 1) * P], bank(f"sm.{p}")[0:META, hh * T + r * P:hh * T + (r + 1) * P], ACT.Copy,
                                 scale=gm[0:META, r, 2 * p + hh:2 * p + hh + 1])
                release(last, f"sm.{p}")
                full(act, PB["lru_in"] + p + 1)
                for c in range(2):
                    release(A(LI[:, 2 * p + c, CONV - 1:], bank(f"li.{2 * p + c}")[:, 0:TM], ACT.Copy), f"li.{2 * p + c}")
                act.wait_ge(retained, p + 1)
                for hh in range(2):
                    h = 2 * p + hh
                    last = A(O[:, :, h * P:(h + 1) * P], bank(f"o.{p}")[:, hh * T:(hh + 1) * T].rearrange("p (r c) -> p r c", r=RT), ACT.Copy,
                             scale=C("gq")[:, h:h + 1])
                release(last, f"o.{p}")
            act.wait_ge(o_summed, 1)
            A(oss, oss, ACT.Sqrt).then_inc(o_rooted, 1)
            act.wait_ge(o_squared, 4)
            for c in range(2):
                full(act, PB["g_ret"] + 2 * c + 2)
                for r in range(RT):
                    release(A(GR[:, r, c * 512:(c + 1) * 512], bank(f"g.{c}.{r}")[:, :], ACT.Silu), f"g.{c}.{r}")
            act.wait_ge(o_rooted, 1)
            for kt in range(KT):
                for which, (dst, bias) in enumerate(((RG, "ba"), (IG, "bx"))):
                    n = 2 * kt + which + 1
                    if kt < KT - 1:
                        act.wait_ge(small_full, n)
                    else:
                        full(act, PB["lru_gates"] + which + 1)
                    release(A(dst[:, kt, :], bank(f"lg.{kt}.{which}")[:, 0:TM], ACT.Sigmoid, bias=W(bias)[:, kt:kt + 1]), f"lg.{kt}.{which}")
            moved(act, "lg.7.0")
            act.wait_ge(lam_ready, 1)
            for kt in range(KT):
                A(TH[:, kt, :], RG[:, kt, :], ACT.Tanh, scale=sp8[:, kt:kt + 1])
                last = A(AA[:, kt, :], RG[:, kt, :], ACT.Exp, scale=nsp8[:, kt:kt + 1])
            chain(last)
            A(A2, AA, ACT.Square).then_inc(decay_ready, 1)
            for j in range(4):
                full(act, PB["lru_gate"] + j + 1)
                release(A(LT[:, 2 * j:2 * j + 2, :], bank(f"lgate.{j}")[:, :].rearrange("p (k t) -> p k t", k=2), ACT.Gelu_apprx_tanh), f"lgate.{j}")
            act.wait_ge(lru_m2, 1)
            A(TH, TH, ACT.Sqrt).then_inc(lru_m, 1)
            act.wait_ge(mem_loaded, 16)
            for r in range(RT):
                A(MT.rearrange("p k t -> p (k t)")[:, r * D:(r + 1) * D], MR[:, r, :], ACT.Square, accum_out=stat["mem"][:, r:r + 1]).then_inc(squares["mem"], 1)
            row_roots("mem")
            for j in range(4):
                full(act, PB["gate_a"] + j + 1)
                release(A(GA[:, 2 * j:2 * j + 2, :], bank(f"ga.{j}")[:, :].rearrange("p (k t) -> p k t", k=2), ACT.Sigmoid), f"ga.{j}")
            for j in range(4):
                full(act, PB["gate_b"] + j + 1)
                release(A(GB[:, 2 * j:2 * j + 2, :], bank(f"gb.{j}")[:, :].rearrange("p (k t) -> p k t", k=2), ACT.Sigmoid), f"gb.{j}")
            for j in range(4):
                act.wait_ge(turned, turns[f"tr.{j}"])
                release(A(RTt[:, 2 * j:2 * j + 2, :], bank(f"tr.{j}")[:, :].rearrange("p (k t) -> p k t", k=2), ACT.Copy), f"tr.{j}")
            moved(act, *_n("out1", 2, 2))
            row_squares("h", X)
            row_roots("h")

            def head_squares(c, r, name, rows_, sq, i, squared, summed, pieces):
                full(act, pieces)
                A(rows_[:, r, c * 512:(c + 1) * 512], bank(name)[:, :], ACT.Copy)
                if i >= 2:
                    act.wait_ge(summed, i - 1)
                release(A(sq[:, i % 2, :], bank(name)[:, :], ACT.Square), name)

            i = 0
            for c in range(2):
                for r in range(RT):
                    head_squares(c, r, f"mk.{c}.{r}", MKR, MSQ, i, mk_squared, mk_summed, PB["mem_k"] + 2 * c + 2)
                    i += 1

            def silus(base, steps, silu_done, act_done):
                def one(it, u, first=False):
                    s = it * 2 + u
                    act.wait_ge(pieces_used, s * 3 + base)
                    if not first:
                        act.wait_ge(act_done, s - 1)
                    A(SILU[:, u % 2, :], banks[4 + 2 * (u % 2)][:, :], ACT.Silu).then_inc(silu_done, 1)
                act.wait_ge(pieces_used, base + 1)
                A(SILU[:, 0, :], banks[4][:, :], ACT.Silu).then_inc(silu_done, 1)
                one(0, 1, True)
                with act.Fori(1, steps // 2) as it:
                    for u in range(2):
                        one(it, u)
                for s in range(2 * (steps // 2), steps):
                    one(s // 2, s % 2)

            silus(PB["ffn"], FSTEPS, ffn_silu, ffn_act)
            act.wait_ge(mk_summed, 5)
            A(mkss, mkss, ACT.Sqrt).then_inc(mk_rooted, 1)
            act.wait_ge(ffn_added, 4)
            row_squares("fin", X)
            row_roots("fin")
            for c in range(2):
                full(act, PB["mem_v"] + 2 * c + 2)
                for r in range(RT):
                    release(A(MV[:, r, c * 512:(c + 1) * 512], bank(f"mv.{c}.{r}")[:, :], ACT.Copy), f"mv.{c}.{r}")
            act.wait_ge(normed["fin"], RT)
            row_squares("y", X)
            row_roots("y")
            act.wait_ge(small_full, 14 + 1)
            release(A(ALT, bank("al")[0:16, 0:T], ACT.Copy), "al")
            for r in range(RT):
                act.wait_ge(small_full, 14 + 2 + r)
                A(IKR[:, r, 0:64], bank(f"ik.{r}")[:, 0:64], ACT.Copy)
                A(iwr[:, r, :], bank(f"ik.{r}")[:, 64:72], ACT.Copy, scale=float(8 ** -0.5 * 64 ** -0.5))
                release(A(IKR[:, r, 64:128], bank(f"ik.{r}")[:, 0:64], ACT.Square, accum_out=ikss[:, r:r + 1]), f"ik.{r}")
            act.wait_ge(ik_summed, 1)
            A(ikss, ikss, ACT.Sqrt).then_inc(ik_rooted, 1)
            moved(act, "z.0", "z.1")
            chain(A(ZA, ZA, ACT.Abs))
            chain(A(ZA, ZA, ACT.Exp, scale=-1.0))
            A(ZA, ZA, ACT.Ln, bias=1.0).then_inc(la_ready, 1)
            for j in range(2):
                full(act, PB["iq"] + j + 1)
                release(A(IQT[:, 2 * j:2 * j + 2, :], bank(f"iq.{j}")[:, :].rearrange("p (k t) -> p k t", k=2), ACT.Copy), f"iq.{j}")
            act.wait_ge(cum_ready, 1)
            A(EC, CUM, ACT.Exp, scale=1.0 / 16).then_inc(e_ready, 1)
            A(EI, CUM, ACT.Exp, scale=-1.0 / 16).then_inc(e_ready, 1)
            for c in range(2):
                full(act, PB["gv"] + 2 * c + 2)
                for r in range(RT):
                    release(A(GV[:, r, c * 512:(c + 1) * 512], bank(f"gv.{c}.{r}")[:, :], ACT.Copy), f"gv.{c}.{r}")
            for i in range(8):
                r, j = i // 4, i % 4
                n = (P, T)[r]
                act.wait_ge(idx_full, i + 1)
                if i >= 2:
                    act.wait_ge(idx_used, i - 1)
                release(A(RL[:, i % 2, 0:2 * n], bank(f"sc{r}.{j}")[:, 0:2 * n], ACT.Relu), f"sc{r}.{j}")
            for h in range(GH):
                act.wait_ge(turned, turns[f"tke.{h}"])
                release(A(KE[:, h, :, :], bank(f"tke.{h}")[:, 0:T].rearrange("p (r d) -> p r d", r=RT), ACT.Copy), f"tke.{h}")
            for r in range(RT):
                full(act, PB["dkv"] + 2)
                A(DKV[:, r, :], bank(f"dkv.{r}")[:, :], ACT.Copy)
                release(A(DSQ[:, r, 0:256], bank(f"dkv.{r}")[:, 0:256], ACT.Square), f"dkv.{r}")
            i = 2
            for c in range(2):
                for r in range(RT):
                    full(act, PB["dq"] + 2 * c + 2)
                    A(DQR[:, r, c * 512:(c + 1) * 512], bank(f"dq.{c}.{r}")[:, :], ACT.Copy)
                    if i < 4:
                        act.wait_ge(dk_summed, i - 1)
                    else:
                        act.wait_ge(dq_summed, i - 3)
                    release(A(DSQ[:, i % 2, :], bank(f"dq.{c}.{r}")[:, :], ACT.Square), f"dq.{c}.{r}")
                    i += 1
            act.wait_ge(dk_summed, 3)
            A(dkss, dkss, ACT.Sqrt).then_inc(dk_rooted, 1)
            act.wait_ge(dq_summed, 5)
            A(dqss, dqss, ACT.Sqrt).then_inc(dq_rooted, 1)
            for h in range(GH):
                act.wait_ge(gla_full, 4 * h + 4)
                release(A(OG[:, :, h * T:(h + 1) * T], bank(f"og.{h}")[:, :].rearrange("p (r c) -> p r c", r=RT), ACT.Copy), f"og.{h}")
            act.wait_ge(og_summed, 1)
            A(ogss, ogss, ACT.Sqrt).then_inc(og_rooted, 1)
            for c in range(2):
                full(act, PB["gg"] + 2 * c + 2)
                for r in range(RT):
                    release(A(GG[:, r, c * 512:(c + 1) * 512], bank(f"gg.{c}.{r}")[:, :], ACT.Silu), f"gg.{c}.{r}")
            act.wait_ge(turned, turns["tdk"])
            release(A(DKT, bank("tdk")[:, :].rearrange("p (g t) -> p g t", g=DKVH), ACT.Copy, scale=W("dkn")[:, 0:1]), "tdk")
            for j in range(4):
                act.wait_ge(turned, turns[f"tdq.{j}"])
                release(A(DQT[:, 2 * j:2 * j + 2, :], bank(f"tdq.{j}")[:, :].rearrange("p (k t) -> p k t", k=2), ACT.Copy, scale=W("dqn")[:, 0:1]), f"tdq.{j}")
            i = 0
            for c in range(2):
                for r in range(RT):
                    full(act, PB["mq"] + 2 * c + 2)
                    if i == 0:
                        moved(act, "og.3")
                        act.wait_ge(gla_full, 4 * GH)
                    A(MQR[:, r, c * 512:(c + 1) * 512], bank(f"mq.{c}.{r}")[:, :], ACT.Copy)
                    if i < 2:
                        act.wait_ge(dq_summed, 4)
                    else:
                        act.wait_ge(mq_summed, i - 1)
                    release(A(DSQ[:, i % 2, :], bank(f"mq.{c}.{r}")[:, :], ACT.Square), f"mq.{c}.{r}")
                    i += 1
            act.wait_ge(mq_summed, 5)
            A(mqss, mqss, ACT.Sqrt).then_inc(mq_rooted, 1)
            for g in range(DKVH):
                for n in range(3):
                    act.wait_ge(dsa_max, 3 * g + n + 1)
                    for hh in range(4 if n == 0 else 2):
                        h = DGRP * g + (hh if n == 0 else 2 * (n - 1) + hh)
                        keys, r = (P, 0) if n == 0 else (T, 1)
                        last = A(DP[:, n, hh * keys:(hh + 1) * keys], DP[:, n, hh * keys:(hh + 1) * keys], ACT.Exp,
                                 bias=dmx[:, r, h:h + 1], accum_out=dsum[:, r, h:h + 1])
                    last.then_inc(dsa_exp, 1)
                for n in range(3):
                    act.wait_ge(dsa_full, 8 * g + 3 + n + 1)
                    dst = DPT0 if n == 0 else DPT1[:, n - 1, :]
                    release(A(dst, bank(f"dp.{g}.{n}")[:, :], ACT.Copy), f"dp.{g}.{n}")
                for r in range(RT):
                    act.wait_ge(dsa_full, 8 * g + 6 + r + 1)
                    release(A(ODT[:, DGRP * g:DGRP * (g + 1), r * P:(r + 1) * P], bank(f"do.{g}.{r}")[:, :].rearrange("p (h t) -> p h t", h=DGRP), ACT.Copy), f"do.{g}.{r}")
            for j in range(4):
                full(act, PB["gate0"] + j + 1)
                for c in range(2):
                    last = A(GS[:, 2 * j + c, :], bank(f"gt0.{j}")[:, c * T:(c + 1) * T], ACT.Sigmoid, bias=W("bgate")[:, 2 * j + c:2 * j + c + 1])
                release(last, f"gt0.{j}")
            for j in range(4):
                r = j // 2
                act.wait_ge(mem_max, j + 1)
                for hh in range(2):
                    h = 2 * (j % 2) + hh
                    last = A(MP[:, j, hh * T:(hh + 1) * T], bank(f"ml.{j}")[:, hh * T:(hh + 1) * T], ACT.Exp, bias=mmx[:, h, r:r + 1],
                             accum_out=msum[:, h, r:r + 1])
                release(last, f"ml.{j}")
            for h in range(MH):
                act.wait_ge(mem_full, 4 + h + 1)
                release(A(MPT[:, h, :, :], bank(f"mp.{h}")[:, :].rearrange("p (s t) -> p s t", s=2), ACT.Copy), f"mp.{h}")
            for h in range(MH):
                act.wait_ge(mem_full, 8 + h + 1)
                release(A(OMT[:, 2 * h:2 * h + 2, :], bank(f"mo.{h}")[:, :].rearrange("p (k t) -> p k t", k=2), ACT.Copy), f"mo.{h}")
            for i, gate in enumerate(("gate1", "gate2")):
                for j in range(4):
                    full(act, PB[gate] + j + 1)
                    if i:
                        moved(act, f"wo1.{j}")
                    for c in range(2):
                        col = 8 * (i + 1) + 2 * j + c
                        last = A(SG[:, j, c * T:(c + 1) * T], bank(f"gt{i + 1}.{j}")[:, c * T:(c + 1) * T], ACT.Sigmoid, bias=W("bgate")[:, col:col + 1])
                    release(last, f"gt{i + 1}.{j}")
            moved(act, *_n("out2", 2, 2))
            row_squares("z", X)
            row_roots("z")
            act.wait_ge(route_max, 1)
            A(gex, gsh, ACT.Exp).then_inc(route_exp, 1)
            act.wait_ge(route_max, 2)
            A(eex, el, ACT.Exp).then_inc(route_exp, 1)
            for j in range(0, 8):
                act.wait_ge(route_full, 2 + j)
                release(A(CB[:, 2 * j:2 * j + 2, :], bank(f"cb.{j}")[:, :].rearrange("p (e t) -> p e t", e=2), ACT.Copy), f"cb.{j}")
            silus(PB["moe"], EXPERTS, moe_silu, moe_act)

        @block.vector
        def _(dve):
            chain = Chain(dve, dve_chain)

            def row_norm(name, src, dst, n=RT, extra=None):
                s = stat[name][:, 0:n]
                dve.wait_ge(squares[name], n)
                V.tensor_scalar(s, s, 1.0 / D, EPS, mult, add).then_inc(meansq[name], 1)
                dve.wait_ge(rooted[name], 1)
                chain(V.reciprocal(s, s))
                for r in range(RT):
                    V.tensor_scalar(dst[:, r, :], src[:, r, :], s[:, r:r + 1], None, mult).then_inc(normed[name], 1)

            def turn_scaled(prefix, dst, w):
                for j in range(4):
                    dve.wait_ge(turned, turns[f"{prefix}.{j}"])
                    release(V.tensor_tensor(dst[:, 2 * j:2 * j + 2, :], bank(f"{prefix}.{j}")[:, :].rearrange("p (k t) -> p k t", k=2),
                                            bc(w[:, 2 * j:2 * j + 2], T), mult), f"{prefix}.{j}")

            V.memset(stat["x"][:, 2:3], 1.0).then_inc(stat_cleared, 1)
            dve.wait_ge(const_loaded, 32)
            row_norm("x", X, XN, 3)
            V.tensor_scalar(XM, XM, stat["x"][0:META, 2:3], None, mult).then_inc(normed["x"], 1)
            turn_scaled("tx", XT[:, :, META:], W("mixw"))
            dve.wait_ge(turned, turns["txm"])
            release(V.tensor_tensor(XT[:, :, 0:META], bank("txm")[:, 0:KT * META].rearrange("p (k t) -> p k t", k=KT), bc(W("mixw"), META), mult), "txm")
            dve.wait_ge(lam_exp, 1)
            l0, l1, l2, l3, l4 = lam[1], lam[2], lam[3], lam[4], lam[5]
            chain(V.tensor_scalar(l1, l0, 2.0, None, add))
            chain(V.reciprocal(l1, l1))
            chain(V.tensor_tensor(l1, l0, l1, mult))
            chain(V.tensor_tensor(l2, l1, l1, mult))
            chain(V.tensor_scalar(l3, l2, 1.0 / 17, 1.0 / 15, mult, add))
            for d in (13, 11, 9, 7, 5, 3, 1):
                chain(V.tensor_tensor(l3, l3, l2, mult))
                chain(V.tensor_scalar(l3, l3, 1.0 / d, None, add))
            chain(V.tensor_tensor(l3, l3, l1, mult))
            chain(V.tensor_scalar(l4, W("lam"), -1.0, 0.0, mult, amax))
            chain(V.scalar_tensor_tensor(l4, l3, 2.0, l4, mult, add))
            V.tensor_scalar(sp8, l4, 8.0, None, mult)
            V.tensor_scalar(nsp8, l4, -8.0, None, mult).then_inc(lam_ready, 1)

            inst = 0
            for what, tiles in (("k", [0, 1, "m"]), ("q", [0, 1])):
                for c in range(2):
                    full(dve, PB[what] + 2 * c + 2)
                    for r in tiles:
                        n = META if r == "m" else P
                        cs, sn = (C("cosm"), C("sinm")) if r == "m" else (C("cos")[:, r * P:(r + 1) * P], C("sin")[:, r * P:(r + 1) * P])
                        src = bank(f"{what}.{c}.{r}")[0:n, :].rearrange("p (h x) -> p h x", h=4)
                        if inst >= 2:
                            dve.wait_ge(rotated, inst - 1)
                        t1, t2 = (ROT[0:n, inst % 2, i, :].rearrange("p (h x) -> p h x", h=4) for i in range(2))
                        V.tensor_tensor(t1, src, bc1(cs[0:n, :], 4), mult)
                        V.tensor_tensor(t2[:, :, 0:64], src[:, :, 64:128], bc1(sn[0:n, 0:64], 4), mult)
                        release(V.tensor_tensor(t2[:, :, 64:128], src[:, :, 0:64], bc1(sn[0:n, 64:128], 4), mult), f"{what}.{c}.{r}")
                        inst += 1
            for p in range(4):
                for h in (2 * p, 2 * p + 1):
                    dve.wait_ge(scored, 3 * p + h % 2 + 1)
                    if p >= 2:
                        dve.wait_ge(retained, p - 1)
                    b, s = bank(f"s.{h}"), ST[:, h % 4, :]
                    V.tensor_scalar(s[:, P:2 * P], b[:, P:2 * P], C("gprev")[:, h:h + 1], None, mult)
                    V.scalar_tensor_tensor(s[:, 0:P], b[:, 0:P], C("gown")[:, h:h + 1], C("tri"), mult, mult)
                    release(V.scalar_tensor_tensor(s[:, 2 * P:3 * P], b[:, 2 * P:3 * P], C("gown")[:, h:h + 1], C("tri"), mult, mult), f"s.{h}")
                if p:
                    dve.wait_ge(o_squared, p)
                    V.tensor_reduce(oss[:, :, 2 * p - 2:2 * p], SQ[:, (p - 1) % 2, :].rearrange("p (r h c) -> p r h c", r=RT, h=2), AX.X, add).then_inc(o_reduced, 1)
                moved(dve, f"li.{2 * p}", f"li.{2 * p + 1}")
                for k in (2 * p, 2 * p + 1):
                    w = W("convw").rearrange("p (j k) -> p j k", j=CONV)
                    chain(V.tensor_scalar(CV[:, k, :], LI[:, k, 0:TM], w[:, 0, k:k + 1], W("convb")[:, k:k + 1], mult, add))
                    for j in range(1, CONV):
                        ins = V.scalar_tensor_tensor(CV[:, k, :], LI[:, k, j:j + TM], w[:, j, k:k + 1], CV[:, k, :], mult, add)
                        if j < CONV - 1:
                            chain(ins)
                        else:
                            ins.then_inc(convolved, 1)
            dve.wait_ge(o_squared, 4)
            V.tensor_reduce(oss[:, :, 6:8], SQ[:, 1, :].rearrange("p (r h c) -> p r h c", r=RT, h=2), AX.X, add).then_inc(o_reduced, 1)
            dve.wait_ge(o_reduced, 4)
            V.tensor_scalar(oss, oss, 1.0 / P, EPS, mult, add).then_inc(o_summed, 1)
            dve.wait_ge(o_rooted, 1)
            chain(V.reciprocal(oss, oss))
            hv = lambda a, n: a.rearrange("p r (h c) -> p r h c", h=n)
            for r in range(RT):
                chain(V.tensor_tensor(hv(O, HR)[:, r], hv(O, HR)[:, r], bc(oss[:, r, :], P), mult))
            moved(dve, *_n("g", 2, 2))
            V.tensor_tensor(O, O, GR, mult).then_inc(o_ready, 1)
            dve.wait_ge(decay_ready, 1)
            V.scalar_tensor_tensor(TH, A2, 1.0, TH, add, mult).then_inc(lru_m2, 1)
            moved(dve, "lg.7.1")
            V.tensor_tensor(IG, IG, CV, mult).then_inc(lru_gated, 1)
            dve.wait_ge(lru_gated, 1)
            dve.wait_ge(lru_m, 1)
            chain(V.tensor_tensor(IG, IG, TH, mult))
            for k in range(KT):
                last = V.tensor_tensor_scan(HS[:, k, :], AA[:, k, :], IG[:, k, :], 0.0, mult, add)
            chain(last)
            moved(dve, *_n("lgate", 4))
            V.tensor_tensor(LT, LT, HS[:, :, META:], mult).then_inc(lru_ready, 1)
            row_norm("mem", MR, MR)
            turn_scaled("tm", MT, W("gmem"))
            for j in range(4):
                full(dve, PB["br_ret"] + j + 1)
                moved(dve, f"ga.{j}")
                release(V.tensor_tensor(MIX[:, 2 * j:2 * j + 2, :], GA[:, 2 * j:2 * j + 2, :], bank(f"br.{j}")[:, :].rearrange("p (k t) -> p k t", k=2), mult), f"br.{j}")
            for j in range(4):
                full(dve, PB["br_lru"] + j + 1)
                moved(dve, f"gb.{j}")
                if j >= 2:
                    dve.wait_ge(mixed, j - 1)
                release(V.tensor_tensor(PART[:, j % 2, :].rearrange("p (k t) -> p k t", k=2), GB[:, 2 * j:2 * j + 2, :],
                                        bank(f"bl.{j}")[:, :].rearrange("p (k t) -> p k t", k=2), mult), f"bl.{j}")
            for c in range(2):
                full(dve, PB["out1"] + 2 * c + 2)
                for r in range(RT):
                    xs = X[:, r, c * 512:(c + 1) * 512]
                    release(V.tensor_tensor(xs, xs, bank(f"out1.{c}.{r}")[:, :], add), f"out1.{c}.{r}")
            row_norm("h", X, XN)
            turn_scaled("th", HT, W("ffnw"))

            def head_sums(names, sq, ss, heads, summed, per=512):
                for i, (name, c, r) in enumerate(names):
                    moved(dve, name)
                    nh = heads
                    V.tensor_reduce(ss[:, r, c * nh:(c + 1) * nh], sq[:, i % 2, 0:per].rearrange("p (h c) -> p h c", h=nh), AX.X, add).then_inc(summed, 1)

            def head_scale(src, ss, dim, summed, count, rooted_, ready, n):
                dve.wait_ge(rooted_, 1)
                chain(V.reciprocal(ss, ss))
                for r in range(RT):
                    last = V.tensor_tensor(hv(src, n)[:, r], hv(src, n)[:, r], bc(ss[:, r, :], dim), mult)
                last.then_inc(ready, 1)

            def head_mean(ss, dim, summed, count):
                dve.wait_ge(summed, count)
                V.tensor_scalar(ss, ss, 1.0 / dim, EPS, mult, add).then_inc(summed, 1)

            head_sums([(f"mk.{c}.{r}", c, r) for c in range(2) for r in range(RT)], MSQ, mkss, 2, mk_summed)
            head_mean(mkss, 256, mk_summed, 4)

            def acts(base, steps, silu_done, act_done, scaled=None):
                def one(it, u):
                    s = it * 2 + u
                    src = SILU
                    dve.wait_ge(silu_done, s + 1)
                    if scaled is not None:
                        V.tensor_tensor(SILC[:, u % 2, :].rearrange("p (f t) -> p f t", f=2), SILU[:, u % 2, :].rearrange("p (f t) -> p f t", f=2),
                                        CB[:, bass.ds(s, 1), :].to_broadcast([P, 2, T]), mult).then_inc(scaled, 1)
                        dve.wait_ge(scaled, s + 1)
                        src = SILC
                    dve.wait_ge(pieces_used, s * 3 + (base + 1))
                    V.tensor_tensor(HID[:, u % 2, :, :].rearrange("p f t -> p (f t)"), src[:, u % 2, :], banks[5 + 2 * (u % 2)][:, :], mult).then_inc(act_done, 1)
                def first():
                    dve.wait_ge(silu_done, 1)
                    src = SILU
                    if scaled is not None:
                        V.tensor_tensor(SILC[:, 0, :].rearrange("p (f t) -> p f t", f=2), SILU[:, 0, :].rearrange("p (f t) -> p f t", f=2),
                                        CB[:, 0:1, :].to_broadcast([P, 2, T]), mult).then_inc(scaled, 1)
                        dve.wait_ge(scaled, 1)
                        src = SILC
                    dve.wait_ge(pieces_used, base + 2)
                    V.tensor_tensor(HID[:, 0, :, :].rearrange("p f t -> p (f t)"), src[:, 0, :], banks[5][:, :], mult).then_inc(act_done, 1)
                first()
                one(0, 1)
                with dve.Fori(1, steps // 2) as it:
                    for u in range(2):
                        one(it, u)
                for s in range(2 * (steps // 2), steps):
                    one(s // 2, s % 2)

            acts(PB["ffn"], FSTEPS, ffn_silu, ffn_act)
            dve.wait_ge(pieces_used, PB["ffn"] + 3 * FSTEPS)
            for r in range(RT):
                for c in range(2):
                    xs = X[:, r, c * 512:(c + 1) * 512]
                    V.tensor_tensor(xs, xs, banks[2 * r + c][:, :], add).then_inc(ffn_added, 1)
            s = stat["fin"][:, 0:RT]
            dve.wait_ge(squares["fin"], RT)
            V.tensor_scalar(s, s, 1.0 / D, EPS, mult, add).then_inc(meansq["fin"], 1)
            dve.wait_ge(rooted["fin"], 1)
            chain(V.reciprocal(s, s))
            dve.wait_ge(final_w_loaded, 16)
            for r in range(RT):
                V.scalar_tensor_tensor(X[:, r, :], X[:, r, :], s[:, r:r + 1], FW, mult, mult).then_inc(normed["fin"], 1)
            head_scale(MKR, mkss, 256, mk_summed, 4, mk_rooted, mk_ready, MH)
            for j in range(4):
                dve.wait_ge(turned, turns[f"tmk.{j}"])
                release(V.tensor_tensor(MKT[:, 2 * j:2 * j + 2, :], bank(f"tmk.{j}")[:, :].rearrange("p (k t) -> p k t", k=2), bc(W("mkn"), T), mult), f"tmk.{j}")
            row_norm("y", X, XN)
            turn_scaled("t2", HT, W("gmix"))
            moved(dve, "ik.0", "ik.1")
            V.tensor_scalar(ikss, ikss, 1.0 / 64, EPS, mult, add).then_inc(ik_summed, 1)
            dve.wait_ge(ik_rooted, 1)
            chain(V.reciprocal(ikss, ikss))
            for r in range(RT):
                V.tensor_scalar(IKR[:, r, 64:128], IKR[:, r, 0:64], ikss[:, r:r + 1], None, mult).then_inc(ik_squared, 1)
                dve.wait_ge(ik_squared, r + 1)
                last = V.tensor_scalar(IKR[:, r, 0:64], IKR[:, r, 0:64], ikss[:, r:r + 1], None, mult)
            last.then_inc(ik_ready, 1)
            for j in range(2):
                dve.wait_ge(small_full, 14 + 4 + j)
                for hh in range(2):
                    h = 2 * j + hh
                    b = bank(f"z.{j}")[:, hh * T:(hh + 1) * T]
                    V.tensor_scalar(ZA[:, h * T:(h + 1) * T], b, W("ba2")[:, h:h + 1], None, add)
                    last = V.tensor_scalar(ZB[:, h * T:(h + 1) * T], b, W("ba2")[:, h:h + 1], 0.0, add, amin)
                release(last, f"z.{j}")
            dve.wait_ge(la_ready, 1)
            chain(V.tensor_tensor(ZB, ZB, ZA, sub))
            dve.wait_ge(padded, 2)
            V.tensor_tensor_scan(CUM, RM, ZB, 0.0, mult, add).then_inc(cum_ready, 1)
            for j in range(2):
                hs = slice(2 * j, 2 * j + 2)
                full(dve, PB["gq"] + j + 1)
                dve.wait_ge(e_ready, 1)
                release(V.scalar_tensor_tensor(QD[:, hs, :].rearrange("p h t -> p (h t)"), bank(f"gq.{j}")[:, :], float(P) ** -0.5, EC[:, j * 512:(j + 1) * 512], mult, mult), f"gq.{j}")
            for j in range(2):
                hs = slice(2 * j, 2 * j + 2)
                full(dve, PB["gk"] + j + 1)
                dve.wait_ge(e_ready, 2)
                release(V.tensor_tensor(KI[:, hs, :].rearrange("p h t -> p (h t)"), bank(f"gk.{j}")[:, :], EI[:, j * 512:(j + 1) * 512], mult), f"gk.{j}")
            chain(V.tensor_copy(dec, EC.rearrange("p (h n c) -> p h n c", h=GH, n=4)[:, :, :, GCH - 1]))
            moved(dve, "gk.0", "gk.1")
            V.tensor_tensor(KET.rearrange("p h (n c) -> p h n c", n=4), KI.rearrange("p h (n c) -> p h n c", n=4), bc(dec, GCH), mult).then_inc(gla_ke, 1)
            dve.wait_ge(turned, turns["tik"])
            release(V.tensor_scalar(IKT, bank("tik")[:, 0:T], W("ikn")[:, 0:1], None, mult), "tik")
            for i in range(8):
                r, j = i // 4, i % 4
                n = (P, T)[r]
                moved(dve, f"sc{r}.{j}")
                for hh in range(2):
                    head = 4 * (j // 2) + 2 * hh + j % 2
                    src, w = RL[:, i % 2, hh * n:(hh + 1) * n], iwr[:, r, head:head + 1]
                    if j == 0 and hh == 0:
                        chain(V.tensor_scalar(SC[r], src, w, None, mult))
                    else:
                        ins = V.scalar_tensor_tensor(SC[r], src, w, SC[r], mult, add)
                        if hh == 0:
                            chain(ins)
                        else:
                            ins.then_inc(idx_used, 1)
                            dve.wait_ge(idx_used, i + 1)
            HID_, LOW, MARK = 3.0e38, -3.0e38, -3.3e38
            triq = C("triq")
            for r in range(RT):
                n = (P, T)[r]
                w, own = WK[r], slice(n - P, n)
                chain(V.tensor_scalar(MB[r][:, own], triq, HID_, -HID_, mult, add))
                if r:
                    V.tensor_copy(w[:, 0:P], SC[r][:, 0:P])
                chain(V.tensor_tensor(w[:, own], SC[r][:, own], triq, mult))
                chain(V.tensor_tensor(w[:, own], w[:, own], MB[r][:, own], add))
                for _ in range(TOPK // 8):
                    chain(V.max(top8[:, r, :], w))
                    chain(V.match_replace(w, top8[:, r, :], w, -3.4e38))
                chain(V.tensor_scalar(MB[r], w, MARK, None, ALU.is_lt))
                chain(V.tensor_tensor(MB[r][:, own], MB[r][:, own], triq, mult))
                V.tensor_scalar(MB[r], MB[r], 1.0e30, -1.0e30, mult, add).then_inc(topped, 1)
            head_sums([("dkv.0", 0, 0), ("dkv.1", 0, 1)], DSQ, dkss, 2, dk_summed, per=256)
            head_sums([(f"dq.{c}.{r}", c, r) for c in range(2) for r in range(RT)], DSQ, dqss, 4, dq_summed)
            head_mean(dkss, P, dk_summed, 2)
            head_mean(dqss, P, dq_summed, 4)
            dve.wait_ge(padded, 3)
            blk = C("blk").bitcast(i32)
            for h in range(GH):
                a = h % 2
                dve.wait_ge(gla_full, 4 * h + 1)
                if h >= 2:
                    dve.wait_ge(gla_full, 4 * (h - 1))
                for rr in range(RT):
                    last = V.copy_predicated(ATM[:, a, rr * P:(rr + 1) * P], blk, bank(f"at.{h}")[:, rr * P:(rr + 1) * P])
                release(last, f"at.{h}")
                dve.wait_ge(gla_full, 4 * h + 2)
                s8, up = ST8[:, a], bank(f"up.{h}.0")
                chain(V.tensor_copy(s8[:, 0, :], up[:, 0:T]))
                dve.wait_ge(gla_full, 4 * h + 3)
                release(V.scalar_tensor_tensor(s8[:, 1, :], s8[:, 0, :], dec[:, h, 1:2], bank(f"up.{h}.1")[:, 0:T], mult, add), f"up.{h}.1")
                moved(dve, f"up.{h}.1")
                release(V.scalar_tensor_tensor(s8[:, 2, :], s8[:, 1, :], dec[:, h, 2:3], up[:, T:2 * T], mult, add), f"up.{h}.0")
            dve.wait_ge(dk_rooted, 1)
            chain(V.reciprocal(dkss, dkss))
            for r in range(RT):
                last = V.tensor_tensor(DKV[:, r, 0:256].rearrange("p (g c) -> p g c", g=2), DKV[:, r, 0:256].rearrange("p (g c) -> p g c", g=2), bc(dkss[:, r, :], P), mult)
            last.then_inc(dk_ready, 1)
            dve.wait_ge(dq_rooted, 1)
            chain(V.reciprocal(dqss, dqss))
            chain(V.tensor_scalar(dqss, dqss, float(P) ** -0.5, None, mult))
            for r in range(RT):
                last = V.tensor_tensor(hv(DQR, DH)[:, r], hv(DQR, DH)[:, r], bc(dqss[:, r, :], P), mult)
            last.then_inc(dq_ready, 1)
            for r in range(RT):
                dve.wait_ge(og_squared, r + 1)
                V.tensor_reduce(ogss[:, r, :], GSQ[:, :].rearrange("p (h c) -> p h c", h=GH), AX.X, add).then_inc(og_reduced, 1)
            dve.wait_ge(og_reduced, 2)
            V.tensor_scalar(ogss, ogss, 1.0 / 256, EPS, mult, add).then_inc(og_summed, 1)
            dve.wait_ge(og_rooted, 1)
            chain(V.reciprocal(ogss, ogss))
            for r in range(RT):
                chain(V.tensor_tensor(hv(OG, GH)[:, r], hv(OG, GH)[:, r], bc(ogss[:, r, :], T), mult))
            moved(dve, *_n("gg", 2, 2))
            V.tensor_tensor(OG, OG, GG, mult).then_inc(og_ready, 1)
            head_sums([(f"mq.{c}.{r}", c, r) for c in range(2) for r in range(RT)], DSQ, mqss, 2, mq_summed)
            head_mean(mqss, 256, mq_summed, 4)
            dve.wait_ge(mq_rooted, 1)
            chain(V.reciprocal(mqss, mqss))
            chain(V.tensor_scalar(mqss, mqss, 1.0 / 16, None, mult))
            for r in range(RT):
                last = V.tensor_tensor(hv(MQR, MH)[:, r], hv(MQR, MH)[:, r], bc(mqss[:, r, :], T), mult)
            last.then_inc(mq_ready, 1)
            for g in range(DKVH):
                for n in range(3):
                    heads, keys, r = (4, P, 0) if n == 0 else (2, T, 1)
                    h0 = DGRP * g + (0 if n == 0 else 2 * (n - 1))
                    dve.wait_ge(dsa_full, 8 * g + n + 1)
                    if g:
                        dve.wait_ge(dsa_full, 6)
                    view = DP[:, n, :].rearrange("p (h s) -> p h s", h=heads)
                    release(V.tensor_tensor(view, bank(f"dl.{g}.{n}")[:, :].rearrange("p (h s) -> p h s", h=heads), bc1(MB[r], heads), add), f"dl.{g}.{n}")
                    moved(dve, f"dl.{g}.{n}")
                    V.tensor_reduce(dmx[:, r, h0:h0 + heads], view, AX.X, amax, negate=True).then_inc(dsa_max, 1)
                for n in range(3):
                    heads, keys, r = (4, P, 0) if n == 0 else (2, T, 1)
                    h0 = DGRP * g + (0 if n == 0 else 2 * (n - 1))
                    view = DP[:, n, :].rearrange("p (h s) -> p h s", h=heads)
                    dve.wait_ge(dsa_exp, 3 * g + n + 1)
                    ds_ = dsum[:, r, h0:h0 + heads]
                    chain(V.reciprocal(ds_, ds_))
                    V.tensor_tensor(view, view, bc(ds_, keys), mult).then_inc(dsa_p, 1)
            for j in range(4):
                dve.wait_ge(turned, turns[f"tog.{j}"])
                release(V.tensor_tensor(OGT[:, 2 * j:2 * j + 2, :], bank(f"tog.{j}")[:, :].rearrange("p (k t) -> p k t", k=2), bc(W("glan"), T), mult), f"tog.{j}")
            for j in range(4):
                dve.wait_ge(turned, turns[f"tmq.{j}"])
                release(V.tensor_tensor(MQT[:, 2 * j:2 * j + 2, :], bank(f"tmq.{j}")[:, :].rearrange("p (k t) -> p k t", k=2), bc(W("mqn"), T), mult), f"tmq.{j}")
            for j in range(4):
                dve.wait_ge(mem_full, j + 1)
                V.tensor_reduce(mmx[:, 2 * (j % 2):2 * (j % 2) + 2, j // 2], bank(f"ml.{j}")[:, :].rearrange("p (h s) -> p h s", h=2), AX.X, amax, negate=True).then_inc(mem_max, 1)
            for j in range(4):
                moved(dve, f"ml.{j}")
                ms_ = msum[:, 2 * (j % 2):2 * (j % 2) + 2, j // 2]
                chain(V.reciprocal(ms_, ms_))
                V.tensor_tensor(MP[:, j, :].rearrange("p (h s) -> p h s", h=2), MP[:, j, :].rearrange("p (h s) -> p h s", h=2), bc(ms_, T), mult).then_inc(mem_p, 1)
            for j in range(4):
                full(dve, PB["o_gla"] + j + 1)
                moved(dve, f"gt0.{j}")
                release(V.tensor_tensor(MRG[:, 2 * j:2 * j + 2, :], GS[:, 2 * j:2 * j + 2, :], bank(f"wo0.{j}")[:, :].rearrange("p (k t) -> p k t", k=2), mult), f"wo0.{j}")
            for i, proj in enumerate(("o_dsa", "o_mem")):
                for j in range(4):
                    full(dve, PB[proj] + j + 1)
                    moved(dve, f"gt{i + 1}.{j}")
                    if 4 * i + j >= 2:
                        dve.wait_ge(merged, 4 * i + j - 1)
                    release(V.tensor_tensor(MPART[:, j % 2, :], SG[:, j, :], bank(f"wo{i + 1}.{j}")[:, :], mult), f"wo{i + 1}.{j}")
            for c in range(2):
                full(dve, PB["out2"] + 2 * c + 2)
                for r in range(RT):
                    xs = X[:, r, c * 512:(c + 1) * 512]
                    release(V.tensor_tensor(xs, xs, bank(f"out2.{c}.{r}")[:, :], add), f"out2.{c}.{r}")
            row_norm("z", X, XN)
            turn_scaled("t3", HT, W("gffn"))
            dve.wait_ge(route_full, 1)
            release(V.tensor_tensor(lr, bank("rl")[:, 0:40].rearrange("p (r c) -> p r c", r=RT), bc1(W("brt"), RT), add), "rl")
            moved(dve, "rl")
            gl = lr[:, :, 0:4]
            chain(V.tensor_reduce(gmx, gl, AX.X, amax))
            V.tensor_tensor(gsh, gl, bc(gmx, 4), sub).then_inc(route_max, 1)

            def first_of(dst, values, peak):
                rk = bc1(C("rank"), RT)
                chain(V.tensor_tensor(dst, values, bc(peak, 4), ALU.is_equal))
                chain(V.tensor_tensor(dst, dst, rk, mult))
                chain(V.tensor_reduce(emx, dst, AX.X, amax))
                chain(V.tensor_tensor(dst, rk, bc(emx, 4), ALU.is_equal))

            first_of(oh, gl, gmx)
            chain(V.tensor_tensor(tmp16, lr[:, :, 4:20].rearrange("p r (g j) -> p r g j", g=4), bc(oh, 4), mult))
            chain(V.tensor_reduce(el, tmp16.rearrange("p r g j -> p r j g"), AX.X, add))
            chain(V.tensor_reduce(gmx, el, AX.X, amax))
            V.tensor_tensor(el, el, bc(gmx, 4), sub).then_inc(route_max, 1)
            dve.wait_ge(route_max, 2)
            chain(V.tensor_reduce(gmx, el, AX.X, amax))
            first_of(oh1, el, gmx)
            chain(V.scalar_tensor_tensor(tmp4, oh1, -3.0e38, el, mult, add))
            chain(V.tensor_reduce(gmx, tmp4, AX.X, amax))
            first_of(oh2, tmp4, gmx)
            chain(V.tensor_tensor(oh1, oh1, oh2, add))
            dve.wait_ge(route_exp, 1)
            chain(V.tensor_reduce(gsm, gex, AX.X, add))
            dve.wait_ge(route_exp, 2)
            chain(V.tensor_tensor(oh1, oh1, eex, mult))
            chain(V.tensor_reduce(gmx, oh1, AX.X, add))
            chain(V.tensor_tensor(gmx, gmx, gsm, mult))
            chain(V.reciprocal(gmx, gmx))
            chain(V.tensor_tensor(oh1, oh1, bc(gmx, 4), mult))
            chain(V.tensor_copy(tmp16, bc(oh, 4)))
            V.tensor_tensor(cmb.rearrange("p r (g j) -> p r g j", g=4), tmp16, oh1.unsqueeze(2).to_broadcast([P, RT, 4, 4]), mult).then_inc(combined, 1)
            dve.wait_ge(turned, turns["tc"])
            release(V.tensor_copy(CT, bank("tc")[0:16, 0:T]), "tc")
            moved(dve, *_n("cb", 8))
            acts(PB["moe"], EXPERTS, moe_silu, moe_act, moe_scaled)
            dve.wait_ge(pieces_used, NP)
            for r in range(RT):
                for c in range(2):
                    xs = X[:, r, c * 512:(c + 1) * 512]
                    V.tensor_tensor(xs, xs, banks[2 * r + c][:, :], add).then_inc(moe_added, 1)

        @block.gpsimd
        def _(pool):
            G.memset(LI[:, :, 0:CONV - 1], 0.0).then_inc(padded, 1)
            names = [f"{w}.{c}.{r}" for w, t in (("k", [0, 1, "m"]), ("q", [0, 1])) for c in range(2) for r in t]
            for i, name in enumerate(names):
                what, c, r = name.split(".")
                c = int(c)
                moved(pool, name)
                if r == "m":
                    dst, n = KM[:, c * 512:(c + 1) * 512], META
                else:
                    dst, n = (KR if what == "k" else QR)[:, int(r), c * 512:(c + 1) * 512], P
                G.tensor_tensor(dst, ROT[0:n, i % 2, 0, :], ROT[0:n, i % 2, 1, :], add).then_inc(rotated, 1)
            for p in range(4):
                moved(pool, f"o.{p}")
                if p >= 2:
                    pool.wait_ge(o_reduced, p - 1)
                o = O[:, :, 2 * p * P:(2 * p + 2) * P]
                G.tensor_tensor(SQ[:, p % 2, :].rearrange("p (r c) -> p r c", r=RT), o, o, mult).then_inc(o_squared, 1)
            for j in range(4):
                moved(pool, f"br.{j}", f"bl.{j}")
                m = MIX[:, 2 * j:2 * j + 2, :]
                G.tensor_tensor(m, m, PART[:, j % 2, :].rearrange("p (k t) -> p k t", k=2), add).then_inc(mixed, 1)
            pool.wait_ge(lru_ready, 1)
            pool.dma_start(FW, final_w.partition_broadcast(P)).then_inc(final_w_loaded, 16)
            pool.wait_ge(lru_ready, 1)
            G.memset(RM, 1.0).then_inc(pool_chain, 1)
            pool.wait_ge(pool_chain, 1)
            G.memset(RM.rearrange("p (n c) -> p n c", c=GCH)[:, :, 0:1], 0.0).then_inc(padded, 1)
            pool.wait_ge(o_ready, 1)
            G.memset(ATM, 0.0).then_inc(padded, 1)
            for r in range(RT):
                moved(pool, *_n("og", GH))
                if r:
                    pool.wait_ge(og_reduced, 1)
                G.tensor_tensor(GSQ, OG[:, r, :], OG[:, r, :], mult).then_inc(og_squared, 1)
            for i in range(2):
                for j in range(4):
                    moved(pool, f"wo0.{j}")
                    moved(pool, f"wo{i + 1}.{j}")
                    if i:
                        pool.wait_ge(merged, j + 1)
                    m = MRG[:, 2 * j:2 * j + 2, :]
                    G.tensor_tensor(m, m, MPART[:, j % 2, :].rearrange("p (k t) -> p k t", k=2), add).then_inc(merged, 1)


def rows_pieces(w):
    n = w.shape[1] // 512
    return w.reshape(2, 4, P, n, 512).transpose(3, 0, 2, 1, 4).reshape(2 * n, P, PW)


def cols_pieces(w):
    n = w.shape[1] // 256
    return w.reshape(KT, P, n, 256).transpose(2, 1, 0, 3).reshape(n, P, PW)


def down_pieces(w):
    n = w.shape[0] // 256
    return w.reshape(n, 2, P, D).transpose(0, 2, 1, 3).reshape(n, P, PW)


def hidden_pieces(gate, up, down):
    n = len(gate)
    out = [gate[0], up[0]]
    for s in range(n):
        if s + 1 < n:
            out += [gate[s + 1], up[s + 1]]
        out.append(down[s])
    return np.stack(out)


def per_partition(v):
    return v.reshape(-1, P).T


def kernel(**a):
    import concourse.bacc as bacc
    from concourse import mybir
    from concourse.bass_utils import run_bass_kernel_spmd

    a = {k: np.asarray(v) for k, v in a.items()}
    w1, w2, ff = a["w_in"][0], a["w_in_2"][0], a["w_ffn_in"][0]
    at = dict(gq=0, gk=512, gv=1024, gg=2048, ga=3072, dq=3088, dk=4112, dv=4368, iq=4624, ik=5136, iw=5200, mq=5208, gate=6232)
    lru = lambda w: w.reshape(LRUB, 2, P, 256).transpose(2, 0, 1, 3).reshape(1, P, PW)
    kv = a["w_mem_kv_2"][0]
    moe = lambda w: w.reshape(EXPERTS, KT, P, 256).transpose(0, 2, 1, 3).reshape(EXPERTS, P, PW)
    parts = {
        "k": rows_pieces(w1[:, 1024:2048]), "q": rows_pieces(w1[:, 0:1024]), "v": rows_pieces(w1[:, 2048:3072]),
        "lru_in": cols_pieces(w1[:, 4096:5120]), "g_ret": rows_pieces(w1[:, 3072:4096]),
        "lru_gates": np.concatenate([lru(a["lru_wa"][0]), lru(a["lru_wx"][0])]),
        "lru_gate": cols_pieces(w1[:, 5120:6144]), "gate_a": cols_pieces(w1[:, 6144:7168]), "gate_b": cols_pieces(w1[:, 7168:8192]),
        "br_ret": cols_pieces(a["w_branch_ret"][0]), "br_lru": cols_pieces(a["w_branch_lru"][0]), "out1": rows_pieces(a["w_out"][0]),
        "mem_k": rows_pieces(kv[:, 0:1024]), "mem_v": rows_pieces(kv[:, 1024:2048]),
        "ffn": hidden_pieces(cols_pieces(ff[:, 0:FFN]), cols_pieces(ff[:, FFN:]), down_pieces(a["w_ffn_out"][0])),
        "iq": cols_pieces(w2[:, at["iq"]:at["iq"] + 512]), "gq": cols_pieces(w2[:, 0:512]), "gk": cols_pieces(w2[:, 512:1024]),
        "gv": rows_pieces(w2[:, 1024:2048]), "gg": rows_pieces(w2[:, 2048:3072]), "dkv": rows_pieces(w2[:, at["dk"]:at["dk"] + 512]),
        "dq": rows_pieces(w2[:, at["dq"]:at["dq"] + 1024]), "mq": rows_pieces(w2[:, at["mq"]:at["mq"] + 1024]),
        "gate0": cols_pieces(w2[:, at["gate"]:at["gate"] + 1024]), "gate1": cols_pieces(w2[:, at["gate"] + 1024:at["gate"] + 2048]),
        "gate2": cols_pieces(w2[:, at["gate"] + 2048:at["gate"] + 3072]),
        "o_gla": cols_pieces(a["w_o_gla_2"][0]), "o_dsa": cols_pieces(a["w_o_dsa_2"][0]), "o_mem": cols_pieces(a["w_o_mem_2"][0]),
        "out2": rows_pieces(a["w_out_2"][0]),
        "moe": hidden_pieces(moe(a["w_gate_2"][0]), moe(a["w_up_2"][0]), down_pieces(a["w_down_2"][0].reshape(EXPERTS * 256, D))),
    }
    weights = np.concatenate([parts[n] for n, _ in PIECES])
    sw = np.concatenate([w2[:, at["ga"]:at["ga"] + 16], w2[:, at["ik"]:at["ik"] + 72], a["w_r1_2"][0], a["w_r2_2"][0]], 1)
    cols = {
        "mixw": per_partition(a["mix_norm_w"][0]), "ffnw": per_partition(a["ffn_norm_w"][0]), "gmix": per_partition(a["g_mix_2"][0]),
        "gmem": per_partition(a["g_mem_2"][0]), "gffn": per_partition(a["g_ffn_2"][0]), "convw": per_partition(a["conv_w"][0].reshape(-1)),
        "convb": per_partition(a["conv_b"][0]), "ba": per_partition(a["lru_ba"][0]), "bx": per_partition(a["lru_bx"][0]),
        "lam": per_partition(a["lru_lambda"][0]), "ba2": per_partition(a["b_gla_a2_2"][0]), "glan": per_partition(a["gla_norm_2"][0]),
        "dqn": per_partition(a["dsa_q_norm_2"][0]), "dkn": per_partition(a["dsa_k_norm_2"][0]),
        "ikn": per_partition(np.concatenate([a["idx_k_norm_2"][0]] * 2)), "mqn": per_partition(a["mem_q_norm_2"][0]),
        "mkn": per_partition(a["mem_k_norm_2"][0]), "bgate": per_partition(a["b_gate_2"][0]),
        "brt": np.broadcast_to(np.concatenate([a["b_r1_2"][0], a["b_r2_2"][0]]), (P, 20)),
        "smallw": sw.reshape(KT, P, 108).transpose(1, 0, 2).reshape(P, KT * 108),
        "wa2": np.concatenate([a["w_gla_a2_2"][0]] * 8),
    }
    arrays = {
        "weights": weights, "x": a["x"][0], "meta": a["meta_tokens"], "mem": a["mem_2"][0], "consts": shape_constants(),
        "params": np.concatenate([cols[n] for n, _ in PARAMS], 1), "final_w": a["final_norm_w"],
    }
    arrays = {k: np.ascontiguousarray(v) for k, v in arrays.items()}
    nc = bacc.Bacc("TRN2", target_bir_lowering=False, num_devices=1)
    f32 = mybir.dt.float32
    aps = {k: nc.dram_tensor(k + "_dram", v.shape, f32, kind="ExternalInput").ap() for k, v in arrays.items()}
    out = nc.dram_tensor("out_dram", (T, D), f32, kind="ExternalOutput").ap()
    program(nc, out=out, **aps)
    r = run_bass_kernel_spmd(nc, [{k + "_dram": v for k, v in arrays.items()}], core_ids=[0])
    return r.results[0]["out_dram"].reshape(1, T, D)
```

```python
from contextlib import ExitStack

import numpy as np

P = 128
T = 256
RT = T // P
D = 1024
KT = D // P
META = 16
TM = META + T
HR = 8
CONV = 4
LRUB = 4
FFN = 2816
FSTEPS = FFN // 256
EXPERTS = 16
GH, GCH = 4, 64
DH, DKVH, DGRP = 8, 2, 4
TOPK = 64
MH = 4
EPS = 1e-6
SLOTS = 3
PW = 2048

PIECES = [("k", 4), ("q", 4), ("v", 4), ("lru_in", 4), ("g_ret", 4), ("lru_gates", 2), ("lru_gate", 4),
          ("gate_a", 4), ("gate_b", 4), ("br_ret", 4), ("br_lru", 4), ("out1", 4), ("mem_k", 4),
          ("ffn", 3 * FSTEPS), ("mem_v", 4), ("iq", 2), ("gq", 2), ("gk", 2), ("gv", 4), ("dkv", 2), ("dq", 4),
          ("gg", 4), ("mq", 4), ("gate0", 4), ("o_gla", 4), ("gate1", 4), ("o_dsa", 4), ("gate2", 4),
          ("o_mem", 4), ("out2", 4), ("moe", 3 * EXPERTS)]
PB, NP = {}, 0
for _name, _n in PIECES:
    PB[_name] = NP
    NP += _n

BANKS = {}
_uses = [0] * 8
_next = 0


def _fill(*names):
    global _next
    for n in names:
        assert n not in BANKS, n
        BANKS[n] = (_next, _uses[_next])
        _uses[_next] += 1
        _next = (_next + 1) % 8


def _n(prefix, *dims):
    out = [prefix]
    for d in dims:
        out = [f"{o}.{i}" for o in out for i in (d if isinstance(d, (list, tuple)) else range(d))]
    return out


_fill(*_n("tx", 4), "txm")
_fill(*_n("k", 2, [0, 1, "m"]), *_n("q", 2, 2), *_n("v", 2, [0, 1, "m"]))
_fill(*_n("tk", 4), "tkm", *_n("tq", 4))
for _p in range(4):
    _fill(f"s.{2 * _p}", f"s.{2 * _p + 1}", f"sm.{_p}", f"li.{2 * _p}", f"li.{2 * _p + 1}", f"o.{_p}")
_fill(*_n("g", 2, 2), *_n("lg", KT, 2), *_n("lgate", 4), *_n("ga", 4), *_n("gb", 4))
_fill(*_n("tm", 4), *_n("tr", 4), *_n("br", 4), *_n("bl", 4), *_n("out1", 2, 2), *_n("mk", 2, 2), *_n("th", 4))
_next = 4
_ffn_uses = list(_uses)
_fill(*_n("mv", 2, 2), *_n("tmk", 4), *_n("t2", 4), "ik.0", "ik.1", "tal")
_fill(*_n("z", 2), *_n("iq", 2), *_n("gq", 2), *_n("gk", 2), "tik", *_n("gv", 2, 2))
_fill(*_n("sc0", 4), *_n("sc1", 4), *_n("tke", 4), *_n("dkv", 2), *_n("dq", 2, 2))
for _h in range(GH):
    _fill(f"at.{_h}", f"up.{_h}.0", f"up.{_h}.1", f"og.{_h}")
_fill(*_n("gg", 2, 2), "tdk", *_n("tdq", 4), *_n("mq", 2, 2))
for _g in range(DKVH):
    _fill(f"dl.{_g}.0", f"dl.{_g}.1", f"dl.{_g}.2", f"dp.{_g}.0", f"dp.{_g}.1", f"dp.{_g}.2", f"do.{_g}.0", f"do.{_g}.1")
_fill(*_n("tog", 4), *_n("tmq", 4), *_n("gt0", 4))
_fill(*_n("ml", 4), *_n("mp", 4), *_n("mo", 4))
_fill(*_n("wo0", 4))
for _b in (1, 2):
    for _j in range(4):
        _fill(f"gt{_b}.{_j}")
    for _j in range(4):
        _fill(f"wo{_b}.{_j}")
_next = 0
_fill(*_n("out2", 2, 2), *_n("t3", 4), "rl", "tc")
for _j in range(8):
    _next = (2 + _j) % 4
    _fill(f"cb.{_j}")

CONSTS = [("ident", P), ("tri", P), ("triq", P), ("blk", P), ("cos", RT * P), ("sin", RT * P), ("cosm", P), ("sinm", P),
          ("gown", HR), ("gprev", HR), ("gq", HR), ("gm", 2 * HR), ("rank", 4)]
PARAMS = [("mixw", 8), ("ffnw", 8), ("gmix", 8), ("gmem", 8), ("gffn", 8), ("convw", 32), ("convb", 8), ("ba", 8),
          ("bx", 8), ("lam", 8), ("ba2", 4), ("glan", 2), ("dqn", 1), ("dkn", 1), ("ikn", 1), ("mqn", 2), ("mkn", 2),
          ("bgate", 24), ("brt", 20), ("wa2", 512)]


def columns(table):
    at, out = 0, {}
    for n, w in table:
        out[n] = (at, at + w)
        at += w
    return out, at


CC, NC_ = columns(CONSTS)
PC, NPAR = columns(PARAMS)


def shape_constants():
    c = np.zeros((P, NC_), np.float32)

    def put(name, a):
        lo, hi = CC[name]
        c[:a.shape[0], lo:hi] = a.reshape(a.shape[0], hi - lo)

    i = np.arange(P)
    put("ident", np.eye(P, dtype=np.float32))
    put("tri", (i[:, None] <= i[None, :]).astype(np.float32))
    put("triq", (i[None, :] <= i[:, None]).astype(np.float32))
    put("blk", ((i[:, None] <= i[None, :]) & (i[:, None] // GCH == i[None, :] // GCH)).astype(np.int32).view(np.float32))
    inv = np.float32(10000.0) ** (-np.arange(0, P, 2, dtype=np.float32) / np.float32(P))
    ang = (np.arange(TM, dtype=np.float32)[:, None] * inv[None, :]).astype(np.float64)
    cos, sin = np.cos(ang).astype(np.float32), np.sin(ang).astype(np.float32)
    cos, sin = np.concatenate([cos, cos], 1), np.concatenate([-sin, sin], 1)
    for name, a in (("cos", cos), ("sin", sin)):
        put(name, a[META:].reshape(RT, P, P).transpose(1, 0, 2))
        put(name + "m", a[:META])
    lg = np.log(1.0 - 2.0 ** (-5.0 - np.arange(HR)))[None, :]
    m, scale = i[:, None].astype(np.float64), float(P) ** -0.5
    put("gown", (np.exp(-(m + 1) * lg) * scale).astype(np.float32))
    put("gprev", (np.exp((P - 1 - m) * lg) * scale).astype(np.float32))
    put("gq", np.exp((m + 1) * lg).astype(np.float32))
    first = np.exp((META - 1 - m[:META]) * lg) * scale
    put("gm", np.stack([first, first * np.exp(P * lg)], 1).astype(np.float32))
    put("rank", np.tile(np.arange(4, 0, -1, dtype=np.float32), (P, 1)))
    return c


def program(nc, weights, x, meta, mem, consts, params, small_w, final_w, out):
    import concourse.bass as bass
    from concourse import mybir

    f32, i32, f32r = mybir.dt.float32, mybir.dt.int32, mybir.dt.float32r
    ALU, ACT, AX = mybir.AluOpType, mybir.ActivationFunctionType, mybir.AxisListType
    V, S, G, E = nc.vector, nc.scalar, nc.gpsimd, nc.tensor
    mult, add, sub, amax, amin = ALU.mult, ALU.add, ALU.subtract, ALU.max, ALU.min

    with ExitStack() as ctx:
        def sb(name, shape, dt=f32):
            return ctx.enter_context(nc.sbuf_tensor(name, shape, dt))

        slab_base = -(-nc.sbuf_base // 64) * 64

        def sem(name):
            return ctx.enter_context(nc.semaphore(name))

        BIG = KT * TM
        sizes = [BIG] * 14
        sizes[8] = KT * (TM + CONV - 1)
        starts = np.concatenate([[0], np.cumsum(sizes)]).tolist()
        fixed = [("raw", SLOTS * PW), ("whi", SLOTS * PW), ("wlo", SLOTS * PW), ("con", NC_), ("par", NPAR),
                 ("swhi", KT * 108), ("swlo", KT * 108), ("small", 448)]
        fixed_at = np.concatenate([[0], np.cumsum([-(-n // 8) * 8 for _, n in fixed])]).tolist()
        slab = sb("slab", [P, fixed_at[-1] + starts[-1]])
        base = slab_base

        def place(name, at, n, dt=f32):
            return nc.alloc_sbuf_tensor_at(name, [P, n], dt, offset=base + 4 * at)

        raw, whi, wlo, con, par, swhi, swlo, small = (
            place(n, at, w, f32r if n in ("whi", "wlo", "swhi", "swlo") else f32) for (n, w), at in zip(fixed, fixed_at))
        raw, whi, wlo = (t[:, :].rearrange("p (s c) -> p s c", s=SLOTS) for t in (raw, whi, wlo))
        buf = [place(f"buf{i}", fixed_at[-1] + starts[i], sizes[i]) for i in range(14)]
        shares = place("shares", fixed_at[-1] + starts[2], 4096)

        def pair(name, hi, lo, n=T):
            out = [place(f"{name}_{part}", fixed_at[-1] + starts[i], KT * n, f32r)[:, :].rearrange("p (k t) -> p k t", k=KT)
                   for part, i in (("hi", hi), ("lo", lo))]
            return tuple(out)

        banks = [ctx.enter_context(nc.psum_tensor(f"bank{i}", [P, 512], f32)) for i in range(8)]

        def C(name):
            return con[:, CC[name][0]:CC[name][1]]

        def W(name):
            return par[:, PC[name][0]:PC[name][1]]

        def rows(b, at=0):
            return buf[b][:, at:at + 2048].rearrange("p (r c) -> p r c", r=RT)

        def cols(b, n=T, at=0):
            return buf[b][:, at:at + KT * n].rearrange("p (k t) -> p k t", k=KT)

        used = [0]

        def tiny(*dims):
            n = int(np.prod(dims))
            a = small[:, used[0]:used[0] + n]
            used[0] += n
            assert used[0] <= 448
            if len(dims) == 2:
                a = a.rearrange("p (a b) -> p a b", a=dims[0])
            if len(dims) == 3:
                a = a.rearrange("p (a b c) -> p a b c", a=dims[0], b=dims[1])
            return a

        def bc(a, *shape):
            return a.unsqueeze(len(a.shape)).to_broadcast(list(a.shape) + list(shape))

        def bc1(a, n):
            return a.unsqueeze(1).to_broadcast([a.shape[0], n] + list(a.shape[1:]))

        ident = C("ident")
        SW = tuple(t[:, :].rearrange("p (k c) -> p k c", k=KT) for t in (swhi, swlo))

        piece_loaded = [sem(f"piece_loaded{s}") for s in range(SLOTS)]
        piece_high = sem("piece_high")
        piece_split = sem("piece_split")
        small_high, small_split = sem("small_high"), sem("small_split")
        high = {n: sem(f"high_{n}") for n in ("tx", "txm", "conv", "lru", "tm", "tr", "mix", "th", "ffn", "t2", "tog", "do", "mo", "merge", "t3", "moe")}
        low = {n: sem(f"low_{n}") for n in ("conv", "lru", "mix", "ffn", "merge", "moe")}
        pieces_used = sem("pieces_used")
        evacuated = [sem(f"evacuated{b}") for b in range(8)]
        const_loaded, x_loaded, mem_loaded, final_w_loaded = (sem(n) for n in ("const_loaded", "x_loaded", "mem_loaded", "final_w_loaded"))
        out_stored = sem("out_stored")
        dve_chain, act_chain, pool_chain = sem("dve_chain"), sem("act_chain"), sem("pool_chain")
        NORMS = ("x", "mem", "h", "fin", "y", "z")
        squares = {n: sem(f"squares_{n}") for n in NORMS}
        meansq = {n: sem(f"meansq_{n}") for n in NORMS}
        rooted = {n: sem(f"rooted_{n}") for n in NORMS}
        normed = {n: sem(f"normed_{n}") for n in NORMS}
        turned = sem("turned")
        rotated = sem("rotated")
        padded = sem("padded")
        stat_cleared = sem("stat_cleared")
        idx_used, o_reduced, og_reduced = sem("idx_used"), sem("o_reduced"), sem("og_reduced")
        scored = sem("scored")
        retained = sem("retained")
        o_squared, o_summed, o_rooted, o_ready = (sem(n) for n in ("o_squared", "o_summed", "o_rooted", "o_ready"))
        lam_exp, lam_ready = sem("lam_exp"), sem("lam_ready")
        convolved = sem("convolved")
        decay_ready, lru_m2, lru_m, lru_gated, lru_ready = (sem(n) for n in ("decay_ready", "lru_m2", "lru_m", "lru_gated", "lru_ready"))
        mix_part, mixed = sem("mix_part"), sem("mixed")
        ffn_silu, ffn_act, ffn_added = sem("ffn_silu"), sem("ffn_act"), sem("ffn_added")
        mk_squared, mk_summed, mk_rooted, mk_ready = (sem(n) for n in ("mk_squared", "mk_summed", "mk_rooted", "mk_ready"))
        small_full = sem("small_full")
        ik_squared, ik_summed, ik_rooted, ik_ready = (sem(n) for n in ("ik_squared", "ik_summed", "ik_rooted", "ik_ready"))
        la_ready, cum_ready, e_ready, gla_ke = (sem(n) for n in ("la_ready", "cum_ready", "e_ready", "gla_ke"))
        idx_full = sem("idx_full")
        topped = sem("topped")
        gla_full = sem("gla_full")
        og_squared, og_summed, og_rooted, og_ready = (sem(n) for n in ("og_squared", "og_summed", "og_rooted", "og_ready"))
        dk_squared, dk_summed, dk_rooted, dk_ready = (sem(n) for n in ("dk_squared", "dk_summed", "dk_rooted", "dk_ready"))
        dq_squared, dq_summed, dq_rooted, dq_ready = (sem(n) for n in ("dq_squared", "dq_summed", "dq_rooted", "dq_ready"))
        mq_squared, mq_summed, mq_rooted, mq_ready = (sem(n) for n in ("mq_squared", "mq_summed", "mq_rooted", "mq_ready"))
        dsa_full, dsa_max, dsa_exp, dsa_p = (sem(n) for n in ("dsa_full", "dsa_max", "dsa_exp", "dsa_p"))
        mem_full, mem_max, mem_exp, mem_p = (sem(n) for n in ("mem_full", "mem_max", "mem_exp", "mem_p"))
        merged = sem("merged")
        route_full, route_max, route_exp, combined, shares_split = (sem(n) for n in ("route_full", "route_max", "route_exp", "combined", "shares_split"))
        moe_silu, moe_scaled, moe_act, moe_added = (sem(n) for n in ("moe_silu", "moe_scaled", "moe_act", "moe_added"))

        g4 = lambda a: a.rearrange("p (h t) -> p h t", h=GH)
        two = lambda b, at=0: buf[b][:, at:at + 1024].rearrange("p (a c) -> p a c", a=2)
        X = rows(0)
        XN, XT = rows(1), pair("xT", 2, 3, TM)
        SWR = buf[13][:, 1024:1024 + KT * 108]
        KR, QR, KTr, QTr, Vr = rows(4), rows(5), cols(6), cols(7), rows(9)
        LI = cols(8, TM + CONV - 1)
        ROT = buf[12][:, 0:2048].rearrange("p (a b c) -> p a b c", a=2, b=2)
        CV, CVP = cols(12, TM), pair("conv", 4, 5, TM)
        ST = buf[11][:, 0:4 * 384].rearrange("p (h c) -> p h c", h=4)
        VM, KM = buf[10][0:META, 0:1024], buf[10][0:META, 1024:2048]
        KTM = buf[10][:, 2048:2048 + 128].rearrange("p (h t) -> p h t", h=HR)
        XM = buf[13][0:META, 0:1024]
        SMT = buf[13][0:META, 0:1024].rearrange("p (a h t) -> p a h t", a=2, h=2)
        SQ = two(13, 1024)
        GR, O = rows(6), rows(1)
        RG, IG, TH, AA, A2, HS = cols(7, TM), cols(9, TM), cols(8, TM), cols(10, TM), cols(11, TM), cols(7, TM)
        LT, LTP = cols(13), pair("lru", 10, 11)
        GA, GB, RTP = cols(4), cols(5), pair("ret", 6, 7)
        MR, MJUNK, MTP = rows(12), rows(7), pair("memT", 8, 9)
        MIX, MIXP, PART = cols(1), pair("mixed", 2, 3), two(13)
        HTP = pair("normedT", 6, 7)
        SILU, SILC, HID = two(10), two(10, 1024), two(12)
        HIDP = tuple(place(f"hidden_{part}", fixed_at[-1] + starts[11] + at, 1024, f32r)[:, :].rearrange("p (a f t) -> p a f t", a=2, f=2)
                     for part, at in (("hi", 0), ("lo", 1024)))
        FW = buf[13][:, 0:1024]
        MKR, MSQ, MV, MKT = rows(4), two(5), rows(2), cols(3)
        ZA, ZB = buf[4][:, 0:1024], buf[4][:, 1024:2048]
        CUM, EC = buf[5][:, 0:1024], buf[5][:, 1024:2048]
        EI, RM = buf[8][:, 0:1024], buf[8][:, 1024:2048]
        QD, KI = g4(buf[9][:, 0:1024]), g4(buf[9][:, 1024:2048])
        KET = g4(buf[10][:, 0:1024])
        KE = buf[10][:, 1024:2048].rearrange("p (h r d) -> p h r d", h=GH, r=RT)
        GV = rows(4)
        ST8 = buf[11][:, 0:1536].rearrange("p (a n c) -> p a n c", a=2, n=3)
        ATM = buf[11][:, 1536:2048].rearrange("p (a c) -> p a c", a=2)
        OG, GG, OGP = rows(1), rows(4), pair("glaT", 9, 10)
        IQT = g4(buf[12][:, 0:1024])
        IKT, IKR = buf[12][:, 1024:1280], buf[12][:, 1280:1536].rearrange("p (r c) -> p r c", r=RT)
        SC = (buf[12][:, 1536:1664], buf[12][:, 1664:1920])
        ALT = buf[12][0:16, 1920:2176]
        RL, GSQ = two(13), buf[13][:, 0:1024]
        WK = (buf[13][:, 1024:1152], buf[13][:, 1152:1408])
        MB = (buf[13][:, 1408:1536], buf[13][:, 1536:1792])
        DQR, DKV = rows(5), buf[8][:, 0:1024].rearrange("p (r c) -> p r c", r=RT)
        DSQ = two(8, 1024)
        DQT, DKT = cols(9), buf[10][:, 0:512].rearrange("p (g t) -> p g t", g=DKVH)
        DP = buf[10][:, 512:2048].rearrange("p (a c) -> p a c", a=3)
        DPT0 = buf[12][:, 0:512]
        DPT1 = buf[12][:, 512:1536].rearrange("p (s c) -> p s c", s=2)
        ODP = pair("dsaT", 5, 4)
        MQR, MQT = rows(11), cols(12)
        MP = buf[8][:, 0:2048].rearrange("p (a c) -> p a c", a=4)
        MPT = buf[13][:, 0:2048].rearrange("p (h s t) -> p h s t", h=MH, s=2)
        OMP = pair("memoT", 11, 12)
        GS = cols(1)
        SG = buf[8][:, 0:2048].rearrange("p (a c) -> p a c", a=4)
        MPART = two(13)
        MRG, MRGP = cols(1), pair("merged", 9, 10)
        CB = shares[:, :].rearrange("p (e t) -> p e t", e=EXPERTS)
        CTP = tuple(place(f"shares_{part}", fixed_at[-1] + starts[13] + at, T, f32r)[0:16, :] for part, at in (("hi", 0), ("lo", T)))
        SEL = place("selector", fixed_at[-1] + starts[13] + 2 * T, 16, f32r)[0:16, :]

        stat = {n: tiny(3) for n in NORMS}
        oss, mkss, ogss = tiny(RT, HR), tiny(RT, MH), tiny(RT, GH)
        ikss, dkss, dqss, mqss = tiny(RT), tiny(RT, DKVH), tiny(RT, DH), tiny(RT, MH)
        lam = [tiny(8) for _ in range(6)]
        sp8, nsp8 = tiny(8), tiny(8)
        iwr = tiny(RT, 8)
        dec = tiny(GH, 4)
        top8 = tiny(RT, 8)
        dmx, dsum, mmx, msum = tiny(RT, DH), tiny(RT, DH), tiny(MH, RT), tiny(MH, RT)
        lr = tiny(RT, 20)
        gmx, gsh, gex, gsm, oh = tiny(RT), tiny(RT, 4), tiny(RT, 4), tiny(RT), tiny(RT, 4)
        el, eex, oh1, oh2, emx, tmp4, tmp16 = tiny(RT, 4), tiny(RT, 4), tiny(RT, 4), tiny(RT, 4), tiny(RT), tiny(RT, 4), tiny(RT, 4, 4)
        cmb = tiny(RT, 16)
        alr = tiny(RT, 16)

        splitters = {}

        def feed(eng, n):
            step, done = splitters[id(eng)]
            for i in range(done, min(n, NP - 1) + 1):
                step(i)
            splitters[id(eng)][1] = max(done, min(n, NP - 1) + 1)

        def full(eng, count):
            if id(eng) in splitters:
                feed(eng, count + 1)
            eng.wait_ge(pieces_used, count)

        def moved(eng, *names):
            for n in names:
                b, use = BANKS[n]
                eng.wait_ge(evacuated[b], use + 1)

        def release(ins, name):
            return ins.then_inc(evacuated[BANKS[name][0]], 1)

        def bank(name):
            return banks[BANKS[name][0]]

        class Chain:
            def __init__(self, eng, s):
                self.eng, self.s, self.n = eng, s, 0

            def __call__(self, ins):
                self.n += 1
                ins.then_inc(self.s, 1)
                self.eng.wait_ge(self.s, self.n)

        turns = {}
        for i, n in enumerate([*_n("tx", 4), "txm", *_n("tk", 4), "tkm", *_n("tq", 4), *_n("tm", 4), *_n("tr", 4), *_n("th", 4),
                               *_n("tmk", 4), *_n("t2", 4), "tal", "tik", *_n("tke", 4), "tdk", *_n("tdq", 4), *_n("tog", 4),
                               *_n("tmq", 4), *_n("t3", 4), "tc"]):
            turns[n] = i + 1

        block = ctx.enter_context(nc.Block())

        @block.sync
        def _(sp):
            sp.dma_start(X, x.rearrange("(r p) c -> p r c", p=P)).then_inc(x_loaded, 16)
            sp.dma_start(XM, meta).then_inc(x_loaded, 16)
            for n in range(SLOTS):
                sp.dma_start(raw[:, n, :], weights[n]).then_inc(piece_loaded[n], 16)
                if n == 0:
                    sp.dma_start(con[:, :], consts).then_inc(const_loaded, 16)
                    sp.dma_start(par[:, :], params).then_inc(const_loaded, 16)
                    sp.dma_start(SWR, small_w).then_inc(const_loaded, 16)
            laps = (NP - SLOTS) // SLOTS
            with sp.Fori(0, laps) as lap:
                for s in range(SLOTS):
                    sp.wait_ge(piece_split, lap * SLOTS + (s + 1))
                    sp.dma_start(raw[:, s, :], weights[bass.ds(lap * SLOTS + (SLOTS + s), 1), :, :].rearrange("a p c -> p (a c)"))\
                        .then_inc(piece_loaded[s], 16)
            for n in range((laps + 1) * SLOTS, NP):
                sp.wait_ge(piece_split, n - SLOTS + 1)
                sp.dma_start(raw[:, n % SLOTS, :], weights[n]).then_inc(piece_loaded[n % SLOTS], 16)
            for r in range(RT):
                sp.wait_ge(moe_added, 2 * r + 2)
                sp.dma_start(out[r * P:(r + 1) * P, :], X[:, r, :]).then_inc(out_stored, 16)
            sp.wait_ge(out_stored, 16 * RT)

        @block.tensor
        def _(pe):
            order = iter(BANKS)

            def begin(name):
                assert next(order) == name, name
                b, use = BANKS[name]
                if use:
                    pe.wait_ge(evacuated[b], use)
                return banks[b]

            def piece(n, at=0):
                pe.wait_ge(piece_split, at + (n + 1))
                return whi[:, n % SLOTS, :], wlo[:, n % SLOTS, :]

            def product(out_, lhs, rhs, start, stop):
                (lh, ll), (rh, rl) = lhs, rhs
                E.matmul(out_, lh, rh, start=start, stop=False)
                E.matmul(out_, lh, rl, start=False, stop=False)
                return E.matmul(out_, ll, rh, start=False, stop=stop)

            def both(pair_, *index):
                return tuple(part[index] for part in pair_)

            def cols_product(n, act, names, width=T, first=0, ready=None):
                w = [part.rearrange("p (k c) -> p k c", k=KT) for part in piece(n)]
                outs = [begin(x) for x in names]
                for c in range(2):
                    o = outs[c][:, 0:width] if len(outs) == 2 else outs[0][:, c * width:(c + 1) * width]
                    for k in range(KT):
                        if ready and c == 0:
                            ready(k)
                        last = product(o, both(w, ALL, k, slice(c * P, (c + 1) * P)), both(act, ALL, k, slice(first, first + width)), k == 0, k == KT - 1)
                last.then_inc(pieces_used, 1)

            def rows_product(n, act, names, tiles, ready=None):
                outs = [begin(x) for x in names]
                for half in range(2):
                    w = [part.rearrange("p (k c) -> p k c", k=4) for part in piece(n + half)]
                    for i, (o, (lo, hi)) in enumerate(zip(outs, tiles)):
                        for k in range(4):
                            if ready and i == 0:
                                ready(4 * half + k)
                            last = product(o[:, :], both(act, ALL, 4 * half + k, slice(lo, hi)), both(w, ALL, k),
                                           half == 0 and k == 0, half == 1 and k == 3)
                    last.then_inc(pieces_used, 1)

            def after_turn(prefix):
                return lambda k: moved(pe, f"{prefix}.{k // 2}") if k % 2 == 0 else None

            def after_parts(part):
                return lambda k: pe.wait_ge(part, k // 2 + 1) if k % 2 == 0 else None

            ALL = slice(None)
            TX = [(META, META + P), (META + P, TM)]
            TT = [(0, P), (P, T)]

            def turn(name, pairs):
                b = begin(name)
                for o, i in pairs:
                    n = i.shape[0]
                    last = E.transpose(b[0:i.shape[1], o:o + n], i, ident[0:n, 0:n])
                last.then_inc(turned, 1)

            def turn_rows(prefix, src):
                for j in range(4):
                    turn(f"{prefix}.{j}", [(kk * T + r * P, src[:, r, (2 * j + kk) * P:(2 * j + kk + 1) * P])
                                           for kk in range(2) for r in range(RT)])

            pe.wait_ge(const_loaded, 32)
            pe.wait_ge(small_split, 1)
            pe.wait_ge(normed["x"], 3)
            turn_rows("tx", XN)
            turn("txm", [(k * META, XM[:, k * P:(k + 1) * P]) for k in range(KT)])

            def ready_x(k):
                moved(pe, f"tx.{k // 2}")
                if k == 3:
                    moved(pe, "txm")

            for c in range(2):
                if c:
                    moved(pe, "txm")
                rows_product(PB["k"] + 2 * c, XT, _n(f"k.{c}", [0, 1, "m"]), TX + [(0, P)], None if c else ready_x)
            for c in range(2):
                rows_product(PB["q"] + 2 * c, XT, _n(f"q.{c}", 2), TX)
            for c in range(2):
                rows_product(PB["v"] + 2 * c, XT, _n(f"v.{c}", [0, 1, "m"]), TX + [(0, P)])
            pe.wait_ge(rotated, 6)
            for j in range(4):
                turn(f"tk.{j}", [(hh * T + r * P, KR[:, r, (2 * j + hh) * P:(2 * j + hh + 1) * P]) for hh in range(2) for r in range(RT)])
            turn("tkm", [(h * META, KM[:, h * P:(h + 1) * P]) for h in range(HR)])
            pe.wait_ge(rotated, 10)
            for j in range(4):
                turn(f"tq.{j}", [(hh * T + r * P, QR[:, r, (2 * j + hh) * P:(2 * j + hh + 1) * P]) for hh in range(2) for r in range(RT)])
            moved(pe, *_n("tk", 4), "tkm", *_n("tq", 4), *_n("v", 2, [0, 1, "m"]))
            for p in range(4):
                for h in (2 * p, 2 * p + 1):
                    b = begin(f"s.{h}")
                    E.matmul(b[:, 0:T], KTr[:, h, 0:P], QTr[:, h, :], start=True, stop=True)
                    E.matmul(b[:, T:T + P], KTr[:, h, P:T], QTr[:, h, P:T], start=True, stop=True).then_inc(scored, 1)
                b = begin(f"sm.{p}")
                for hh in range(2):
                    h = 2 * p + hh
                    last = E.matmul(b[0:META, hh * T:(hh + 1) * T], KTM[:, h, :], QTr[:, h, :], start=True, stop=True)
                last.then_inc(scored, 1)
                cols_product(PB["lru_in"] + p, XT, [f"li.{2 * p}", f"li.{2 * p + 1}"], TM)
                b = begin(f"o.{p}")
                moved(pe, f"s.{2 * p}", f"s.{2 * p + 1}", f"sm.{p}")
                for hh in range(2):
                    h = 2 * p + hh
                    hc = slice(h * P, (h + 1) * P)
                    s, sm = ST[:, h % 4, :], SMT[:, p % 2, hh, :]
                    for r in range(RT):
                        o = b[:, (hh * RT + r) * P:(hh * RT + r + 1) * P]
                        E.matmul(o, s[:, 0:P] if r == 0 else s[:, 2 * P:3 * P], Vr[:, r, hc], start=True, stop=False)
                        if r:
                            E.matmul(o, s[:, P:2 * P], Vr[:, 0, hc], start=False, stop=False)
                        last = E.matmul(o, sm[:, r * P:(r + 1) * P], VM[:, hc], start=False, stop=True)
                last.then_inc(retained, 1)
            for c in range(2):
                rows_product(PB["g_ret"] + 2 * c, XT, _n(f"g.{c}", 2), TX)
            wa, wx = ([part.rearrange("p (g k c) -> p g k c", g=LRUB, k=2) for part in piece(PB["lru_gates"] + i)] for i in range(2))
            pe.wait_ge(low["conv"], 4)
            for kt in range(KT):
                g, c = kt // 2, kt % 2
                for which, w in enumerate((wa, wx)):
                    b = begin(f"lg.{kt}.{which}")
                    for k in range(2):
                        last = product(b[:, 0:TM], both(w, ALL, g, k, slice(c * P, (c + 1) * P)), both(CVP, ALL, 2 * g + k), k == 0, k == 1)
                    if kt < KT - 1:
                        last.then_inc(small_full, 1)
                    else:
                        last.then_inc(pieces_used, 1)
            for j in range(4):
                cols_product(PB["lru_gate"] + j, XT, [f"lgate.{j}"], first=META)
            for j in range(4):
                cols_product(PB["gate_a"] + j, XT, [f"ga.{j}"], first=META)
            for j in range(4):
                cols_product(PB["gate_b"] + j, XT, [f"gb.{j}"], first=META)
            pe.wait_ge(normed["mem"], RT)
            turn_rows("tm", MR)
            pe.wait_ge(o_ready, 1)
            turn_rows("tr", O)
            for j in range(4):
                cols_product(PB["br_ret"] + j, RTP, [f"br.{j}"], ready=None if j else after_turn("tr"))
            pe.wait_ge(low["lru"], 1)
            for j in range(4):
                cols_product(PB["br_lru"] + j, LTP, [f"bl.{j}"])
            for c in range(2):
                rows_product(PB["out1"] + 2 * c, MIXP, _n(f"out1.{c}", 2), TT, None if c else after_parts(low["mix"]))
            moved(pe, *_n("tm", 4))
            for c in range(2):
                rows_product(PB["mem_k"] + 2 * c, MTP, _n(f"mk.{c}", 2), TT)
            pe.wait_ge(normed["h"], RT)
            turn_rows("th", XN)

            def up_step(n, at, s, gate_free=None, up_free=None, ready=None):
                for which, free in ((0, gate_free), (1, up_free)):
                    w = [part.rearrange("p (k c) -> p k c", k=KT) for part in piece(n + which, at)]
                    if free is not None:
                        pe.wait_ge(*free)
                    b = banks[4 + 2 * (s % 2) + which]
                    for c in range(2):
                        for k in range(KT):
                            if ready and which == 0 and c == 0:
                                ready(k)
                            last = product(b[:, c * T:(c + 1) * T], both(w, ALL, k, slice(c * P, (c + 1) * P)), both(HTP, ALL, k), k == 0, k == KT - 1)
                    last.then_inc(pieces_used, 1)

            def down_step(n, at, s, hidden_low, count, first=False, final=False):
                w = [part.rearrange("p (f c) -> p f c", f=2) for part in piece(n, at)]
                pe.wait_ge(hidden_low, count)
                for f in range(2):
                    for r in range(RT):
                        for c in range(2):
                            last = product(banks[2 * r + c][:, :], both(HIDP, ALL, s % 2, f, slice(r * P, (r + 1) * P)),
                                           both(w, ALL, f, slice(c * 512, (c + 1) * 512)), first and f == 0, final and f == 1)
                last.then_inc(pieces_used, 1)

            def hidden(base, steps, silu_done, act_done, hidden_low, ready=None, between=(), before_down=lambda: None):
                up_step(base, 0, 0, ready=ready)
                for step in between:
                    step()
                up_step(base + 2, 0, 1)
                before_down()
                down_step(base + 4, 0, 0, hidden_low, 1, first=True)
                pairs = (steps - 2) // 2
                with pe.Fori(0, pairs) as it:
                    for u in range(2):
                        n = base + 5 + 3 * u
                        up_step(n, it * 6, u, (silu_done, it * 2 + (1 + u)), (act_done, it * 2 + (1 + u)))
                        down_step(n + 2, it * 6, 1 + u, hidden_low, it * 2 + (2 + u))
                for s in range(1 + 2 * pairs, steps - 1):
                    n = base + 2 + 3 * s
                    up_step(n, 0, s + 1, (silu_done, s), (act_done, s))
                    down_step(n + 2, 0, s, hidden_low, s + 1)
                down_step(base + 3 * steps - 1, 0, steps - 1, hidden_low, steps, final=True)

            th_banks = [BANKS[f"th.{j}"][0] for j in range(4)]
            for b in range(8):
                if b not in th_banks:
                    pe.wait_ge(evacuated[b], _ffn_uses[b])
            hidden(PB["ffn"], FSTEPS, ffn_silu, ffn_act, low["ffn"], ready=after_turn("th"))
            pe.wait_ge(ffn_silu, FSTEPS)
            for c in range(2):
                rows_product(PB["mem_v"] + 2 * c, MTP, _n(f"mv.{c}", 2), TT)
            pe.wait_ge(ffn_added, 4)
            pe.wait_ge(mk_ready, 1)
            turn_rows("tmk", MKR)
            pe.wait_ge(normed["y"], RT)
            turn_rows("t2", XN)
            for r in range(RT):
                b = begin(f"ik.{r}")
                for k in range(KT):
                    if r == 0:
                        after_turn("t2")(k)
                    last = product(b[:, 0:88], both(HTP, ALL, k, slice(r * P, (r + 1) * P)), both(SW, ALL, k, slice(0, 88)), k == 0, k == KT - 1)
                last.then_inc(small_full, 1)
            moved(pe, "ik.0", "ik.1")
            turn("tal", [(r * P, alr[:, r, :]) for r in range(RT)])
            moved(pe, "tal")
            for j in range(2):
                b = begin(f"z.{j}")
                for hh in range(2):
                    h = 2 * j + hh
                    last = E.matmul(b[:, hh * T:(hh + 1) * T], W("wa2")[0:16, h * P:(h + 1) * P], ALT, start=True, stop=True)
                last.then_inc(small_full, 1)
            for j in range(2):
                cols_product(PB["iq"] + j, HTP, [f"iq.{j}"])
            for j in range(2):
                cols_product(PB["gq"] + j, HTP, [f"gq.{j}"])
            for j in range(2):
                cols_product(PB["gk"] + j, HTP, [f"gk.{j}"])
            pe.wait_ge(ik_ready, 1)
            turn("tik", [(r * P, IKR[:, r, :]) for r in range(RT)])
            for c in range(2):
                rows_product(PB["gv"] + 2 * c, HTP, _n(f"gv.{c}", 2), TT)
            moved(pe, "tik", "iq.0", "iq.1")
            for r, n in enumerate((P, T)):
                for j in range(4):
                    b = begin(f"sc{r}.{j}")
                    half = slice(64 * (j % 2), 64 * (j % 2) + 64)
                    for hh in range(2):
                        last = E.matmul(b[:, hh * n:(hh + 1) * n], IQT[half, 2 * (j // 2) + hh, r * P:(r + 1) * P], IKT[half, 0:n], start=True, stop=True)
                    last.then_inc(idx_full, 1)
            pe.wait_ge(gla_ke, 1)
            for h in range(GH):
                turn(f"tke.{h}", [(r * P, KET[:, h, r * P:(r + 1) * P]) for r in range(RT)])
            rows_product(PB["dkv"], HTP, _n("dkv", 2), TT)
            for c in range(2):
                rows_product(PB["dq"] + 2 * c, HTP, _n(f"dq.{c}", 2), TT)
            moved(pe, *_n("tke", 4), *_n("gv", 2, 2), "gk.0", "gk.1", "gq.0", "gq.1")
            pe.wait_ge(gla_ke, 1)
            for h in range(GH):
                hv = slice(h * T, (h + 1) * T)
                b = begin(f"at.{h}")
                for r in range(RT):
                    last = E.matmul(b[:, r * P:(r + 1) * P], KI[:, h, r * P:(r + 1) * P], QD[:, h, r * P:(r + 1) * P], start=True, stop=True)
                last.then_inc(gla_full, 1)
                b = begin(f"up.{h}.0")
                for r in range(RT):
                    last = E.matmul(b[:, r * T:(r + 1) * T], KE[0:GCH, h, r, :], GV[0:GCH, r, hv], start=True, stop=True)
                last.then_inc(gla_full, 1)
                b = begin(f"up.{h}.1")
                E.matmul(b[:, 0:T], KE[GCH:P, h, 0, :], GV[GCH:P, 0, hv], start=True, stop=True).then_inc(gla_full, 1)
                b = begin(f"og.{h}")
                moved(pe, f"at.{h}", f"up.{h}.0", f"up.{h}.1")
                for r in range(RT):
                    E.matmul(b[:, r * T:(r + 1) * T], ATM[:, h % 2, r * P:(r + 1) * P], GV[:, r, hv], start=True, stop=True, skip_group_check=True)
                    for n in range(2):
                        chunk = 2 * r + n
                        if chunk:
                            last = E.matmul(b[GCH * n:GCH * (n + 1), r * T:(r + 1) * T], QD[:, h, GCH * chunk:GCH * (chunk + 1)],
                                            ST8[:, h % 2, chunk - 1, :], start=False, stop=True, skip_group_check=True)
                last.then_inc(gla_full, 1)
            for c in range(2):
                rows_product(PB["gg"] + 2 * c, HTP, _n(f"gg.{c}", 2), TT)
            pe.wait_ge(dk_ready, 1)
            turn("tdk", [(g * T + r * P, DKV[:, r, g * P:(g + 1) * P]) for g in range(DKVH) for r in range(RT)])
            pe.wait_ge(dq_ready, 1)
            turn_rows("tdq", DQR)
            for c in range(2):
                rows_product(PB["mq"] + 2 * c, HTP, _n(f"mq.{c}", 2), TT)
            moved(pe, "tdk", *_n("tdq", 4), *_n("dkv", 2))
            for g in range(DKVH):
                for n in range(3):
                    b = begin(f"dl.{g}.{n}")
                    for hh in range(4 if n == 0 else 2):
                        h = DGRP * g + (hh if n == 0 else 2 * (n - 1) + hh)
                        keys, r = (P, 0) if n == 0 else (T, 1)
                        last = E.matmul(b[:, hh * keys:(hh + 1) * keys], DQT[:, h, r * P:(r + 1) * P], DKT[:, g, 0:keys], start=True, stop=True)
                    last.then_inc(dsa_full, 1)
                for n in range(3):
                    b = begin(f"dp.{g}.{n}")
                    pe.wait_ge(dsa_p, 3 * g + (1 if n == 0 else 3))
                    for hh in range(4):
                        if n == 0:
                            src = DP[:, 0, hh * P:(hh + 1) * P]
                        else:
                            src = DP[:, 1 + hh // 2, (hh % 2) * T + (n - 1) * P:(hh % 2) * T + n * P]
                        last = E.transpose(b[:, hh * P:(hh + 1) * P], src, ident)
                    last.then_inc(dsa_full, 1)
                for r in range(RT):
                    b = begin(f"do.{g}.{r}")
                    vc = slice(DKVH * P + g * P, DKVH * P + (g + 1) * P)
                    if r == 0:
                        moved(pe, f"dp.{g}.0")
                        E.matmul(b[:, :], DKV[:, 0, vc], DPT0, start=True, stop=True).then_inc(dsa_full, 1)
                    else:
                        moved(pe, f"dp.{g}.1", f"dp.{g}.2")
                        for s in range(2):
                            last = E.matmul(b[:, :], DKV[:, s, vc], DPT1[:, s, :], start=s == 0, stop=s == 1)
                        last.then_inc(dsa_full, 1)
            pe.wait_ge(og_ready, 1)
            turn_rows("tog", OG)
            pe.wait_ge(mq_ready, 1)
            turn_rows("tmq", MQR)
            for j in range(4):
                cols_product(PB["gate0"] + j, HTP, [f"gt0.{j}"])
            moved(pe, *_n("tmq", 4), *_n("tmk", 4), *_n("mv", 2, 2))
            for j in range(4):
                r = j // 2
                b = begin(f"ml.{j}")
                for hh in range(2):
                    h = 2 * (j % 2) + hh
                    for k in range(2):
                        last = E.matmul(b[:, hh * T:(hh + 1) * T], MQT[:, 2 * h + k, r * P:(r + 1) * P], MKT[:, 2 * h + k, :], start=k == 0, stop=k == 1)
                last.then_inc(mem_full, 1)
            pe.wait_ge(mem_p, 4)
            for h in range(MH):
                b = begin(f"mp.{h}")
                for s in range(2):
                    for r in range(RT):
                        last = E.transpose(b[:, s * T + r * P:s * T + (r + 1) * P],
                                           MP[:, 2 * r + h // 2, (h % 2) * T + s * P:(h % 2) * T + (s + 1) * P], ident)
                last.then_inc(mem_full, 1)
            for h in range(MH):
                b = begin(f"mo.{h}")
                moved(pe, f"mp.{h}")
                for c in range(2):
                    for s in range(2):
                        last = E.matmul(b[:, c * T:(c + 1) * T], MV[:, s, h * T + c * P:h * T + (c + 1) * P], MPT[:, h, s, :], start=s == 0, stop=s == 1)
                last.then_inc(mem_full, 1)
            moved(pe, *_n("tog", 4))
            for j in range(4):
                cols_product(PB["o_gla"] + j, OGP, [f"wo0.{j}"])
            for i, (gate, proj, act) in enumerate((("gate1", "o_dsa", ODP), ("gate2", "o_mem", OMP))):
                for j in range(4):
                    cols_product(PB[gate] + j, HTP, [f"gt{i + 1}.{j}"])
                if i == 0:
                    moved(pe, *_n("do", 2, 2))
                else:
                    moved(pe, *_n("mo", 4))
                for j in range(4):
                    cols_product(PB[proj] + j, act, [f"wo{i + 1}.{j}"])
            for c in range(2):
                rows_product(PB["out2"] + 2 * c, MRGP, _n(f"out2.{c}", 2), TT, None if c else after_parts(low["merge"]))
            pe.wait_ge(normed["z"], RT)
            turn_rows("t3", XN)
            b = begin("rl")
            for r in range(RT):
                for k in range(KT):
                    if r == 0:
                        after_turn("t3")(k)
                    last = product(b[:, r * 20:(r + 1) * 20], both(HTP, ALL, k, slice(r * P, (r + 1) * P)), both(SW, ALL, k, slice(88, 108)), k == 0, k == KT - 1)
            last.then_inc(route_full, 1)

            def turn_shares():
                pe.wait_ge(combined, 1)
                turn("tc", [(r * P, cmb[:, r, :]) for r in range(RT)])

            def spread_shares():
                pe.wait_ge(shares_split, 1)
                moved(pe, "tc")
                for j in range(8):
                    b = begin(f"cb.{j}")
                    for e in range(2):
                        sel = SEL[:, 2 * j + e:2 * j + e + 1].to_broadcast([16, P])
                        E.matmul(b[:, e * T:(e + 1) * T], sel, CTP[0], start=True, stop=False)
                        last = E.matmul(b[:, e * T:(e + 1) * T], sel, CTP[1], start=False, stop=True)
                    last.then_inc(route_full, 1)
                moved(pe, *_n("cb", 8))

            hidden(PB["moe"], EXPERTS, moe_silu, moe_act, low["moe"], between=[turn_shares], before_down=spread_shares)
            assert next(order, None) is None

        @block.scalar
        def _(act):
            chain = Chain(act, act_chain)

            def A(out_, in_, func, **kw):
                return S.activation(out_, in_, func, **kw)

            def round_piece(n, at=0, laps=0):
                act.wait_ge(piece_loaded[n % SLOTS], laps + 16 * (n // SLOTS + 1))
                if n >= SLOTS:
                    act.wait_ge(pieces_used, at + (n - SLOTS + 1))
                A(whi[:, n % SLOTS, :], raw[:, n % SLOTS, :], ACT.Copy).then_inc(piece_high, 1)

            splitters[id(act)] = [round_piece, 0]


            def row_squares(name, src):
                for r in range(RT):
                    A(XN[:, r, :], src[:, r, :], ACT.Square, accum_out=stat[name][:, r:r + 1]).then_inc(squares[name], 1)

            def row_roots(name, n=RT):
                act.wait_ge(meansq[name], 1)
                A(stat[name][:, 0:n], stat[name][:, 0:n], ACT.Sqrt).then_inc(rooted[name], 1)

            def turned_high(name, dst, w=None, n=T):
                for j in range(4):
                    act.wait_ge(turned, turns[f"{name}.{j}"])
                    if w is None:
                        last = A(dst[:, 2 * j:2 * j + 2, :], bank(f"{name}.{j}")[:, :].rearrange("p (k t) -> p k t", k=2), ACT.Copy)
                    else:
                        for c in range(2):
                            k = 2 * j + c
                            last = A(dst[:, k, :], bank(f"{name}.{j}")[:, c * T:(c + 1) * T], ACT.Copy, scale=w[:, k % w.shape[1]:k % w.shape[1] + 1])
                    last.then_inc(high[name], 1)

            act.wait_ge(x_loaded, 32)
            act.wait_ge(stat_cleared, 1)
            row_squares("x", X)
            A(ROT[0:META, 0, :, :].rearrange("p a c -> p (a c)"), XM, ACT.Square, accum_out=stat["x"][0:META, 2:3]).then_inc(squares["x"], 1)
            row_roots("x", 3)
            act.wait_ge(const_loaded, 48)
            A(swhi[:, :], SWR, ACT.Copy).then_inc(small_high, 1)
            chain(A(lam[0], W("lam"), ACT.Abs))
            A(lam[1], lam[0], ACT.Exp, scale=-1.0).then_inc(lam_exp, 1)
            feed(act, 0)
            turned_high("tx", XT[0][:, :, META:], W("mixw"))
            act.wait_ge(turned, turns["txm"])
            for k in range(KT):
                last = A(XT[0][:, k, 0:META], bank("txm")[:, k * META:(k + 1) * META], ACT.Copy, scale=W("mixw")[:, k:k + 1])
            last.then_inc(high["txm"], 1)
            feed(act, 2)
            for c in range(PB["v"]):
                feed(act, c + 1)
            for c in range(2):
                full(act, PB["v"] + 2 * c + 2)
                for r in range(RT):
                    release(A(Vr[:, r, c * 512:(c + 1) * 512], bank(f"v.{c}.{r}")[:, :], ACT.Copy), f"v.{c}.{r}")
                release(A(VM[:, c * 512:(c + 1) * 512], bank(f"v.{c}.m")[0:META, :], ACT.Copy), f"v.{c}.m")
            for j in range(4):
                act.wait_ge(turned, turns[f"tk.{j}"])
                release(A(KTr[:, 2 * j:2 * j + 2, :], bank(f"tk.{j}")[:, :].rearrange("p (k t) -> p k t", k=2), ACT.Copy), f"tk.{j}")
            act.wait_ge(turned, turns["tkm"])
            release(A(KTM, bank("tkm")[:, 0:P].rearrange("p (h t) -> p h t", h=HR), ACT.Copy), "tkm")
            for j in range(4):
                act.wait_ge(turned, turns[f"tq.{j}"])
                release(A(QTr[:, 2 * j:2 * j + 2, :], bank(f"tq.{j}")[:, :].rearrange("p (k t) -> p k t", k=2), ACT.Copy), f"tq.{j}")
            gm = C("gm").rearrange("p (c h) -> p c h", c=2)
            act.wait_ge(padded, 1)
            for p in range(4):
                feed(act, PB["lru_in"] + p + 1)
                act.wait_ge(scored, 3 * p + 3)
                if p >= 2:
                    act.wait_ge(retained, p - 1)
                for hh in range(2):
                    for r in range(RT):
                        last = A(SMT[:, p % 2, hh, r * P:(r + 1) * P], bank(f"sm.{p}")[0:META, hh * T + r * P:hh * T + (r + 1) * P], ACT.Copy,
                                 scale=gm[0:META, r, 2 * p + hh:2 * p + hh + 1])
                release(last, f"sm.{p}")
                act.wait_ge(pieces_used, PB["lru_in"] + p + 1)
                for c in range(2):
                    release(A(LI[:, 2 * p + c, CONV - 1:], bank(f"li.{2 * p + c}")[:, 0:TM], ACT.Copy), f"li.{2 * p + c}")
                act.wait_ge(retained, p + 1)
                for hh in range(2):
                    h = 2 * p + hh
                    last = A(O[:, :, h * P:(h + 1) * P], bank(f"o.{p}")[:, hh * T:(hh + 1) * T].rearrange("p (r c) -> p r c", r=RT), ACT.Copy,
                             scale=C("gq")[:, h:h + 1])
                release(last, f"o.{p}")
                act.wait_ge(convolved, 2 * p + 2)
                A(CVP[0][:, 2 * p:2 * p + 2, :], CV[:, 2 * p:2 * p + 2, :], ACT.Copy).then_inc(high["conv"], 1)
            feed(act, PB["g_ret"] + 1)
            feed(act, PB["g_ret"] + 2)
            act.wait_ge(o_summed, 1)
            A(oss, oss, ACT.Sqrt).then_inc(o_rooted, 1)
            for c in range(2):
                full(act, PB["g_ret"] + 2 * c + 2)
                for r in range(RT):
                    release(A(GR[:, r, c * 512:(c + 1) * 512], bank(f"g.{c}.{r}")[:, :], ACT.Silu), f"g.{c}.{r}")
            feed(act, PB["lru_gate"])
            act.wait_ge(o_rooted, 1)
            for kt in range(KT):
                for which, (dst, bias) in enumerate(((RG, "ba"), (IG, "bx"))):
                    n = 2 * kt + which + 1
                    if kt < KT - 1:
                        act.wait_ge(small_full, n)
                    else:
                        act.wait_ge(pieces_used, PB["lru_gates"] + which + 1)
                    release(A(dst[:, kt, :], bank(f"lg.{kt}.{which}")[:, 0:TM], ACT.Sigmoid, bias=W(bias)[:, kt:kt + 1]), f"lg.{kt}.{which}")
            moved(act, "lg.7.0")
            act.wait_ge(lam_ready, 1)
            feed(act, PB["lru_gate"] + 1)
            for kt in range(KT):
                A(TH[:, kt, :], RG[:, kt, :], ACT.Tanh, scale=sp8[:, kt:kt + 1])
                last = A(AA[:, kt, :], RG[:, kt, :], ACT.Exp, scale=nsp8[:, kt:kt + 1])
                if kt in (3, 7):
                    chain(last)
                    feed(act, PB["lru_gate"] + (2 if kt == 3 else 3))
            A(A2, AA, ACT.Square).then_inc(decay_ready, 1)
            for j in range(4):
                full(act, PB["lru_gate"] + j + 1)
                release(A(LT[:, 2 * j:2 * j + 2, :], bank(f"lgate.{j}")[:, :].rearrange("p (k t) -> p k t", k=2), ACT.Gelu_apprx_tanh), f"lgate.{j}")
            act.wait_ge(lru_m2, 1)
            A(TH, TH, ACT.Sqrt).then_inc(lru_m, 1)
            act.wait_ge(lru_gated, 1)
            act.dma_start(MR, mem.rearrange("(r p) c -> p r c", p=P)).then_inc(mem_loaded, 16)
            for j in range(4):
                full(act, PB["gate_a"] + j + 1)
                release(A(GA[:, 2 * j:2 * j + 2, :], bank(f"ga.{j}")[:, :].rearrange("p (k t) -> p k t", k=2), ACT.Sigmoid), f"ga.{j}")
            act.wait_ge(lru_ready, 1)
            A(LTP[0], LT, ACT.Copy).then_inc(high["lru"], 1)
            full(act, PB["gate_b"] + 1)
            release(A(GB[:, 0:2, :], bank("gb.0")[:, :].rearrange("p (k t) -> p k t", k=2), ACT.Sigmoid), "gb.0")
            act.wait_ge(mem_loaded, 16)
            for r in range(RT):
                A(MJUNK[:, r, :], MR[:, r, :], ACT.Square, accum_out=stat["mem"][:, r:r + 1]).then_inc(squares["mem"], 1)
            row_roots("mem")
            for j in range(1, 4):
                full(act, PB["gate_b"] + j + 1)
                release(A(GB[:, 2 * j:2 * j + 2, :], bank(f"gb.{j}")[:, :].rearrange("p (k t) -> p k t", k=2), ACT.Sigmoid), f"gb.{j}")
            turned_high("tm", MTP[0], W("gmem"))
            turned_high("tr", RTP[0])
            for j in range(4):
                feed(act, PB["br_lru"] + j + 2)
                act.wait_ge(mixed, j + 1)
                A(MIXP[0][:, 2 * j:2 * j + 2, :], MIX[:, 2 * j:2 * j + 2, :], ACT.Copy).then_inc(high["mix"], 1)
            full(act, PB["out1"] + 4)
            moved(act, *_n("out1", 2, 2))
            row_squares("h", X)
            feed(act, PB["mem_k"] + 2)
            row_roots("h")

            def head_squares(c, r, name, rows_, sq, i, summed, pieces):
                full(act, pieces)
                A(rows_[:, r, c * 512:(c + 1) * 512], bank(name)[:, :], ACT.Copy)
                if i >= 2:
                    act.wait_ge(summed, i - 1)
                release(A(sq[:, i % 2, :], bank(name)[:, :], ACT.Square), name)

            i = 0
            for c in range(2):
                for r in range(RT):
                    head_squares(c, r, f"mk.{c}.{r}", MKR, MSQ, i, mk_summed, PB["mem_k"] + 2 * c + 2)
                    i += 1
            act.wait_ge(mk_summed, 5)
            A(mkss, mkss, ACT.Sqrt).then_inc(mk_rooted, 1)
            turned_high("th", HTP[0], W("ffnw"))

            def silus(base, steps, silu_done, act_done, hidden_high, hidden_low):
                def one(it, u):
                    s = it * 2 + u
                    n, at, laps = base + 3 * u + 2, it * 6, it * 32
                    static = isinstance(it, int)
                    n0 = n + 6 * it if static else n
                    go = (lambda k: feed(act, n0 + k)) if static else (lambda k: round_piece(n0 + k, at, laps))
                    act.wait_ge(pieces_used, base + (1 if static and s == 0 else s * 3) if static else s * 3 + base)
                    if not (static and s < 2):
                        act.wait_ge(act_done, s - 1)
                    A(SILU[:, u % 2, :], banks[4 + 2 * (u % 2)][:, :], ACT.Silu).then_inc(silu_done, 1)
                    go(0)
                    go(1)
                    act.wait_ge(act_done, s + 1)
                    if not (static and s < 2):
                        act.wait_ge(pieces_used, s * 3 + (base - 1))
                    A(HIDP[0][:, u % 2].rearrange("p f t -> p (f t)"), HID[:, u % 2, :], ACT.Copy).then_inc(hidden_high, 1)
                    go(2)
                feed(act, base + 1)
                one(0, 0)
                one(0, 1)
                last = (steps - (base + 3 * steps == NP)) // 2
                with act.Fori(1, last) as it:
                    for u in range(2):
                        one(it, u)
                splitters[id(act)][1] = base + 6 * last + 2
                for s in range(2 * last, steps):
                    one(s // 2, s % 2)

            silus(PB["ffn"], FSTEPS, ffn_silu, ffn_act, high["ffn"], low["ffn"])
            act.wait_ge(ffn_added, 4)
            row_squares("fin", X)
            row_roots("fin")
            full(act, PB["mem_v"] + 2)
            act.wait_ge(normed["fin"], RT)
            row_squares("y", X)
            row_roots("y")
            for c in range(2):
                full(act, PB["mem_v"] + 2 * c + 2)
                for r in range(RT):
                    release(A(MV[:, r, c * 512:(c + 1) * 512], bank(f"mv.{c}.{r}")[:, :], ACT.Copy), f"mv.{c}.{r}")
            turned_high("t2", HTP[0], W("gmix"))
            feed(act, PB["iq"] + 1)
            for r in range(RT):
                act.wait_ge(small_full, 14 + 1 + r)
                A(alr[:, r, :], bank(f"ik.{r}")[:, 0:16], ACT.Copy)
                A(IKR[:, r, 0:64], bank(f"ik.{r}")[:, 16:80], ACT.Copy)
                A(iwr[:, r, :], bank(f"ik.{r}")[:, 80:88], ACT.Copy, scale=float(8 ** -0.5 * 64 ** -0.5))
                release(A(IKR[:, r, 64:128], bank(f"ik.{r}")[:, 16:80], ACT.Square, accum_out=ikss[:, r:r + 1]), f"ik.{r}")
            act.wait_ge(turned, turns["tal"])
            release(A(ALT, bank("tal")[0:16, 0:T], ACT.Copy), "tal")
            act.wait_ge(ik_summed, 1)
            A(ikss, ikss, ACT.Sqrt).then_inc(ik_rooted, 1)
            feed(act, PB["gq"])
            moved(act, "z.0", "z.1")
            chain(A(ZA, ZA, ACT.Abs))
            chain(A(ZA, ZA, ACT.Exp, scale=-1.0))
            A(ZA, ZA, ACT.Ln, bias=1.0).then_inc(la_ready, 1)
            for j in range(2):
                full(act, PB["iq"] + j + 1)
                release(A(IQT[:, 2 * j:2 * j + 2, :], bank(f"iq.{j}")[:, :].rearrange("p (k t) -> p k t", k=2), ACT.Copy), f"iq.{j}")
            act.wait_ge(cum_ready, 1)
            A(EC, CUM, ACT.Exp, scale=1.0 / 16).then_inc(e_ready, 1)
            feed(act, PB["iq"] + 4)
            A(EI, CUM, ACT.Exp, scale=-1.0 / 16).then_inc(e_ready, 1)
            for c in range(4):
                feed(act, PB["gq"] + c + 2)
            for c in range(2):
                full(act, PB["gv"] + 2 * c + 2)
                for r in range(RT):
                    release(A(GV[:, r, c * 512:(c + 1) * 512], bank(f"gv.{c}.{r}")[:, :], ACT.Copy), f"gv.{c}.{r}")
            for i in range(8):
                r, j = i // 4, i % 4
                n = (P, T)[r]
                act.wait_ge(idx_full, i + 1)
                if i >= 2:
                    act.wait_ge(idx_used, i - 1)
                release(A(RL[:, i % 2, 0:2 * n], bank(f"sc{r}.{j}")[:, 0:2 * n], ACT.Relu), f"sc{r}.{j}")
            for h in range(GH):
                act.wait_ge(turned, turns[f"tke.{h}"])
                release(A(KE[:, h, :, :], bank(f"tke.{h}")[:, 0:T].rearrange("p (r d) -> p r d", r=RT), ACT.Copy), f"tke.{h}")
            for r in range(RT):
                full(act, PB["dkv"] + 2)
                A(DKV[:, r, :], bank(f"dkv.{r}")[:, :], ACT.Copy)
                release(A(DSQ[:, r, 0:256], bank(f"dkv.{r}")[:, 0:256], ACT.Square), f"dkv.{r}")
            i = 2
            for c in range(2):
                for r in range(RT):
                    full(act, PB["dq"] + 2 * c + 2)
                    A(DQR[:, r, c * 512:(c + 1) * 512], bank(f"dq.{c}.{r}")[:, :], ACT.Copy)
                    if i < 4:
                        act.wait_ge(dk_summed, i - 1)
                    else:
                        act.wait_ge(dq_summed, i - 3)
                    release(A(DSQ[:, i % 2, :], bank(f"dq.{c}.{r}")[:, :], ACT.Square), f"dq.{c}.{r}")
                    i += 1
            act.wait_ge(dk_summed, 3)
            A(dkss, dkss, ACT.Sqrt).then_inc(dk_rooted, 1)
            act.wait_ge(dq_summed, 5)
            A(dqss, dqss, ACT.Sqrt).then_inc(dq_rooted, 1)
            feed(act, PB["gg"] + 1)
            for h in range(GH):
                act.wait_ge(gla_full, 4 * h + 4)
                release(A(OG[:, :, h * T:(h + 1) * T], bank(f"og.{h}")[:, :].rearrange("p (r c) -> p r c", r=RT), ACT.Copy), f"og.{h}")
            for c in range(2):
                full(act, PB["gg"] + 2 * c + 2)
                for r in range(RT):
                    release(A(GG[:, r, c * 512:(c + 1) * 512], bank(f"gg.{c}.{r}")[:, :], ACT.Silu), f"gg.{c}.{r}")
            act.wait_ge(og_summed, 1)
            A(ogss, ogss, ACT.Sqrt).then_inc(og_rooted, 1)
            act.wait_ge(turned, turns["tdk"])
            release(A(DKT, bank("tdk")[:, :].rearrange("p (g t) -> p g t", g=DKVH), ACT.Copy, scale=W("dkn")[:, 0:1]), "tdk")
            for j in range(4):
                act.wait_ge(turned, turns[f"tdq.{j}"])
                release(A(DQT[:, 2 * j:2 * j + 2, :], bank(f"tdq.{j}")[:, :].rearrange("p (k t) -> p k t", k=2), ACT.Copy, scale=W("dqn")[:, 0:1]), f"tdq.{j}")
            i = 0
            for c in range(2):
                for r in range(RT):
                    full(act, PB["mq"] + 2 * c + 2)
                    A(MQR[:, r, c * 512:(c + 1) * 512], bank(f"mq.{c}.{r}")[:, :], ACT.Copy)
                    if i < 2:
                        act.wait_ge(dq_summed, 4)
                    else:
                        act.wait_ge(mq_summed, i - 1)
                    release(A(DSQ[:, i % 2, :], bank(f"mq.{c}.{r}")[:, :], ACT.Square), f"mq.{c}.{r}")
                    i += 1
            act.wait_ge(mq_summed, 5)
            A(mqss, mqss, ACT.Sqrt).then_inc(mq_rooted, 1)
            feed(act, PB["gate0"] + 1)
            for g in range(DKVH):
                for n in range(3):
                    act.wait_ge(dsa_max, 3 * g + n + 1)
                    for hh in range(4 if n == 0 else 2):
                        h = DGRP * g + (hh if n == 0 else 2 * (n - 1) + hh)
                        keys, r = (P, 0) if n == 0 else (T, 1)
                        last = A(DP[:, n, hh * keys:(hh + 1) * keys], DP[:, n, hh * keys:(hh + 1) * keys], ACT.Exp,
                                 bias=dmx[:, r, h:h + 1], accum_out=dsum[:, r, h:h + 1])
                    last.then_inc(dsa_exp, 1)
                for n in range(3):
                    act.wait_ge(dsa_full, 8 * g + 3 + n + 1)
                    dst = DPT0 if n == 0 else DPT1[:, n - 1, :]
                    release(A(dst, bank(f"dp.{g}.{n}")[:, :], ACT.Copy), f"dp.{g}.{n}")
                for r in range(RT):
                    act.wait_ge(dsa_full, 8 * g + 6 + r + 1)
                    A(ODP[0][:, DGRP * g:DGRP * (g + 1), r * P:(r + 1) * P], bank(f"do.{g}.{r}")[:, :].rearrange("p (h t) -> p h t", h=DGRP), ACT.Copy)\
                        .then_inc(high["do"], 1)
            turned_high("tog", OGP[0], W("glan"))
            for j in range(4):
                full(act, PB["gate0"] + j + 1)
                for c in range(2):
                    last = A(GS[:, 2 * j + c, :], bank(f"gt0.{j}")[:, c * T:(c + 1) * T], ACT.Sigmoid, bias=W("bgate")[:, 2 * j + c:2 * j + c + 1])
                release(last, f"gt0.{j}")
            for j in range(4):
                r = j // 2
                act.wait_ge(mem_max, j + 1)
                for hh in range(2):
                    h = 2 * (j % 2) + hh
                    last = A(MP[:, j, hh * T:(hh + 1) * T], bank(f"ml.{j}")[:, hh * T:(hh + 1) * T], ACT.Exp, bias=mmx[:, h, r:r + 1],
                             accum_out=msum[:, h, r:r + 1])
                release(last, f"ml.{j}")
            for h in range(MH):
                act.wait_ge(mem_full, 4 + h + 1)
                release(A(MPT[:, h, :, :], bank(f"mp.{h}")[:, :].rearrange("p (s t) -> p s t", s=2), ACT.Copy), f"mp.{h}")
            for h in range(MH):
                act.wait_ge(mem_full, 8 + h + 1)
                A(OMP[0][:, 2 * h:2 * h + 2, :], bank(f"mo.{h}")[:, :].rearrange("p (k t) -> p k t", k=2), ACT.Copy).then_inc(high["mo"], 1)
            for c in range(PB["o_gla"] + 2, PB["gate1"] + 2):
                feed(act, c)
            for i, gate in enumerate(("gate1", "gate2")):
                for j in range(4):
                    full(act, PB[gate] + j + 1)
                    if i:
                        moved(act, f"wo1.{j}")
                    for c in range(2):
                        col = 8 * (i + 1) + 2 * j + c
                        last = A(SG[:, j, c * T:(c + 1) * T], bank(f"gt{i + 1}.{j}")[:, c * T:(c + 1) * T], ACT.Sigmoid, bias=W("bgate")[:, col:col + 1])
                    release(last, f"gt{i + 1}.{j}")
                for j in range(4):
                    feed(act, PB[gate] + 4 + j + 2)
                    if i:
                        act.wait_ge(merged, 4 + j + 1)
                        A(MRGP[0][:, 2 * j:2 * j + 2, :], MRG[:, 2 * j:2 * j + 2, :], ACT.Copy).then_inc(high["merge"], 1)
            full(act, PB["out2"] + 4)
            moved(act, *_n("out2", 2, 2))
            row_squares("z", X)
            row_roots("z")
            turned_high("t3", HTP[0], W("gffn"))
            feed(act, PB["moe"] + 2)
            act.wait_ge(route_max, 1)
            A(gex, gsh, ACT.Exp).then_inc(route_exp, 1)
            act.wait_ge(route_max, 2)
            A(eex, el, ACT.Exp).then_inc(route_exp, 1)
            feed(act, PB["moe"] + 3)
            for j in range(0, 8):
                act.wait_ge(route_full, 2 + j)
                release(A(CB[:, 2 * j:2 * j + 2, :], bank(f"cb.{j}")[:, :].rearrange("p (e t) -> p e t", e=2), ACT.Copy), f"cb.{j}")
            silus(PB["moe"], EXPERTS, moe_silu, moe_act, high["moe"], low["moe"])

        @block.vector
        def _(dve):
            chain = Chain(dve, dve_chain)

            def split_piece(n, at=0):
                dve.wait_ge(piece_high, at + (n + 1))
                V.tensor_tensor(wlo[:, n % SLOTS, :], raw[:, n % SLOTS, :], whi[:, n % SLOTS, :].bitcast(f32), sub).then_inc(piece_split, 1)

            splitters[id(dve)] = [split_piece, 0]

            def row_norm(name, src, dst, n=RT):
                s = stat[name][:, 0:n]
                dve.wait_ge(squares[name], n)
                V.tensor_scalar(s, s, 1.0 / D, EPS, mult, add).then_inc(meansq[name], 1)
                dve.wait_ge(rooted[name], 1)
                chain(V.reciprocal(s, s))
                for r in range(RT):
                    V.tensor_scalar(dst[:, r, :], src[:, r, :], s[:, r:r + 1], None, mult).then_inc(normed[name], 1)

            def turned_low(name, dst, w=None):
                for j in range(4):
                    dve.wait_ge(high[name], j + 1)
                    b, (hi, lo) = bank(f"{name}.{j}"), dst
                    if w is None:
                        last = V.tensor_tensor(lo[:, 2 * j:2 * j + 2, :], b[:, :].rearrange("p (k t) -> p k t", k=2), hi[:, 2 * j:2 * j + 2, :].bitcast(f32), sub)
                    else:
                        for c in range(2):
                            k = 2 * j + c
                            last = V.scalar_tensor_tensor(lo[:, k, :], b[:, c * T:(c + 1) * T], w[:, k % w.shape[1]:k % w.shape[1] + 1], hi[:, k, :].bitcast(f32), mult, sub)
                    release(last, f"{name}.{j}")

            def turned_scaled(prefix, dst, w):
                for j in range(4):
                    dve.wait_ge(turned, turns[f"{prefix}.{j}"])
                    release(V.tensor_tensor(dst[:, 2 * j:2 * j + 2, :], bank(f"{prefix}.{j}")[:, :].rearrange("p (k t) -> p k t", k=2), bc(w, T), mult), f"{prefix}.{j}")

            V.memset(stat["x"][:, 2:3], 1.0).then_inc(stat_cleared, 1)
            dve.wait_ge(const_loaded, 48)
            row_norm("x", X, XN, 3)
            V.tensor_scalar(XM, XM, stat["x"][0:META, 2:3], None, mult).then_inc(normed["x"], 1)
            dve.wait_ge(small_high, 1)
            V.tensor_tensor(swlo[:, :], SWR, swhi[:, :].bitcast(f32), sub).then_inc(small_split, 1)
            feed(dve, 0)
            turned_low("tx", tuple(part[:, :, META:] for part in XT), W("mixw"))
            dve.wait_ge(high["txm"], 1)
            for k in range(KT):
                last = V.scalar_tensor_tensor(XT[1][:, k, 0:META], bank("txm")[:, k * META:(k + 1) * META], W("mixw")[:, k:k + 1], XT[0][:, k, 0:META].bitcast(f32), mult, sub)
            release(last, "txm")
            feed(dve, 2)
            dve.wait_ge(lam_exp, 1)
            l0, l1, l2, l3, l4 = lam[1], lam[2], lam[3], lam[4], lam[5]
            chain(V.tensor_scalar(l1, l0, 2.0, None, add))
            chain(V.reciprocal(l1, l1))
            chain(V.tensor_tensor(l1, l0, l1, mult))
            chain(V.tensor_tensor(l2, l1, l1, mult))
            chain(V.tensor_scalar(l3, l2, 1.0 / 17, 1.0 / 15, mult, add))
            for d in (13, 11, 9, 7, 5, 3, 1):
                chain(V.tensor_tensor(l3, l3, l2, mult))
                chain(V.tensor_scalar(l3, l3, 1.0 / d, None, add))
            chain(V.tensor_tensor(l3, l3, l1, mult))
            chain(V.tensor_scalar(l4, W("lam"), -1.0, 0.0, mult, amax))
            chain(V.scalar_tensor_tensor(l4, l3, 2.0, l4, mult, add))
            V.tensor_scalar(sp8, l4, 8.0, None, mult)
            V.tensor_scalar(nsp8, l4, -8.0, None, mult).then_inc(lam_ready, 1)

            inst = 0
            for what, tiles in (("k", [0, 1, "m"]), ("q", [0, 1])):
                for c in range(2):
                    full(dve, PB[what] + 2 * c + 2)
                    for r in tiles:
                        n = META if r == "m" else P
                        cs, sn = (C("cosm"), C("sinm")) if r == "m" else (C("cos")[:, r * P:(r + 1) * P], C("sin")[:, r * P:(r + 1) * P])
                        src = bank(f"{what}.{c}.{r}")[0:n, :].rearrange("p (h x) -> p h x", h=4)
                        if inst >= 2:
                            dve.wait_ge(rotated, inst - 1)
                        t1, t2 = (ROT[0:n, inst % 2, i, :].rearrange("p (h x) -> p h x", h=4) for i in range(2))
                        V.tensor_tensor(t1, src, bc1(cs[0:n, :], 4), mult)
                        V.tensor_tensor(t2[:, :, 0:64], src[:, :, 64:128], bc1(sn[0:n, 0:64], 4), mult)
                        release(V.tensor_tensor(t2[:, :, 64:128], src[:, :, 0:64], bc1(sn[0:n, 64:128], 4), mult), f"{what}.{c}.{r}")
                        inst += 1
            for p in range(4):
                feed(dve, PB["lru_in"] + p + 1)
                for h in (2 * p, 2 * p + 1):
                    dve.wait_ge(scored, 3 * p + h % 2 + 1)
                    if p >= 2:
                        dve.wait_ge(retained, p - 1)
                    b, s = bank(f"s.{h}"), ST[:, h % 4, :]
                    V.tensor_scalar(s[:, P:2 * P], b[:, P:2 * P], C("gprev")[:, h:h + 1], None, mult)
                    V.scalar_tensor_tensor(s[:, 0:P], b[:, 0:P], C("gown")[:, h:h + 1], C("tri"), mult, mult)
                    release(V.scalar_tensor_tensor(s[:, 2 * P:3 * P], b[:, 2 * P:3 * P], C("gown")[:, h:h + 1], C("tri"), mult, mult), f"s.{h}")
                if p:
                    dve.wait_ge(o_squared, p)
                    V.tensor_reduce(oss[:, :, 2 * p - 2:2 * p], SQ[:, (p - 1) % 2, :].rearrange("p (r h c) -> p r h c", r=RT, h=2), AX.X, add).then_inc(o_reduced, 1)
                moved(dve, f"li.{2 * p}", f"li.{2 * p + 1}")
                w = W("convw").rearrange("p (j k) -> p j k", j=CONV)
                for k in (2 * p, 2 * p + 1):
                    chain(V.tensor_scalar(CV[:, k, :], LI[:, k, 0:TM], w[:, 0, k:k + 1], W("convb")[:, k:k + 1], mult, add))
                    for j in range(1, CONV):
                        ins = V.scalar_tensor_tensor(CV[:, k, :], LI[:, k, j:j + TM], w[:, j, k:k + 1], CV[:, k, :], mult, add)
                        if j < CONV - 1:
                            chain(ins)
                        else:
                            ins.then_inc(convolved, 1)
            feed(dve, PB["g_ret"] + 1)
            dve.wait_ge(o_squared, 4)
            V.tensor_reduce(oss[:, :, 6:8], SQ[:, 1, :].rearrange("p (r h c) -> p r h c", r=RT, h=2), AX.X, add).then_inc(o_reduced, 1)
            dve.wait_ge(o_reduced, 4)
            V.tensor_scalar(oss, oss, 1.0 / P, EPS, mult, add).then_inc(o_summed, 1)
            feed(dve, PB["g_ret"] + 2)
            dve.wait_ge(o_rooted, 1)
            chain(V.reciprocal(oss, oss))
            hv = lambda a, n: a.rearrange("p r (h c) -> p r h c", h=n)
            for r in range(RT):
                chain(V.tensor_tensor(hv(O, HR)[:, r], hv(O, HR)[:, r], bc(oss[:, r, :], P), mult))
            for c in range(3):
                feed(dve, PB["g_ret"] + 3 + c)
            moved(dve, *_n("g", 2, 2))
            V.tensor_tensor(O, O, GR, mult).then_inc(o_ready, 1)
            feed(dve, PB["lru_gate"])
            moved(dve, "lg.7.1")
            feed(dve, PB["lru_gate"] + 1)
            V.tensor_tensor(IG, IG, CV, mult).then_inc(lru_gated, 1)
            feed(dve, PB["lru_gate"] + 2)
            dve.wait_ge(decay_ready, 1)
            V.scalar_tensor_tensor(TH, A2, 1.0, TH, add, mult).then_inc(lru_m2, 1)
            dve.wait_ge(lru_gated, 1)
            for c in range(3):
                feed(dve, PB["lru_gate"] + 3 + c)
            dve.wait_ge(lru_m, 1)
            chain(V.tensor_tensor(IG, IG, TH, mult))
            feed(dve, PB["gate_a"] + 2)
            for k in range(KT):
                last = V.tensor_tensor_scan(HS[:, k, :], AA[:, k, :], IG[:, k, :], 0.0, mult, add)
            chain(last)
            feed(dve, PB["gate_a"] + 3)
            moved(dve, *_n("lgate", 4))
            V.tensor_tensor(LT, LT, HS[:, :, META:], mult).then_inc(lru_ready, 1)
            feed(dve, PB["gate_b"])
            feed(dve, PB["gate_b"] + 1)
            dve.wait_ge(high["lru"], 1)
            V.tensor_tensor(LTP[1], LT, LTP[0].bitcast(f32), sub).then_inc(low["lru"], 1)
            feed(dve, PB["gate_b"] + 2)
            row_norm("mem", MR, MR)
            feed(dve, PB["gate_b"] + 3)
            feed(dve, PB["br_ret"])
            feed(dve, PB["br_ret"] + 1)
            turned_low("tm", MTP, W("gmem"))
            turned_low("tr", RTP)
            for j in range(4):
                full(dve, PB["br_ret"] + j + 1)
                moved(dve, f"ga.{j}")
                release(V.tensor_tensor(MIX[:, 2 * j:2 * j + 2, :], GA[:, 2 * j:2 * j + 2, :], bank(f"br.{j}")[:, :].rearrange("p (k t) -> p k t", k=2), mult), f"br.{j}")
            for j in range(4):
                full(dve, PB["br_lru"] + j + 1)
                moved(dve, f"gb.{j}")
                if j >= 2:
                    dve.wait_ge(mixed, j - 1)
                release(V.tensor_tensor(PART[:, j % 2, :].rearrange("p (k t) -> p k t", k=2), GB[:, 2 * j:2 * j + 2, :],
                                        bank(f"bl.{j}")[:, :].rearrange("p (k t) -> p k t", k=2), mult), f"bl.{j}")
            for j in range(4):
                dve.wait_ge(high["mix"], j + 1)
                V.tensor_tensor(MIXP[1][:, 2 * j:2 * j + 2, :], MIX[:, 2 * j:2 * j + 2, :], MIXP[0][:, 2 * j:2 * j + 2, :].bitcast(f32), sub).then_inc(low["mix"], 1)
            for c in range(2):
                full(dve, PB["out1"] + 2 * c + 2)
                for r in range(RT):
                    xs = X[:, r, c * 512:(c + 1) * 512]
                    release(V.tensor_tensor(xs, xs, bank(f"out1.{c}.{r}")[:, :], add), f"out1.{c}.{r}")
            row_norm("h", X, XN)
            feed(dve, PB["mem_k"] + 2)

            def head_sums(names, sq, ss, heads, summed, per=512):
                for i, (name, c, r, *pieces) in enumerate(names):
                    if pieces:
                        feed(dve, pieces[0] + 1)
                    moved(dve, name)
                    V.tensor_reduce(ss[:, r, c * heads:(c + 1) * heads], sq[:, i % 2, 0:per].rearrange("p (h c) -> p h c", h=heads), AX.X, add).then_inc(summed, 1)

            def head_scale(src, ss, dim, rooted_, ready, n):
                dve.wait_ge(rooted_, 1)
                chain(V.reciprocal(ss, ss))
                for r in range(RT):
                    last = V.tensor_tensor(hv(src, n)[:, r], hv(src, n)[:, r], bc(ss[:, r, :], dim), mult)
                last.then_inc(ready, 1)

            def head_mean(ss, dim, summed, count):
                dve.wait_ge(summed, count)
                V.tensor_scalar(ss, ss, 1.0 / dim, EPS, mult, add).then_inc(summed, 1)

            head_sums([(f"mk.{c}.{r}", c, r, PB["mem_k"] + 2 * c + 2) for c in range(2) for r in range(RT)], MSQ, mkss, 2, mk_summed)
            head_mean(mkss, 256, mk_summed, 4)
            turned_low("th", HTP, W("ffnw"))

            def acts(base, steps, silu_done, act_done, hidden_high, hidden_low, scaled=None):
                def one(it, u):
                    s = it * 2 + u
                    static = isinstance(it, int)
                    n = base + 3 * u + 2
                    go = (lambda k: feed(dve, n + 6 * it + k)) if static else (lambda k: split_piece(n + k, it * 6))
                    src = SILU
                    dve.wait_ge(silu_done, s + 1)
                    if scaled is not None:
                        V.tensor_tensor(SILC[:, u % 2, :].rearrange("p (f t) -> p f t", f=2), SILU[:, u % 2, :].rearrange("p (f t) -> p f t", f=2),
                                        CB[:, bass.ds(s, 1), :].to_broadcast([P, 2, T]), mult).then_inc(scaled, 1)
                        src = SILC
                    go(0)
                    if scaled is not None:
                        dve.wait_ge(scaled, s + 1)
                    dve.wait_ge(pieces_used, base + 2 if static and s == 0 else s * 3 + (base + 1))
                    V.tensor_tensor(HID[:, u % 2, :], src[:, u % 2, :], banks[5 + 2 * (u % 2)][:, :], mult).then_inc(act_done, 1)
                    go(1)
                    dve.wait_ge(hidden_high, s + 1)
                    V.tensor_tensor(HIDP[1][:, u % 2].rearrange("p f t -> p (f t)"), HID[:, u % 2, :],
                                    HIDP[0][:, u % 2].rearrange("p f t -> p (f t)").bitcast(f32), sub).then_inc(hidden_low, 1)
                    go(2)
                feed(dve, base + 1)
                one(0, 0)
                one(0, 1)
                last = (steps - (base + 3 * steps == NP)) // 2
                with dve.Fori(1, last) as it:
                    for u in range(2):
                        one(it, u)
                splitters[id(dve)][1] = base + 6 * last + 2
                for s in range(2 * last, steps):
                    one(s // 2, s % 2)

            acts(PB["ffn"], FSTEPS, ffn_silu, ffn_act, high["ffn"], low["ffn"])
            dve.wait_ge(pieces_used, PB["ffn"] + 3 * FSTEPS)
            for r in range(RT):
                for c in range(2):
                    xs = X[:, r, c * 512:(c + 1) * 512]
                    V.tensor_tensor(xs, xs, banks[2 * r + c][:, :], add).then_inc(ffn_added, 1)
            s = stat["fin"][:, 0:RT]
            dve.wait_ge(squares["fin"], RT)
            V.tensor_scalar(s, s, 1.0 / D, EPS, mult, add).then_inc(meansq["fin"], 1)
            dve.wait_ge(rooted["fin"], 1)
            chain(V.reciprocal(s, s))
            dve.wait_ge(final_w_loaded, 16)
            for r in range(RT):
                V.scalar_tensor_tensor(X[:, r, :], X[:, r, :], s[:, r:r + 1], FW, mult, mult).then_inc(normed["fin"], 1)
            feed(dve, PB["mem_v"] + 2)
            head_scale(MKR, mkss, 256, mk_rooted, mk_ready, MH)
            feed(dve, PB["mem_v"] + 3)
            row_norm("y", X, XN)
            feed(dve, PB["iq"])
            turned_scaled("tmk", MKT, W("mkn"))
            turned_low("t2", HTP, W("gmix"))
            feed(dve, PB["iq"] + 1)
            moved(dve, "ik.0", "ik.1")
            V.tensor_scalar(ikss, ikss, 1.0 / 64, EPS, mult, add).then_inc(ik_summed, 1)
            dve.wait_ge(ik_rooted, 1)
            chain(V.reciprocal(ikss, ikss))
            for r in range(RT):
                V.tensor_scalar(IKR[:, r, 64:128], IKR[:, r, 0:64], ikss[:, r:r + 1], None, mult).then_inc(ik_squared, 1)
                dve.wait_ge(ik_squared, r + 1)
                last = V.tensor_scalar(IKR[:, r, 0:64], IKR[:, r, 0:64], ikss[:, r:r + 1], None, mult)
            last.then_inc(ik_ready, 1)
            for j in range(2):
                dve.wait_ge(small_full, 14 + 3 + j)
                for hh in range(2):
                    h = 2 * j + hh
                    b = bank(f"z.{j}")[:, hh * T:(hh + 1) * T]
                    V.tensor_scalar(ZA[:, h * T:(h + 1) * T], b, W("ba2")[:, h:h + 1], None, add)
                    last = V.tensor_scalar(ZB[:, h * T:(h + 1) * T], b, W("ba2")[:, h:h + 1], 0.0, add, amin)
                release(last, f"z.{j}")
            feed(dve, PB["gq"])
            dve.wait_ge(la_ready, 1)
            chain(V.tensor_tensor(ZB, ZB, ZA, sub))
            dve.wait_ge(padded, 2)
            V.tensor_tensor_scan(CUM, RM, ZB, 0.0, mult, add).then_inc(cum_ready, 1)
            feed(dve, PB["gq"] + 1)
            for j in range(2):
                hs = slice(2 * j, 2 * j + 2)
                full(dve, PB["gq"] + j + 1)
                dve.wait_ge(e_ready, 1)
                release(V.scalar_tensor_tensor(QD[:, hs, :].rearrange("p h t -> p (h t)"), bank(f"gq.{j}")[:, :], float(P) ** -0.5, EC[:, j * 512:(j + 1) * 512], mult, mult), f"gq.{j}")
            for j in range(2):
                hs = slice(2 * j, 2 * j + 2)
                full(dve, PB["gk"] + j + 1)
                dve.wait_ge(e_ready, 2)
                release(V.tensor_tensor(KI[:, hs, :].rearrange("p h t -> p (h t)"), bank(f"gk.{j}")[:, :], EI[:, j * 512:(j + 1) * 512], mult), f"gk.{j}")
            chain(V.tensor_copy(dec, EC.rearrange("p (h n c) -> p h n c", h=GH, n=4)[:, :, :, GCH - 1]))
            moved(dve, "gk.0", "gk.1")
            V.tensor_tensor(KET.rearrange("p h (n c) -> p h n c", n=4), KI.rearrange("p h (n c) -> p h n c", n=4), bc(dec, GCH), mult).then_inc(gla_ke, 1)
            dve.wait_ge(turned, turns["tik"])
            release(V.tensor_scalar(IKT, bank("tik")[:, 0:T], W("ikn")[:, 0:1], None, mult), "tik")
            for c in range(3):
                feed(dve, PB["gv"] + 1 + c)
            feed(dve, PB["dkv"])
            feed(dve, PB["dkv"] + 1)
            for i in range(8):
                r, j = i // 4, i % 4
                n = (P, T)[r]
                moved(dve, f"sc{r}.{j}")
                for hh in range(2):
                    head = 4 * (j // 2) + 2 * hh + j % 2
                    src, w = RL[:, i % 2, hh * n:(hh + 1) * n], iwr[:, r, head:head + 1]
                    if j == 0 and hh == 0:
                        chain(V.tensor_scalar(SC[r], src, w, None, mult))
                    else:
                        ins = V.scalar_tensor_tensor(SC[r], src, w, SC[r], mult, add)
                        if hh == 0:
                            chain(ins)
                        else:
                            ins.then_inc(idx_used, 1)
                            dve.wait_ge(idx_used, i + 1)
            head_sums([("dkv.0", 0, 0, PB["dkv"] + 2), ("dkv.1", 0, 1)], DSQ, dkss, 2, dk_summed, per=256)
            feed(dve, PB["dq"] + 2)
            OUT, MARK = 3.0e38, -3.3e38
            triq = C("triq")

            def select(r, turns_, at):
                n = (P, T)[r]
                w, own = WK[r], slice(n - P, n)
                if turns_[0] == 0:
                    chain(V.tensor_scalar(MB[r][:, own], triq, OUT, -OUT, mult, add))
                    if r:
                        V.tensor_copy(w[:, 0:P], SC[r][:, 0:P])
                    chain(V.tensor_tensor(w[:, own], SC[r][:, own], triq, mult))
                    chain(V.tensor_tensor(w[:, own], w[:, own], MB[r][:, own], add))
                for _ in turns_:
                    chain(V.max(top8[:, r, :], w))
                    chain(V.match_replace(w, top8[:, r, :], w, -3.4e38))
                if turns_[-1] == TOPK // 8 - 1:
                    chain(V.tensor_scalar(MB[r], w, MARK, None, ALU.is_lt))
                    chain(V.tensor_tensor(MB[r][:, own], MB[r][:, own], triq, mult))
                    V.tensor_scalar(MB[r], MB[r], 1.0e30, -1.0e30, mult, add).then_inc(topped, 1)

            select(0, range(0, 8), 0)
            for c in range(2):
                feed(dve, PB["dq"] + 3 + c)
                head_sums([(f"dq.{c}.{r}", c, r) for r in range(RT)], DSQ, dqss, 4, dq_summed)
            head_mean(dkss, P, dk_summed, 2)
            head_mean(dqss, P, dq_summed, 4)
            dve.wait_ge(padded, 3)
            blk = C("blk").bitcast(i32)
            for h in range(GH):
                a = h % 2
                dve.wait_ge(gla_full, 4 * h + 1)
                if h >= 2:
                    dve.wait_ge(gla_full, 4 * (h - 1))
                for rr in range(RT):
                    last = V.copy_predicated(ATM[:, a, rr * P:(rr + 1) * P], blk, bank(f"at.{h}")[:, rr * P:(rr + 1) * P])
                release(last, f"at.{h}")
                dve.wait_ge(gla_full, 4 * h + 2)
                s8, up = ST8[:, a], bank(f"up.{h}.0")
                chain(V.tensor_copy(s8[:, 0, :], up[:, 0:T]))
                dve.wait_ge(gla_full, 4 * h + 3)
                release(V.scalar_tensor_tensor(s8[:, 1, :], s8[:, 0, :], dec[:, h, 1:2], bank(f"up.{h}.1")[:, 0:T], mult, add), f"up.{h}.1")
                moved(dve, f"up.{h}.1")
                release(V.scalar_tensor_tensor(s8[:, 2, :], s8[:, 1, :], dec[:, h, 2:3], up[:, T:2 * T], mult, add), f"up.{h}.0")
            feed(dve, PB["gg"] + 1)
            dve.wait_ge(dk_rooted, 1)
            chain(V.reciprocal(dkss, dkss))
            for r in range(RT):
                last = V.tensor_tensor(DKV[:, r, 0:256].rearrange("p (g c) -> p g c", g=2), DKV[:, r, 0:256].rearrange("p (g c) -> p g c", g=2), bc(dkss[:, r, :], P), mult)
            last.then_inc(dk_ready, 1)
            dve.wait_ge(dq_rooted, 1)
            chain(V.reciprocal(dqss, dqss))
            chain(V.tensor_scalar(dqss, dqss, float(P) ** -0.5, None, mult))
            for r in range(RT):
                last = V.tensor_tensor(hv(DQR, DH)[:, r], hv(DQR, DH)[:, r], bc(dqss[:, r, :], P), mult)
            last.then_inc(dq_ready, 1)
            feed(dve, PB["gg"] + 2)
            select(1, range(0, 2), 0)
            feed(dve, PB["gg"] + 3)
            select(1, range(2, 5), 0)
            feed(dve, PB["mq"])
            select(1, range(5, 8), 0)
            feed(dve, PB["mq"] + 1)
            for r in range(RT):
                dve.wait_ge(og_squared, r + 1)
                V.tensor_reduce(ogss[:, r, :], GSQ[:, :].rearrange("p (h c) -> p h c", h=GH), AX.X, add).then_inc(og_reduced, 1)
            dve.wait_ge(og_reduced, 2)
            V.tensor_scalar(ogss, ogss, 1.0 / 256, EPS, mult, add).then_inc(og_summed, 1)
            dve.wait_ge(og_rooted, 1)
            chain(V.reciprocal(ogss, ogss))
            for r in range(RT):
                chain(V.tensor_tensor(hv(OG, GH)[:, r], hv(OG, GH)[:, r], bc(ogss[:, r, :], T), mult))
            moved(dve, *_n("gg", 2, 2))
            V.tensor_tensor(OG, OG, GG, mult).then_inc(og_ready, 1)
            feed(dve, PB["mq"] + 2)
            head_sums([(f"mq.{c}.{r}", c, r, PB["mq"] + 2 * c + 2) for c in range(2) for r in range(RT)], DSQ, mqss, 2, mq_summed)
            head_mean(mqss, 256, mq_summed, 4)
            dve.wait_ge(mq_rooted, 1)
            chain(V.reciprocal(mqss, mqss))
            chain(V.tensor_scalar(mqss, mqss, 1.0 / 16, None, mult))
            for r in range(RT):
                last = V.tensor_tensor(hv(MQR, MH)[:, r], hv(MQR, MH)[:, r], bc(mqss[:, r, :], T), mult)
            last.then_inc(mq_ready, 1)
            feed(dve, PB["gate0"] + 1)
            for g in range(DKVH):
                for n in range(3):
                    heads, keys, r = (4, P, 0) if n == 0 else (2, T, 1)
                    h0 = DGRP * g + (0 if n == 0 else 2 * (n - 1))
                    dve.wait_ge(dsa_full, 8 * g + n + 1)
                    view = DP[:, n, :].rearrange("p (h s) -> p h s", h=heads)
                    release(V.tensor_tensor(view, bank(f"dl.{g}.{n}")[:, :].rearrange("p (h s) -> p h s", h=heads), bc1(MB[r], heads), add), f"dl.{g}.{n}")
                    moved(dve, f"dl.{g}.{n}")
                    V.tensor_reduce(dmx[:, r, h0:h0 + heads], view, AX.X, amax, negate=True).then_inc(dsa_max, 1)
                for n in range(3):
                    heads, keys, r = (4, P, 0) if n == 0 else (2, T, 1)
                    h0 = DGRP * g + (0 if n == 0 else 2 * (n - 1))
                    view = DP[:, n, :].rearrange("p (h s) -> p h s", h=heads)
                    dve.wait_ge(dsa_exp, 3 * g + n + 1)
                    ds_ = dsum[:, r, h0:h0 + heads]
                    chain(V.reciprocal(ds_, ds_))
                    V.tensor_tensor(view, view, bc(ds_, keys), mult).then_inc(dsa_p, 1)
                for r in range(RT):
                    dve.wait_ge(high["do"], RT * g + r + 1)
                    hd = (slice(None), slice(DGRP * g, DGRP * (g + 1)), slice(r * P, (r + 1) * P))
                    release(V.tensor_tensor(ODP[1][hd], bank(f"do.{g}.{r}")[:, :].rearrange("p (h t) -> p h t", h=DGRP), ODP[0][hd].bitcast(f32), sub), f"do.{g}.{r}")
            turned_low("tog", OGP, W("glan"))
            turned_scaled("tmq", MQT, W("mqn"))
            for c in range(4):
                feed(dve, PB["gate0"] + 2 + c)
            for j in range(4):
                dve.wait_ge(mem_full, j + 1)
                V.tensor_reduce(mmx[:, 2 * (j % 2):2 * (j % 2) + 2, j // 2], bank(f"ml.{j}")[:, :].rearrange("p (h s) -> p h s", h=2), AX.X, amax, negate=True).then_inc(mem_max, 1)
            for j in range(4):
                moved(dve, f"ml.{j}")
                ms_ = msum[:, 2 * (j % 2):2 * (j % 2) + 2, j // 2]
                chain(V.reciprocal(ms_, ms_))
                V.tensor_tensor(MP[:, j, :].rearrange("p (h s) -> p h s", h=2), MP[:, j, :].rearrange("p (h s) -> p h s", h=2), bc(ms_, T), mult).then_inc(mem_p, 1)
            for h in range(MH):
                dve.wait_ge(high["mo"], h + 1)
                release(V.tensor_tensor(OMP[1][:, 2 * h:2 * h + 2, :], bank(f"mo.{h}")[:, :].rearrange("p (k t) -> p k t", k=2), OMP[0][:, 2 * h:2 * h + 2, :].bitcast(f32), sub), f"mo.{h}")
            for j in range(4):
                full(dve, PB["o_gla"] + j + 1)
                moved(dve, f"gt0.{j}")
                release(V.tensor_tensor(MRG[:, 2 * j:2 * j + 2, :], GS[:, 2 * j:2 * j + 2, :], bank(f"wo0.{j}")[:, :].rearrange("p (k t) -> p k t", k=2), mult), f"wo0.{j}")
            for i, proj in enumerate(("o_dsa", "o_mem")):
                for j in range(4):
                    feed(dve, PB[proj] - 4 + j + 2)
                for j in range(4):
                    full(dve, PB[proj] + j + 1)
                    moved(dve, f"gt{i + 1}.{j}")
                    if 4 * i + j >= 2:
                        dve.wait_ge(merged, 4 * i + j - 1)
                    release(V.tensor_tensor(MPART[:, j % 2, :], SG[:, j, :], bank(f"wo{i + 1}.{j}")[:, :], mult), f"wo{i + 1}.{j}")
            for j in range(4):
                dve.wait_ge(high["merge"], j + 1)
                V.tensor_tensor(MRGP[1][:, 2 * j:2 * j + 2, :], MRG[:, 2 * j:2 * j + 2, :], MRGP[0][:, 2 * j:2 * j + 2, :].bitcast(f32), sub).then_inc(low["merge"], 1)
            for c in range(2):
                full(dve, PB["out2"] + 2 * c + 2)
                for r in range(RT):
                    xs = X[:, r, c * 512:(c + 1) * 512]
                    release(V.tensor_tensor(xs, xs, bank(f"out2.{c}.{r}")[:, :], add), f"out2.{c}.{r}")
            row_norm("z", X, XN)
            turned_low("t3", HTP, W("gffn"))
            V.tensor_copy(SEL, ident[0:16, 0:16]).then_inc(shares_split, 1)
            feed(dve, PB["moe"] + 2)
            dve.wait_ge(route_full, 1)
            release(V.tensor_tensor(lr, bank("rl")[:, 0:40].rearrange("p (r c) -> p r c", r=RT), bc1(W("brt"), RT), add), "rl")
            moved(dve, "rl")
            gl = lr[:, :, 0:4]
            chain(V.tensor_reduce(gmx, gl, AX.X, amax))
            V.tensor_tensor(gsh, gl, bc(gmx, 4), sub).then_inc(route_max, 1)

            def first_of(dst, values, peak):
                rk = bc1(C("rank"), RT)
                chain(V.tensor_tensor(dst, values, bc(peak, 4), ALU.is_equal))
                chain(V.tensor_tensor(dst, dst, rk, mult))
                chain(V.tensor_reduce(emx, dst, AX.X, amax))
                chain(V.tensor_tensor(dst, rk, bc(emx, 4), ALU.is_equal))

            first_of(oh, gl, gmx)
            chain(V.tensor_tensor(tmp16, lr[:, :, 4:20].rearrange("p r (g j) -> p r g j", g=4), bc(oh, 4), mult))
            chain(V.tensor_reduce(el, tmp16.rearrange("p r g j -> p r j g"), AX.X, add))
            chain(V.tensor_reduce(gmx, el, AX.X, amax))
            V.tensor_tensor(el, el, bc(gmx, 4), sub).then_inc(route_max, 1)
            dve.wait_ge(route_max, 2)
            chain(V.tensor_reduce(gmx, el, AX.X, amax))
            first_of(oh1, el, gmx)
            chain(V.scalar_tensor_tensor(tmp4, oh1, -3.0e38, el, mult, add))
            chain(V.tensor_reduce(gmx, tmp4, AX.X, amax))
            first_of(oh2, tmp4, gmx)
            chain(V.tensor_tensor(oh1, oh1, oh2, add))
            dve.wait_ge(route_exp, 1)
            chain(V.tensor_reduce(gsm, gex, AX.X, add))
            dve.wait_ge(route_exp, 2)
            chain(V.tensor_tensor(oh1, oh1, eex, mult))
            chain(V.tensor_reduce(gmx, oh1, AX.X, add))
            chain(V.tensor_tensor(gmx, gmx, gsm, mult))
            chain(V.reciprocal(gmx, gmx))
            chain(V.tensor_tensor(oh1, oh1, bc(gmx, 4), mult))
            chain(V.tensor_copy(tmp16, bc(oh, 4)))
            V.tensor_tensor(cmb.rearrange("p r (g j) -> p r g j", g=4), tmp16, oh1.unsqueeze(2).to_broadcast([P, RT, 4, 4]), mult).then_inc(combined, 1)
            feed(dve, PB["moe"] + 3)
            dve.wait_ge(turned, turns["tc"])
            chain(V.tensor_copy(CTP[0], bank("tc")[0:16, 0:T]))
            release(V.tensor_tensor(CTP[1], bank("tc")[0:16, 0:T], CTP[0].bitcast(f32), sub), "tc")
            moved(dve, *_n("cb", 8))
            acts(PB["moe"], EXPERTS, moe_silu, moe_act, high["moe"], low["moe"], moe_scaled)
            dve.wait_ge(pieces_used, NP)
            for r in range(RT):
                for c in range(2):
                    xs = X[:, r, c * 512:(c + 1) * 512]
                    V.tensor_tensor(xs, xs, banks[2 * r + c][:, :], add).then_inc(moe_added, 1)

        @block.gpsimd
        def _(pool):
            G.memset(LI[:, :, 0:CONV - 1], 0.0).then_inc(padded, 1)
            names = [f"{w}.{c}.{r}" for w, t in (("k", [0, 1, "m"]), ("q", [0, 1])) for c in range(2) for r in t]
            for i, name in enumerate(names):
                what, c, r = name.split(".")
                c = int(c)
                moved(pool, name)
                if r == "m":
                    dst, n = KM[:, c * 512:(c + 1) * 512], META
                else:
                    dst, n = (KR if what == "k" else QR)[:, int(r), c * 512:(c + 1) * 512], P
                G.tensor_tensor(dst, ROT[0:n, i % 2, 0, :], ROT[0:n, i % 2, 1, :], add).then_inc(rotated, 1)
            for p in range(4):
                moved(pool, f"o.{p}")
                if p >= 2:
                    pool.wait_ge(o_reduced, p - 1)
                o = O[:, :, 2 * p * P:(2 * p + 2) * P]
                G.tensor_tensor(SQ[:, p % 2, :].rearrange("p (r c) -> p r c", r=RT), o, o, mult).then_inc(o_squared, 1)
                pool.wait_ge(high["conv"], p + 1)
                two_ = slice(2 * p, 2 * p + 2)
                G.tensor_tensor(CVP[1][:, two_, :], CV[:, two_, :], CVP[0][:, two_, :].bitcast(f32), sub).then_inc(low["conv"], 1)
            for j in range(4):
                moved(pool, f"br.{j}", f"bl.{j}")
                m = MIX[:, 2 * j:2 * j + 2, :]
                G.tensor_tensor(m, m, PART[:, j % 2, :].rearrange("p (k t) -> p k t", k=2), add).then_inc(mixed, 1)
            pool.wait_ge(mixed, 4)
            pool.dma_start(FW, final_w.partition_broadcast(P)).then_inc(final_w_loaded, 16)
            pool.wait_ge(pieces_used, PB["mem_v"] + 4)
            G.memset(RM, 1.0).then_inc(pool_chain, 1)
            pool.wait_ge(pool_chain, 1)
            G.memset(RM.rearrange("p (n c) -> p n c", c=GCH)[:, :, 0:1], 0.0).then_inc(padded, 1)
            G.memset(ATM, 0.0).then_inc(padded, 1)
            for r in range(RT):
                moved(pool, *_n("og", GH))
                if r:
                    pool.wait_ge(og_reduced, 1)
                G.tensor_tensor(GSQ, OG[:, r, :], OG[:, r, :], mult).then_inc(og_squared, 1)
            for i in range(2):
                for j in range(4):
                    moved(pool, f"wo0.{j}")
                    moved(pool, f"wo{i + 1}.{j}")
                    if i:
                        pool.wait_ge(merged, j + 1)
                    m = MRG[:, 2 * j:2 * j + 2, :]
                    G.tensor_tensor(m, m, MPART[:, j % 2, :].rearrange("p (k t) -> p k t", k=2), add).then_inc(merged, 1)


def rows_pieces(w):
    n = w.shape[1] // 512
    return w.reshape(2, 4, P, n, 512).transpose(3, 0, 2, 1, 4).reshape(2 * n, P, PW)


def cols_pieces(w):
    n = w.shape[1] // 256
    return w.reshape(KT, P, n, 256).transpose(2, 1, 0, 3).reshape(n, P, PW)


def down_pieces(w):
    n = w.shape[0] // 256
    return w.reshape(n, 2, P, D).transpose(0, 2, 1, 3).reshape(n, P, PW)


def hidden_pieces(gate, up, down):
    n = len(gate)
    out = [gate[0], up[0]]
    for s in range(n):
        if s + 1 < n:
            out += [gate[s + 1], up[s + 1]]
        out.append(down[s])
    return np.stack(out)


def per_partition(v):
    return v.reshape(-1, P).T


def kernel(**a):
    import concourse.bacc as bacc
    from concourse import mybir
    from concourse.bass_utils import run_bass_kernel_spmd

    a = {k: np.asarray(v) for k, v in a.items()}
    w1, w2, ff = a["w_in"][0], a["w_in_2"][0], a["w_ffn_in"][0]
    at = dict(gq=0, gk=512, gv=1024, gg=2048, ga=3072, dq=3088, dk=4112, dv=4368, iq=4624, ik=5136, iw=5200, mq=5208, gate=6232)
    lru = lambda w: w.reshape(LRUB, 2, P, 256).transpose(2, 0, 1, 3).reshape(1, P, PW)
    kv = a["w_mem_kv_2"][0]
    moe = lambda w: w.reshape(EXPERTS, KT, P, 256).transpose(0, 2, 1, 3).reshape(EXPERTS, P, PW)
    parts = {
        "k": rows_pieces(w1[:, 1024:2048]), "q": rows_pieces(w1[:, 0:1024]), "v": rows_pieces(w1[:, 2048:3072]),
        "lru_in": cols_pieces(w1[:, 4096:5120]), "g_ret": rows_pieces(w1[:, 3072:4096]),
        "lru_gates": np.concatenate([lru(a["lru_wa"][0]), lru(a["lru_wx"][0])]),
        "lru_gate": cols_pieces(w1[:, 5120:6144]), "gate_a": cols_pieces(w1[:, 6144:7168]), "gate_b": cols_pieces(w1[:, 7168:8192]),
        "br_ret": cols_pieces(a["w_branch_ret"][0]), "br_lru": cols_pieces(a["w_branch_lru"][0]), "out1": rows_pieces(a["w_out"][0]),
        "mem_k": rows_pieces(kv[:, 0:1024]), "mem_v": rows_pieces(kv[:, 1024:2048]),
        "ffn": hidden_pieces(cols_pieces(ff[:, 0:FFN]), cols_pieces(ff[:, FFN:]), down_pieces(a["w_ffn_out"][0])),
        "iq": cols_pieces(w2[:, at["iq"]:at["iq"] + 512]), "gq": cols_pieces(w2[:, 0:512]), "gk": cols_pieces(w2[:, 512:1024]),
        "gv": rows_pieces(w2[:, 1024:2048]), "gg": rows_pieces(w2[:, 2048:3072]), "dkv": rows_pieces(w2[:, at["dk"]:at["dk"] + 512]),
        "dq": rows_pieces(w2[:, at["dq"]:at["dq"] + 1024]), "mq": rows_pieces(w2[:, at["mq"]:at["mq"] + 1024]),
        "gate0": cols_pieces(w2[:, at["gate"]:at["gate"] + 1024]), "gate1": cols_pieces(w2[:, at["gate"] + 1024:at["gate"] + 2048]),
        "gate2": cols_pieces(w2[:, at["gate"] + 2048:at["gate"] + 3072]),
        "o_gla": cols_pieces(a["w_o_gla_2"][0]), "o_dsa": cols_pieces(a["w_o_dsa_2"][0]), "o_mem": cols_pieces(a["w_o_mem_2"][0]),
        "out2": rows_pieces(a["w_out_2"][0]),
        "moe": hidden_pieces(moe(a["w_gate_2"][0]), moe(a["w_up_2"][0]), down_pieces(a["w_down_2"][0].reshape(EXPERTS * 256, D))),
    }
    weights = np.concatenate([parts[n] for n, _ in PIECES])
    sw = np.concatenate([w2[:, at["ga"]:at["ga"] + 16], w2[:, at["ik"]:at["ik"] + 72], a["w_r1_2"][0], a["w_r2_2"][0]], 1)
    cols = {
        "mixw": per_partition(a["mix_norm_w"][0]), "ffnw": per_partition(a["ffn_norm_w"][0]), "gmix": per_partition(a["g_mix_2"][0]),
        "gmem": per_partition(a["g_mem_2"][0]), "gffn": per_partition(a["g_ffn_2"][0]), "convw": per_partition(a["conv_w"][0].reshape(-1)),
        "convb": per_partition(a["conv_b"][0]), "ba": per_partition(a["lru_ba"][0]), "bx": per_partition(a["lru_bx"][0]),
        "lam": per_partition(a["lru_lambda"][0]), "ba2": per_partition(a["b_gla_a2_2"][0]), "glan": per_partition(a["gla_norm_2"][0]),
        "dqn": per_partition(a["dsa_q_norm_2"][0]), "dkn": per_partition(a["dsa_k_norm_2"][0]),
        "ikn": per_partition(np.concatenate([a["idx_k_norm_2"][0]] * 2)), "mqn": per_partition(a["mem_q_norm_2"][0]),
        "mkn": per_partition(a["mem_k_norm_2"][0]), "bgate": per_partition(a["b_gate_2"][0]),
        "brt": np.broadcast_to(np.concatenate([a["b_r1_2"][0], a["b_r2_2"][0]]), (P, 20)),
        "wa2": np.concatenate([a["w_gla_a2_2"][0]] * 8),
    }
    arrays = {
        "weights": weights, "x": a["x"][0], "meta": a["meta_tokens"], "mem": a["mem_2"][0], "consts": shape_constants(),
        "params": np.concatenate([cols[n] for n, _ in PARAMS], 1), "small_w": sw.reshape(KT, P, 108).transpose(1, 0, 2).reshape(P, KT * 108), "final_w": a["final_norm_w"],
    }
    arrays = {k: np.ascontiguousarray(v) for k, v in arrays.items()}
    nc = bacc.Bacc("TRN2", target_bir_lowering=False, num_devices=1)
    f32 = mybir.dt.float32
    aps = {k: nc.dram_tensor(k + "_dram", v.shape, f32, kind="ExternalInput").ap() for k, v in arrays.items()}
    out = nc.dram_tensor("out_dram", (T, D), f32, kind="ExternalOutput").ap()
    program(nc, out=out, **aps)
    r = run_bass_kernel_spmd(nc, [{k + "_dram": v for k, v in arrays.items()}], core_ids=[0])
    return r.results[0]["out_dram"].reshape(1, T, D)
```
